# Optimizing a Trainium2 kernel written in Bass

```python
import math
import jax
import jax.numpy as jnp
from jax import lax
import numpy as np
import jax, jax.numpy as jnp

D_MODEL = 1024
BATCH = 1
SEQ = 256
DEPTH = 1

N_MIXERS = 4
NORM_EPS = 1e-6
NEG_INF = -1e30
F32 = jnp.float32

MOBA_HEADS = 16
MOBA_HEAD_DIM = D_MODEL // MOBA_HEADS
MOBA_BLOCK = 256
MOBA_TOPK = 3
MOBA_Q_CHUNK = 16

RWKV_HEAD_DIM = 64
RWKV_HEADS = D_MODEL // RWKV_HEAD_DIM
RWKV_DECAY_LORA = 64
RWKV_AAA_LORA = 64
RWKV_GATE_LORA = 160
RWKV_GN_EPS = 64e-5
RWKV_N_MIX = 6

SSD_D_INNER = 2 * D_MODEL
SSD_HEAD_DIM = 64
SSD_HEADS = SSD_D_INNER // SSD_HEAD_DIM
SSD_GROUPS = 4
SSD_STATE = 128
SSD_CONV = 4
SSD_CHUNK = 128
SSD_CONV_DIM = SSD_D_INNER + 2 * SSD_GROUPS * SSD_STATE
SSD_IN_DIM = SSD_D_INNER + SSD_CONV_DIM + SSD_HEADS
SSD_NORM_EPS = 1e-5

CONF_KERNEL = 31
CONF_LN_EPS = 1e-5

D_FF = 2816
FFN_CONV = 3


def _rmsnorm(x, g):
    x32 = x.astype(F32)
    y = x32 * lax.rsqrt(jnp.mean(x32 * x32, axis=-1, keepdims=True) + NORM_EPS)
    return (y * g.astype(F32)).astype(x.dtype)

def _layernorm(x, w, b, eps):
    x32 = x.astype(F32)
    mu = jnp.mean(x32, axis=-1, keepdims=True)
    var = jnp.mean(jnp.square(x32 - mu), axis=-1, keepdims=True)
    return ((x32 - mu) * lax.rsqrt(var + eps) * w.astype(F32) + b.astype(F32)).astype(x.dtype)

def _causal_dwconv(x, w, b):
    k, c = w.shape
    y = lax.conv_general_dilated(x, w[:, None, :], window_strides=(1,), padding=[(k - 1, 0)],
                                 dimension_numbers=('NWC', 'WIO', 'NWC'), feature_group_count=c)
    return y + b

def _moba(x, w_qkv, w_o):
    b, s, d = x.shape
    h, dh, bs, qc = MOBA_HEADS, MOBA_HEAD_DIM, MOBA_BLOCK, MOBA_Q_CHUNK
    qkv = jnp.einsum('bsd,de->bse', x, w_qkv).reshape(b, s, 3, h, dh)
    q = jnp.transpose(qkv[:, :, 0], (0, 2, 1, 3)) * dh ** -0.5
    k = jnp.transpose(qkv[:, :, 1], (0, 2, 1, 3))
    v = jnp.transpose(qkv[:, :, 2], (0, 2, 1, 3))
    n_blk = -(-s // bs)
    pad = n_blk * bs - s
    kb = jnp.pad(k, ((0, 0), (0, 0), (0, pad), (0, 0))).reshape(b, h, n_blk, bs, dh)
    vb = jnp.pad(v, ((0, 0), (0, 0), (0, pad), (0, 0))).reshape(b, h, n_blk, bs, dh)
    k_mean = jnp.mean(kb, axis=3)
    q_blk = jnp.arange(s) // bs
    gate = jnp.einsum('bhsd,bhnd->bhsn', q, k_mean).astype(F32)
    fully_past = jnp.arange(n_blk)[None, :] < q_blk[:, None]
    gate = jnp.where(fully_past, gate, NEG_INF)
    n_sel = min(MOBA_TOPK, n_blk)
    _, sel = lax.top_k(gate, n_sel)
    sel_valid = sel < q_blk[:, None]
    bi = jnp.arange(b)[:, None, None, None]
    hi = jnp.arange(h)[None, :, None, None]

    def chunk(c):
        start = c * qc
        q_c = lax.dynamic_slice_in_dim(q, start, qc, axis=2)
        sel_c = lax.dynamic_slice_in_dim(sel, start, qc, axis=2)
        val_c = lax.dynamic_slice_in_dim(sel_valid, start, qc, axis=2)
        k_sel = kb[bi, hi, sel_c]
        v_sel = vb[bi, hi, sel_c]
        own = start // bs
        k_own = lax.dynamic_index_in_dim(kb, own, axis=2, keepdims=False)
        v_own = lax.dynamic_index_in_dim(vb, own, axis=2, keepdims=False)
        s_sel = jnp.einsum('bhqd,bhqnkd->bhqnk', q_c, k_sel).astype(F32)
        s_sel = jnp.where(val_c[..., None], s_sel, NEG_INF).reshape(b, h, qc, n_sel * bs)
        s_own = jnp.einsum('bhqd,bhkd->bhqk', q_c, k_own).astype(F32)
        q_pos = start + jnp.arange(qc)
        k_pos = own * bs + jnp.arange(bs)
        s_own = jnp.where(k_pos[None, :] <= q_pos[:, None], s_own, NEG_INF)
        p = jax.nn.softmax(jnp.concatenate([s_sel, s_own], axis=-1), axis=-1).astype(v.dtype)
        p_sel = p[..., :n_sel * bs].reshape(b, h, qc, n_sel, bs)
        p_own = p[..., n_sel * bs:]
        return (jnp.einsum('bhqnk,bhqnkd->bhqd', p_sel, v_sel)
                + jnp.einsum('bhqk,bhkd->bhqd', p_own, v_own))

    o = lax.map(chunk, jnp.arange(s // qc))
    o = jnp.transpose(o, (1, 0, 3, 2, 4)).reshape(b, s, d)
    return o @ w_o

def _rwkv7(x, mu, w_rkv, w0, w1, w2, a0, a1, a2, g1, g2, k_k, k_a, r_k, gn_w, gn_b, w_o):
    b, s, d = x.shape
    h, n = RWKV_HEADS, RWKV_HEAD_DIM
    xx = jnp.pad(x, ((0, 0), (1, 0), (0, 0)))[:, :-1] - x
    xm = x[:, :, None, :] + xx[:, :, None, :] * mu
    rkv = jnp.einsum('bsid,ide->bsie', xm[:, :, :3], w_rkv)
    r, k, v = rkv[:, :, 0], rkv[:, :, 1], rkv[:, :, 2]
    xw, xa, xg = xm[:, :, 3], xm[:, :, 4], xm[:, :, 5]
    w = -jax.nn.softplus(-(w0 + jnp.tanh(xw @ w1) @ w2).astype(F32)) - 0.5
    decay = jnp.exp(-jnp.exp(w))
    a = jax.nn.sigmoid(a0 + (xa @ a1) @ a2)
    g = jax.nn.sigmoid(xg @ g1) @ g2
    kk = (k * k_k).reshape(b, s, h, n).astype(F32)
    kk = kk / jnp.maximum(jnp.sqrt(jnp.sum(kk * kk, axis=-1, keepdims=True)), 1e-12)
    k = k * (1.0 + (a - 1.0) * k_a)
    r, k, v, a = (t.reshape(b, s, h, n) for t in (r, k, v, a))

    def to_time(t):
        return jnp.swapaxes(t.astype(F32), 0, 1)

    xs = (to_time(r), to_time(decay.reshape(b, s, h, n)), to_time(k), to_time(v),
          to_time(-kk), to_time(kk * a))

    def step(state, inp):
        r_t, w_t, k_t, v_t, a_t, b_t = inp
        sa = jnp.einsum('bhij,bhj->bhi', state, a_t)
        state = (state * w_t[:, :, None, :] + sa[..., None] * b_t[:, :, None, :]
                 + v_t[..., None] * k_t[:, :, None, :])
        return state, jnp.einsum('bhij,bhj->bhi', state, r_t)

    _, y = lax.scan(step, jnp.zeros((b, h, n, n), F32), xs)
    y = jnp.swapaxes(y, 0, 1)
    mu_y = jnp.mean(y, axis=-1, keepdims=True)
    var_y = jnp.mean(jnp.square(y - mu_y), axis=-1, keepdims=True)
    yn = ((y - mu_y) * lax.rsqrt(var_y + RWKV_GN_EPS)).reshape(b, s, d)
    yn = yn * gn_w.astype(F32) + gn_b.astype(F32)
    bonus = (jnp.sum(r * k * r_k, axis=-1, keepdims=True) * v).reshape(b, s, d).astype(F32)
    return ((yn + bonus).astype(x.dtype) * g) @ w_o

def _segsum(a):
    t = a.shape[-1]
    rep = jnp.broadcast_to(a[..., :, None], a.shape + (t,))
    rep = jnp.where(jnp.tril(jnp.ones((t, t), bool), -1), rep, 0.0)
    cs = jnp.cumsum(rep, axis=-2)
    return jnp.where(jnp.tril(jnp.ones((t, t), bool)), cs, -jnp.inf)

def _ssd_chunked(xd, adt, bm, cm):
    b, s, h, p = xd.shape
    g, n = bm.shape[2], bm.shape[3]
    e = h // g
    lc = SSD_CHUNK
    c = s // lc
    xc = xd.reshape(b, c, lc, g, e, p)
    bc = bm.reshape(b, c, lc, g, n)
    cc = cm.reshape(b, c, lc, g, n)
    ac = jnp.transpose(adt.reshape(b, c, lc, g, e), (0, 3, 4, 1, 2))
    a_cs = jnp.cumsum(ac, axis=-1)
    lmat = jnp.exp(_segsum(ac))
    cb = jnp.einsum('bclgn,bcsgn->bgcls', cc, bc)
    y_diag = jnp.einsum('bgecls,bcsgep->bclgep', cb[:, :, None] * lmat, xc)
    decay_states = jnp.exp(a_cs[..., -1:] - a_cs)
    states = jnp.einsum('bclgn,bgecl,bclgep->bcgepn', bc, decay_states, xc)
    states = jnp.concatenate([jnp.zeros_like(states[:, :1]), states], axis=1)
    chunk_a = jnp.pad(a_cs[..., -1], ((0, 0), (0, 0), (0, 0), (1, 0)))
    decay_chunk = jnp.exp(_segsum(chunk_a))
    states = jnp.einsum('bgezc,bcgepn->bzgepn', decay_chunk, states)[:, :-1]
    y_off = jnp.einsum('bclgn,bcgepn,bgecl->bclgep', cc, states, jnp.exp(a_cs))
    return (y_diag + y_off).reshape(b, s, h, p)

def _mamba2(x, w_in, conv_w, conv_b, dt_bias, a_log, d_skip, norm_w, w_out):
    b, s, _ = x.shape
    di, h, p, g, n = SSD_D_INNER, SSD_HEADS, SSD_HEAD_DIM, SSD_GROUPS, SSD_STATE
    zxbcdt = x @ w_in
    z, xbc, dt = jnp.split(zxbcdt, [di, di + SSD_CONV_DIM], axis=-1)
    xbc = jax.nn.silu(_causal_dwconv(xbc, conv_w, conv_b))
    xs, bm, cm = jnp.split(xbc, [di, di + g * n], axis=-1)
    dt = jax.nn.softplus((dt + dt_bias).astype(F32))
    a = -jnp.exp(a_log.astype(F32))
    xh = xs.reshape(b, s, h, p).astype(F32)
    y = _ssd_chunked(xh * dt[..., None], dt * a,
                     bm.reshape(b, s, g, n).astype(F32), cm.reshape(b, s, g, n).astype(F32))
    y = (y + xh * d_skip.astype(F32)[:, None]).reshape(b, s, di)
    yz = (y * jax.nn.silu(z.astype(F32))).reshape(b, s, g, di // g)
    yz = yz * lax.rsqrt(jnp.mean(yz * yz, axis=-1, keepdims=True) + SSD_NORM_EPS)
    yz = yz.reshape(b, s, di) * norm_w.astype(F32)
    return yz.astype(x.dtype) @ w_out

def _conformer_conv(x, w_pw1, b_pw1, dw_w, dw_b, ln_w, ln_b, w_pw2, b_pw2):
    u = jax.nn.glu(x @ w_pw1 + b_pw1, axis=-1)
    u = _causal_dwconv(u, dw_w, dw_b)
    u = jax.nn.silu(_layernorm(u, ln_w, ln_b, CONF_LN_EPS))
    return u @ w_pw2 + b_pw2

def _conv_ffn(x, w_up, conv_w, conv_b, w_down):
    u = _causal_dwconv(x @ w_up, conv_w, conv_b)
    gate, up = jnp.split(u, 2, axis=-1)
    return (jax.nn.silu(gate) * up) @ w_down

def _count(kind):
    return len(range(kind, DEPTH, N_MIXERS))

def first_inputs(seed: int = 0) -> dict:
    key = jax.random.key(seed)
    ks = iter(jax.random.split(key, 64))

    def nrm(shape, scale):
        return jax.random.normal(next(ks), shape, F32) * scale

    def uni(shape, lo, hi):
        return jax.random.uniform(next(ks), shape, F32, lo, hi)

    d = D_MODEL
    n_a, n_b, n_c, n_d = (_count(m) for m in range(N_MIXERS))
    dt0 = jnp.exp(uni((n_c, SSD_HEADS), math.log(1e-3), math.log(1e-1)))
    return {
        'x': nrm((BATCH, SEQ, d), 1.0),
        'norm_mix': 1.0 + nrm((DEPTH, d), 0.02),
        'norm_ffn': 1.0 + nrm((DEPTH, d), 0.02),
        'norm_final': 1.0 + nrm((d,), 0.02),
        'ffn_w_up': nrm((DEPTH, d, 2 * D_FF), d ** -0.5),
        'ffn_conv_w': nrm((DEPTH, FFN_CONV, 2 * D_FF), FFN_CONV ** -0.5),
        'ffn_conv_b': nrm((DEPTH, 2 * D_FF), 0.01),
        'ffn_w_down': nrm((DEPTH, D_FF, d), D_FF ** -0.5),
        'moba_w_qkv': nrm((n_a, d, 3 * d), d ** -0.5),
        'moba_w_o': nrm((n_a, d, d), d ** -0.5),
        'rwkv_mu': uni((n_b, RWKV_N_MIX, d), 0.0, 1.0),
        'rwkv_w_rkv': nrm((n_b, 3, d, d), d ** -0.5),
        'rwkv_w0': uni((n_b, d), -6.0, 1.0),
        'rwkv_w1': nrm((n_b, d, RWKV_DECAY_LORA), d ** -0.5),
        'rwkv_w2': nrm((n_b, RWKV_DECAY_LORA, d), 0.1 * RWKV_DECAY_LORA ** -0.5),
        'rwkv_a0': nrm((n_b, d), 0.1),
        'rwkv_a1': nrm((n_b, d, RWKV_AAA_LORA), d ** -0.5),
        'rwkv_a2': nrm((n_b, RWKV_AAA_LORA, d), 0.1 * RWKV_AAA_LORA ** -0.5),
        'rwkv_g1': nrm((n_b, d, RWKV_GATE_LORA), d ** -0.5),
        'rwkv_g2': nrm((n_b, RWKV_GATE_LORA, d), RWKV_GATE_LORA ** -0.5),
        'rwkv_k_k': 0.85 + nrm((n_b, d), 0.02),
        'rwkv_k_a': 1.0 + nrm((n_b, d), 0.02),
        'rwkv_r_k': nrm((n_b, RWKV_HEADS, RWKV_HEAD_DIM), 0.1),
        'rwkv_gn_w': 1.0 + nrm((n_b, d), 0.02),
        'rwkv_gn_b': nrm((n_b, d), 0.01),
        'rwkv_w_o': nrm((n_b, d, d), d ** -0.5),
        'ssd_w_in': nrm((n_c, d, SSD_IN_DIM), d ** -0.5),
        'ssd_conv_w': nrm((n_c, SSD_CONV, SSD_CONV_DIM), SSD_CONV ** -0.5),
        'ssd_conv_b': nrm((n_c, SSD_CONV_DIM), 0.01),
        'ssd_dt_bias': dt0 + jnp.log(-jnp.expm1(-dt0)),
        'ssd_a_log': jnp.log(uni((n_c, SSD_HEADS), 1.0, 16.0)),
        'ssd_d': 1.0 + nrm((n_c, SSD_HEADS), 0.1),
        'ssd_norm_w': 1.0 + nrm((n_c, SSD_D_INNER), 0.02),
        'ssd_w_out': nrm((n_c, SSD_D_INNER, d), SSD_D_INNER ** -0.5),
        'conf_w_pw1': nrm((n_d, d, 2 * d), d ** -0.5),
        'conf_b_pw1': nrm((n_d, 2 * d), 0.01),
        'conf_dw_w': nrm((n_d, CONF_KERNEL, d), CONF_KERNEL ** -0.5),
        'conf_dw_b': nrm((n_d, d), 0.01),
        'conf_ln_w': 1.0 + nrm((n_d, d), 0.02),
        'conf_ln_b': nrm((n_d, d), 0.01),
        'conf_w_pw2': nrm((n_d, d, d), d ** -0.5),
        'conf_b_pw2': nrm((n_d, d), 0.01),
    }

def first_block(x, norm_mix, norm_ffn, norm_final, ffn_w_up, ffn_conv_w, ffn_conv_b, ffn_w_down,
              moba_w_qkv, moba_w_o,
              rwkv_mu, rwkv_w_rkv, rwkv_w0, rwkv_w1, rwkv_w2, rwkv_a0, rwkv_a1, rwkv_a2,
              rwkv_g1, rwkv_g2, rwkv_k_k, rwkv_k_a, rwkv_r_k, rwkv_gn_w, rwkv_gn_b, rwkv_w_o,
              ssd_w_in, ssd_conv_w, ssd_conv_b, ssd_dt_bias, ssd_a_log, ssd_d, ssd_norm_w, ssd_w_out,
              conf_w_pw1, conf_b_pw1, conf_dw_w, conf_dw_b, conf_ln_w, conf_ln_b, conf_w_pw2, conf_b_pw2):
    for i in range(DEPTH):
        kind, j = i % N_MIXERS, i // N_MIXERS
        hn = _rmsnorm(x, norm_mix[i])
        if kind == 0:
            mix = _moba(hn, moba_w_qkv[j], moba_w_o[j])
        elif kind == 1:
            mix = _rwkv7(hn, rwkv_mu[j], rwkv_w_rkv[j], rwkv_w0[j], rwkv_w1[j], rwkv_w2[j],
                         rwkv_a0[j], rwkv_a1[j], rwkv_a2[j], rwkv_g1[j], rwkv_g2[j],
                         rwkv_k_k[j], rwkv_k_a[j], rwkv_r_k[j], rwkv_gn_w[j], rwkv_gn_b[j], rwkv_w_o[j])
        elif kind == 2:
            mix = _mamba2(hn, ssd_w_in[j], ssd_conv_w[j], ssd_conv_b[j], ssd_dt_bias[j],
                          ssd_a_log[j], ssd_d[j], ssd_norm_w[j], ssd_w_out[j])
        else:
            mix = _conformer_conv(hn, conf_w_pw1[j], conf_b_pw1[j], conf_dw_w[j], conf_dw_b[j],
                                  conf_ln_w[j], conf_ln_b[j], conf_w_pw2[j], conf_b_pw2[j])
        x = x + mix
        x = x + _conv_ffn(_rmsnorm(x, norm_ffn[i]), ffn_w_up[i], ffn_conv_w[i], ffn_conv_b[i], ffn_w_down[i])
    return _rmsnorm(x, norm_final)


DEPTH_2 = 2

N_MIXERS_2 = 2
HEAD_DIM = 64
A_Q_HEADS = D_MODEL // HEAD_DIM
A_KV_HEADS = A_Q_HEADS // 4
A_GROUP = A_Q_HEADS // A_KV_HEADS
WINDOW = 128
B_HEADS = D_MODEL // HEAD_DIM
BLOCK = 128
REL_BUCKETS = 32
REL_MAX_DIST = 128
EPS = 1e-6
FORGET_BIAS_INIT = 2.0
N_A_LAYERS = (DEPTH_2 + 1) // 2
N_B_LAYERS = DEPTH_2 // 2
A_IN = (A_Q_HEADS + 2 * A_KV_HEADS) * HEAD_DIM
B_IN = 3 * B_HEADS * HEAD_DIM + B_HEADS


def rmsnorm(x, g):
    xf = x.astype(jnp.float32)
    y = xf * lax.rsqrt(jnp.mean(xf * xf, axis=-1, keepdims=True) + EPS) * g.astype(jnp.float32)
    return y.astype(x.dtype)

def modulate(x, g, shift, scale):
    return rmsnorm(x, g) * (1 + scale[:, None, :]) + shift[:, None, :]

def swiglu(h, w13, w2):
    gate, up = jnp.split(h @ w13, 2, axis=-1)
    return (jax.nn.silu(gate) * up) @ w2

def rel_bucket(dist):
    n = jnp.maximum(dist, 0)
    max_exact = REL_BUCKETS // 2
    nf = jnp.maximum(n, 1).astype(jnp.float32)
    large = max_exact + (jnp.log(nf / max_exact) / math.log(REL_MAX_DIST / max_exact)
                         * (REL_BUCKETS - max_exact)).astype(jnp.int32)
    large = jnp.minimum(large, REL_BUCKETS - 1)
    return jnp.where(n < max_exact, n, large)

def swa_mixer(h, w_in, w_out, q_g, k_g, sink, rel_bias):
    B, S, _ = h.shape
    nblk = S // BLOCK
    proj = h @ w_in
    q, k, v = jnp.split(proj, [A_Q_HEADS * HEAD_DIM, (A_Q_HEADS + A_KV_HEADS) * HEAD_DIM], axis=-1)
    q = rmsnorm(q.reshape(B, S, A_KV_HEADS, A_GROUP, HEAD_DIM), q_g) * (HEAD_DIM ** -0.5)
    k = rmsnorm(k.reshape(B, S, A_KV_HEADS, HEAD_DIM), k_g)
    v = v.reshape(B, S, A_KV_HEADS, HEAD_DIM)
    pad = ((0, 0), (BLOCK, 0), (0, 0), (0, 0))
    kp = jnp.pad(k, pad)
    vp = jnp.pad(v, pad)
    qi = jnp.arange(BLOCK)[:, None] + BLOCK
    kj = jnp.arange(2 * BLOCK)[None, :]
    dist = qi - kj
    band = (dist >= 0) & (dist < WINDOW)
    bias = jnp.transpose(rel_bias[rel_bucket(dist)], (2, 0, 1)).astype(jnp.float32)
    bias = bias.reshape(A_KV_HEADS, A_GROUP, BLOCK, 2 * BLOCK)
    sink_f = sink.astype(jnp.float32).reshape(A_KV_HEADS, A_GROUP)[None, :, :, None]

    def block(i):
        start = i * BLOCK
        qb = lax.dynamic_slice_in_dim(q, start, BLOCK, axis=1)
        kb = lax.dynamic_slice_in_dim(kp, start, 2 * BLOCK, axis=1)
        vb = lax.dynamic_slice_in_dim(vp, start, 2 * BLOCK, axis=1)
        s = jnp.einsum('bqhgd,bkhd->bhgqk', qb, kb).astype(jnp.float32) + bias
        valid = band & (start - BLOCK + kj >= 0)
        s = jnp.where(valid, s, -jnp.inf)
        m = jnp.maximum(jnp.max(s, axis=-1), sink_f)
        p = jnp.exp(s - m[..., None])
        denom = jnp.sum(p, axis=-1) + jnp.exp(sink_f - m)
        p = p / denom[..., None]
        return jnp.einsum('bhgqk,bkhd->bqhgd', p.astype(vb.dtype), vb)

    out = lax.map(block, jnp.arange(nblk))
    out = jnp.moveaxis(out, 0, 1).reshape(B, S, A_Q_HEADS * HEAD_DIM)
    return out @ w_out

def fox_mixer(h, w_in, w_out, b_f, q_g, k_g):
    B, S, _ = h.shape
    nblk = S // BLOCK
    HD = B_HEADS * HEAD_DIM
    proj = h @ w_in
    q, k, v, fl = jnp.split(proj, [HD, 2 * HD, 3 * HD], axis=-1)
    q = rmsnorm(q.reshape(B, S, B_HEADS, HEAD_DIM), q_g) * (HEAD_DIM ** -0.5)
    k = rmsnorm(k.reshape(B, S, B_HEADS, HEAD_DIM), k_g)
    v = v.reshape(B, S, B_HEADS, HEAD_DIM)
    log_f = jax.nn.log_sigmoid(fl.astype(jnp.float32) + b_f.astype(jnp.float32))
    F = jnp.transpose(jnp.cumsum(log_f, axis=1), (0, 2, 1))
    kpos = jnp.arange(S)

    def block(i):
        start = i * BLOCK
        qb = lax.dynamic_slice_in_dim(q, start, BLOCK, axis=1)
        Fq = lax.dynamic_slice_in_dim(F, start, BLOCK, axis=2)
        s = jnp.einsum('bqhd,bkhd->bhqk', qb, k).astype(jnp.float32)
        s = s + Fq[..., None] - F[:, :, None, :]
        qpos = start + jnp.arange(BLOCK)
        s = jnp.where(kpos[None, :] <= qpos[:, None], s, -jnp.inf)
        p = jax.nn.softmax(s, axis=-1)
        return jnp.einsum('bhqk,bkhd->bqhd', p.astype(v.dtype), v)

    out = lax.map(block, jnp.arange(nblk))
    out = jnp.moveaxis(out, 0, 1).reshape(B, S, HD)
    return out @ w_out

def second_inputs(seed: int = 0) -> dict:
    key = jax.random.key(seed)
    ks = jax.random.split(key, 20)
    D = D_MODEL

    def nrm(k, shape, s):
        return jax.random.normal(k, shape, jnp.float32) * s

    return {
        'x': nrm(ks[0], (BATCH, SEQ, D), 1.0),
        'c': nrm(ks[1], (BATCH, D), 1.0),
        'ada_w': nrm(ks[2], (DEPTH_2, D, 9 * D), 0.5 * D ** -0.5),
        'ada_b': nrm(ks[3], (DEPTH_2, 9 * D), 0.02),
        'norm_g': 1.0 + nrm(ks[4], (DEPTH_2, 3, D), 0.02),
        'ffn_w13': nrm(ks[5], (DEPTH_2, 2, D, 2 * D_FF), D ** -0.5),
        'ffn_w2': nrm(ks[6], (DEPTH_2, 2, D_FF, D), D_FF ** -0.5),
        'rel_bias': nrm(ks[7], (REL_BUCKETS, A_Q_HEADS), 0.5),
        'swa_w_in': nrm(ks[8], (N_A_LAYERS, D, A_IN), D ** -0.5),
        'swa_w_out': nrm(ks[9], (N_A_LAYERS, A_Q_HEADS * HEAD_DIM, D), (A_Q_HEADS * HEAD_DIM) ** -0.5),
        'swa_q_g': 1.0 + nrm(ks[10], (N_A_LAYERS, HEAD_DIM), 0.02),
        'swa_k_g': 1.0 + nrm(ks[11], (N_A_LAYERS, HEAD_DIM), 0.02),
        'swa_sink': nrm(ks[12], (N_A_LAYERS, A_Q_HEADS), 0.5),
        'fox_w_in': nrm(ks[13], (N_B_LAYERS, D, B_IN), D ** -0.5),
        'fox_w_out': nrm(ks[14], (N_B_LAYERS, B_HEADS * HEAD_DIM, D), (B_HEADS * HEAD_DIM) ** -0.5),
        'fox_b_f': FORGET_BIAS_INIT + nrm(ks[15], (N_B_LAYERS, B_HEADS), 0.1),
        'fox_q_g': 1.0 + nrm(ks[16], (N_B_LAYERS, HEAD_DIM), 0.02),
        'fox_k_g': 1.0 + nrm(ks[17], (N_B_LAYERS, HEAD_DIM), 0.02),
    }

def second_block(x, c, ada_w, ada_b, norm_g, ffn_w13, ffn_w2, rel_bias,
              swa_w_in, swa_w_out, swa_q_g, swa_k_g, swa_sink,
              fox_w_in, fox_w_out, fox_b_f, fox_q_g, fox_k_g):
    B = x.shape[0]
    c_act = jax.nn.silu(c)
    for layer in range(DEPTH_2):
        mod = (c_act @ ada_w[layer] + ada_b[layer]).reshape(B, 3, 3, D_MODEL)
        h = modulate(x, norm_g[layer, 0], mod[:, 0, 0], mod[:, 0, 1])
        x = x + 0.5 * mod[:, 0, 2][:, None, :] * swiglu(h, ffn_w13[layer, 0], ffn_w2[layer, 0])
        h = modulate(x, norm_g[layer, 1], mod[:, 1, 0], mod[:, 1, 1])
        j = layer // N_MIXERS_2
        if layer % N_MIXERS_2 == 0:
            y = swa_mixer(h, swa_w_in[j], swa_w_out[j], swa_q_g[j], swa_k_g[j], swa_sink[j], rel_bias)
        else:
            y = fox_mixer(h, fox_w_in[j], fox_w_out[j], fox_b_f[j], fox_q_g[j], fox_k_g[j])
        x = x + mod[:, 1, 2][:, None, :] * y
        h = modulate(x, norm_g[layer, 2], mod[:, 2, 0], mod[:, 2, 1])
        x = x + 0.5 * mod[:, 2, 2][:, None, :] * swiglu(h, ffn_w13[layer, 1], ffn_w2[layer, 1])
    return x


def setup_inputs(seed=0):
    out = dict(first_inputs(seed))
    for name, value in second_inputs(seed + 1).items():
        if name != "x":
            out[name + "_2"] = value
    return out


def reference(
    x, norm_mix, norm_ffn, norm_final, ffn_w_up, ffn_conv_w, ffn_conv_b, ffn_w_down, moba_w_qkv,
    moba_w_o, rwkv_mu, rwkv_w_rkv, rwkv_w0, rwkv_w1, rwkv_w2, rwkv_a0, rwkv_a1, rwkv_a2,
    rwkv_g1, rwkv_g2, rwkv_k_k, rwkv_k_a, rwkv_r_k, rwkv_gn_w, rwkv_gn_b, rwkv_w_o, ssd_w_in,
    ssd_conv_w, ssd_conv_b, ssd_dt_bias, ssd_a_log, ssd_d, ssd_norm_w, ssd_w_out, conf_w_pw1,
    conf_b_pw1, conf_dw_w, conf_dw_b, conf_ln_w, conf_ln_b, conf_w_pw2, conf_b_pw2, c_2,
    ada_w_2, ada_b_2, norm_g_2, ffn_w13_2, ffn_w2_2, rel_bias_2, swa_w_in_2, swa_w_out_2,
    swa_q_g_2, swa_k_g_2, swa_sink_2, fox_w_in_2, fox_w_out_2, fox_b_f_2, fox_q_g_2, fox_k_g_2,
):
    x = first_block(
        x, norm_mix, norm_ffn, norm_final, ffn_w_up, ffn_conv_w, ffn_conv_b, ffn_w_down,
        moba_w_qkv, moba_w_o, rwkv_mu, rwkv_w_rkv, rwkv_w0, rwkv_w1, rwkv_w2, rwkv_a0, rwkv_a1,
        rwkv_a2, rwkv_g1, rwkv_g2, rwkv_k_k, rwkv_k_a, rwkv_r_k, rwkv_gn_w, rwkv_gn_b, rwkv_w_o,
        ssd_w_in, ssd_conv_w, ssd_conv_b, ssd_dt_bias, ssd_a_log, ssd_d, ssd_norm_w, ssd_w_out,
        conf_w_pw1, conf_b_pw1, conf_dw_w, conf_dw_b, conf_ln_w, conf_ln_b, conf_w_pw2,
        conf_b_pw2,
    )
    return second_block(
        x, c_2, ada_w_2, ada_b_2, norm_g_2, ffn_w13_2, ffn_w2_2, rel_bias_2, swa_w_in_2,
        swa_w_out_2, swa_q_g_2, swa_k_g_2, swa_sink_2, fox_w_in_2, fox_w_out_2, fox_b_f_2,
        fox_q_g_2, fox_k_g_2,
    )


_drawn_inputs = setup_inputs


def setup_inputs(seed=0):
    import zlib

    import numpy as np

    out = dict(_drawn_inputs(seed))
    spreads = {}
    factors = {'norm_mix': 7.493,
     'norm_ffn': 4.002,
     'norm_final': 2.805,
     'ffn_conv_b': 7.712,
     'norm_g_2': 7.357,
     'swa_q_g_2': 8.0,
     'swa_k_g_2': 8.0,
     'swa_sink_2': 64.0,
     'fox_b_f_2': 23.226,
     'fox_q_g_2': 8.0,
     'fox_k_g_2': 8.0}
    for name, (base, spread) in spreads.items():
        noise = np.random.default_rng([zlib.crc32(name.encode()), seed]).standard_normal(out[name].shape)
        drawn = base * np.exp(spread * noise) if base else spread * noise
        out[name] = jnp.asarray(drawn.astype(out[name].dtype))
    for name, factor in factors.items():
        out[name] = (out[name] * factor).astype(out[name].dtype)
    return out
```

```python
from contextlib import ExitStack

import numpy as np
import concourse.bass as bass
from concourse import mybir

ALU = mybir.AluOpType
ACT = mybir.ActivationFunctionType
F32 = mybir.dt.float32
F32R = mybir.dt.float32r

P = 128
D = 1024
T = 256
C = D // P
FF = 2816
HEADS = 16
DH = 64
COLS = 256
HALF = 4 * COLS
SLOTS = 4
UP_STEPS = FF // COLS
HID = FF // P
KEYS = 3 * P
EPS = 1e-6
MASKED = -1e30
BUCKETS, MAX_DIST = 32, 128
BIAS_ROW = 3 * P

V_MIX, V_FFN, V_FINAL = 0, C, 2 * C
V_NORM_G = 3 * C
V_ADA_B = V_NORM_G + 6 * C
V_C = V_ADA_B + 6 * 3 * C
V_CONV = V_C + C
V_QK_G = V_CONV + UP_STEPS * 16
V_SINK = V_QK_G + 4
V_BF = V_SINK + HEADS
V_COLS = V_BF + HEADS

QKV = {"moba": (4, 4, 4), "swa": (4, 1, 1), "fox": (4, 4, 4)}
ATTN = ["moba", "swa", "fox"]
ORDER = ["moba", "ffn0", "ffn1", "swa", "ffn2", "ffn3", "fox", "ffn4"]
O_UNITS = D // COLS
BASE = {}
_h = 0
for _s in ORDER:
    BASE[_s] = _h
    _h += 2 * (sum(QKV[_s]) + O_UNITS) if _s in QKV else 2 * (2 * UP_STEPS + HID // 2)
HALVES = _h
NORMS = ["moba", "ffn0", "final", "ffn1", "swa", "ffn2", "ffn3", "fox", "ffn4"]
SPLIT_NORMS = [n for n in NORMS if n != "final"]
MOD_SET = {"ffn1": 0, "swa": 1, "ffn2": 2, "ffn3": 3, "fox": 4, "ffn4": 5}
MOD_UNITS = 3 * D // COLS
MOD_IN_UP = {"ffn1": 1, "ffn2": 3, "ffn3": 4}
MOD_IN_DOWN = {"ffn0": 0, "ffn1": 2, "ffn3": 5}
UNITS_BEFORE = {"moba": 0, "swa": 12, "fox": 18}
EXPS = {"moba": 2, "swa": 3, "fox": 2}
EXPS_BEFORE = {"moba": 0, "swa": 2 * HEADS, "fox": 5 * HEADS}
NORMED_BEFORE = {"swa": 0, "fox": 5}


def build(nc, a, out):
    ctx = ExitStack()
    with ctx:
        def sb(name, shape, dt=F32):
            return ctx.enter_context(nc.sbuf_tensor(name, shape, dt))

        def sem(name):
            return ctx.enter_context(nc.semaphore(name))

        raw_w = sb("raw_w", [P, SLOTS, HALF])
        w_hi = sb("w_hi", [P, SLOTS, HALF], F32R)
        w_lo = sb("w_lo", [P, SLOTS, HALF], F32R)
        xT = sb("xT", [P, C, T])
        hn = sb("hn", [P, C, T])
        in_hi = sb("in_hi", [P, C, T], F32R)
        in_lo = sb("in_lo", [P, C, T], F32R)
        sq = sb("sq", [P, 2, T])
        ln_ms = sb("ln_ms", [P, T])
        rstd = sb("rstd", [P, T])
        hid_hi = sb("hid_hi", [P, HID, T], F32R)
        hid_lo = sb("hid_lo", [P, HID, T], F32R)
        shared = sb("shared", [P, 3 * C * T])
        qT = shared[:, 0:C * T]
        kT = shared[:, C * T:2 * C * T]
        v_tok = shared[:, 2 * C * T:3 * C * T].rearrange("p (t d) -> p t d", t=2)
        mod_sum = shared[:, 0:3 * D]
        silu_gate = shared[:, 3072:3584]
        hidden = shared[:, 3584:4096]
        conv_gate = shared[:, 4096:4608]
        conv_up = shared[:, 4608:5120]
        ada_raw = sb("ada_raw", [P, 2, HALF])
        c_act = sb("c_act", [P, C])
        mods = sb("mods", [P, 6, 3 * C])
        mod_gain = sb("mod_gain", [P, 6, C])
        probs = sb("probs", [P, 3, KEYS])
        probsT = sb("probsT", [P, 2, KEYS])
        norm_sq = sb("norm_sq", [P, 2 * T])
        norm_rstd = sb("norm_rstd", [P, 2 * T])
        row_max = sb("row_max", [P, HEADS, 2])
        neg_max = sb("neg_max", [P, HEADS, 2])
        row_sum = sb("row_sum", [P, HEADS, 2])
        sink_exp = sb("sink_exp", [P, HEADS, 2])
        row_den = sb("row_den", [P, HEADS, 2])
        row_inv = sb("row_inv", [P, HEADS, 2])
        gq8 = sb("gq8", [P, 2])
        bias = sb("bias", [P, HEADS, 2 * P])
        rel_aug = sb("rel_aug", [BUCKETS + 1, HEADS])
        bucket_sb = sb("bucket_sb", [BUCKETS + 1, BIAS_ROW])
        bias_rows = sb("bias_rows", [HEADS, BIAS_ROW])
        tail_raw = sb("tail_raw", [P, C, HEADS])
        tail_hi = sb("tail_hi", [P, C, HEADS], F32R)
        tail_lo = sb("tail_lo", [P, C, HEADS], F32R)
        fl = sb("fl", [P, 2, HEADS])
        fl_abs = sb("fl_abs", [P, 2, HEADS])
        fl_exp = sb("fl_exp", [P, 2, HEADS])
        fl_ln = sb("fl_ln", [P, 2, HEADS])
        fl_min = sb("fl_min", [P, 2, HEADS])
        log_f = sb("log_f", [P, 2, HEADS])
        neg_F = sb("neg_F", [HEADS, T])
        vec = sb("vec", [P, V_COLS])
        ident = sb("ident", [P, P])
        ones = sb("ones", [P, P])
        head_ones = sb("head_ones", [P, P])
        neg_tri = sb("neg_tri", [P, T])
        mask = sb("mask", [P, KEYS])
        eps_col = sb("eps_col", [P, 1])

        B = [ctx.enter_context(nc.psum_tensor(f"bank{i}", [P, 512], F32)) for i in range(8)]
        GATE, UP, STAT, MODB = B[0], B[1], B[2], B[3]
        Y = B[4:8]
        SCORE = B[0:3]
        PT_BANK = [B[3], B[4]]
        O_BANK = [B[5], B[6]]
        FORGET = B[7]

        bias_dram = nc.dram_tensor("bias_scratch", (HEADS, P, BIAS_ROW), F32, kind="Internal")

        raw_in = [sem(f"raw_in{i}") for i in range(SLOTS)]
        hi_ready = sem("hi_ready")
        lo_ready = sem("lo_ready")
        pe_used = sem("pe_used")
        x_in = sem("x_in")
        vec_in = sem("vec_in")
        bias_in = sem("bias_in")
        bias_out = sem("bias_out")
        bias_back = sem("bias_back")
        tail_in = sem("tail_in")
        ada_in = [sem(f"ada_in{i}") for i in range(2)]
        out_done = sem("out_done")
        consts = sem("consts")
        memsets = sem("memsets")
        xt_ready = sem("xt_ready")
        x_ready = sem("x_ready")
        sq_done = sem("sq_done")
        sumsq = sem("sumsq")
        ln_done = sem("ln_done")
        rstd_done = sem("rstd_done")
        hn_done = sem("hn_done")
        in_hi_done = sem("in_hi_done")
        in_lo_done = sem("in_lo_done")
        silu_done = sem("silu_done")
        affine_done = sem("affine_done")
        tap_done = sem("tap_done")
        gate_taps = sem("gate_taps")
        hid_done = sem("hid_done")
        hid_hi_done = sem("hid_hi_done")
        hid_lo_done = sem("hid_lo_done")
        y_done = sem("y_done")
        c_done = sem("c_done")
        mod_step = sem("mod_step")
        mod_ps = sem("mod_ps")
        mod_add = sem("mod_add")
        mod_done = sem("mod_done")
        proj_free = sem("proj_free")
        norm_sq_done = sem("norm_sq_done")
        norm_stat = sem("norm_stat")
        norm_ln = sem("norm_ln")
        norm_rstd_done = sem("norm_rstd_done")
        k_swapped = sem("k_swapped")
        score_done = sem("score_done")
        max_done = sem("max_done")
        neg_max_done = sem("neg_max_done")
        exp_done = sem("exp_done")
        den_done = sem("den_done")
        inv_done = sem("inv_done")
        prob_done = sem("prob_done")
        pt_ps = sem("pt_ps")
        pt_done = sem("pt_done")
        pv_done = sem("pv_done")
        o_hi_done = sem("o_hi_done")
        o_lo_done = sem("o_lo_done")
        tail_hi_done = sem("tail_hi_done")
        tail_lo_done = sem("tail_lo_done")
        fl_ps = sem("fl_ps")
        fl_done = sem("fl_done")
        fl_act = sem("fl_act")
        logf_done = sem("logf_done")
        F_ps = sem("F_ps")
        F_done = sem("F_done")
        bias_ps = sem("bias_ps")
        bias_sb = sem("bias_sb")
        out_ps = sem("out_ps")
        out_low = sem("out_low")
        out_high = sem("out_high")
        up_taps = sem("up_taps")
        fl_part = sem("fl_part")
        gains_done = sem("gains_done")

        block = ctx.enter_context(nc.Block())

        def cols_view(w):
            return w.rearrange("(k p) n -> p k n", p=P)

        QKV_W = {"moba": cols_view(a["moba_w_qkv"][0]), "swa": cols_view(a["swa_w_in_2"][0]),
                 "fox": cols_view(a["fox_w_in_2"][0])}
        O_W = {"moba": cols_view(a["moba_w_o"][0]), "swa": cols_view(a["swa_w_out_2"][0]),
               "fox": cols_view(a["fox_w_out_2"][0])}
        UP_W = {"ffn0": cols_view(a["ffn_w_up"][0])}
        DOWN_W = {"ffn0": cols_view(a["ffn_w_down"][0])}
        for i in range(4):
            UP_W[f"ffn{i + 1}"] = cols_view(a["ffn_w13_2"][i // 2, i % 2])
            DOWN_W[f"ffn{i + 1}"] = cols_view(a["ffn_w2_2"][i // 2, i % 2])
        ADA_W = [cols_view(a["ada_w_2"][i]) for i in range(2)]

        hn_tok = hn[:].rearrange("p c t -> p (c t)").rearrange("p (t d) -> p t d", t=2)

        @block.sync
        def _(sp):
            sp.dma_start(hn_tok, a["x"][0].rearrange("(t p) d -> p t d", p=P)).then_inc(x_in, 16)
            sp.dma_start(vec[:], a["vectors"]).then_inc(vec_in, 16)

            def load(h, i, src):
                s = h % SLOTS
                if isinstance(i, int):
                    if h + 4 * i >= SLOTS:
                        sp.wait_ge(lo_ready, h + 4 * i - SLOTS + 1)
                else:
                    sp.wait_ge(lo_ready, i * 4 + (h - SLOTS + 1))
                sp.dma_start(raw_w[:, s, :].rearrange("p (k n) -> p k n", k=src.shape[1]), src).then_inc(raw_in[s], 16)

            def load_cols(h, i, w, col):
                for hf in range(2):
                    load(h + hf, i, w[:, 4 * hf:4 * hf + 4, bass.ds(col, COLS)])

            def attention(st):
                b, w, units = BASE[st], QKV_W[st], sum(QKV[st])
                for u in range(2):
                    load_cols(b + 2 * u, 0, w, u * COLS)
                with sp.Fori(1, units // 2) as i:
                    for u in range(2):
                        load_cols(b + 2 * u, i, w, i * (2 * COLS) + u * COLS)
                b += 2 * units
                for c in range(C):
                    load(b + c, 0, O_W[st][:, c:c + 1, :])

            def ffn(st):
                b, w = BASE[st], UP_W[st]
                with sp.Fori(0, UP_STEPS) as i:
                    load_cols(b, i, w, i * COLS)
                    load_cols(b + 2, i, w, i * COLS + FF)
                b += 4 * UP_STEPS
                w = DOWN_W[st]
                for c in range(2):
                    load(b + c, 0, w[:, c:c + 1, :])
                with sp.Fori(0, HID // 4) as i:
                    for c in range(4):
                        load(b + 2 + c, i, w[:, bass.ds(i * 4 + 2 + c, 1), :])

            for st in ORDER:
                (attention if st in QKV else ffn)(st)

            for t in range(2):
                sp.wait_ge(out_low, t + 1)
                sp.wait_ge(out_high, t + 1)
                sp.dma_start(out[0, t * P:(t + 1) * P, :], hn_tok[:, t, :]).then_inc(out_done, 16)
            sp.wait_ge(out_done, 32)

        @block.gpsimd
        def _(pool):
            def const(ins):
                ins.then_inc(consts, 1)

            pool.memset(ones[:], 1.0).then_inc(memsets, 1)
            pool.memset(ident[:], 0.0).then_inc(memsets, 1)
            pool.memset(neg_tri[:], -1.0).then_inc(memsets, 1)
            pool.memset(mask[:], 0.0).then_inc(memsets, 1)
            pool.memset(head_ones[:], 1.0).then_inc(memsets, 1)
            pool.memset(eps_col[:], EPS).then_inc(memsets, 1)
            pool.memset(rel_aug[:], MASKED).then_inc(memsets, 1)
            pool.wait_ge(memsets, 7)
            const(pool.affine_select(out=ident[:], in_=ident[:], compare_op=ALU.not_equal, fill=1.0, base=0,
                                     pattern=[[-1, P]], channel_multiplier=1))
            const(pool.affine_select(out=neg_tri[:], in_=neg_tri[:], compare_op=ALU.is_ge, fill=0.0, base=0,
                                     pattern=[[1, T]], channel_multiplier=-1))
            for at in (0, 2 * P):
                const(pool.affine_select(out=mask[:, at:at + P], in_=mask[:, at:at + P], compare_op=ALU.is_ge,
                                         fill=MASKED, base=0, pattern=[[-1, P]], channel_multiplier=1))
            const(pool.affine_select(out=head_ones[:, 0:DH], in_=head_ones[:, 0:DH], compare_op=ALU.is_ge, fill=0.0,
                                     base=DH - 1, pattern=[[0, DH]], channel_multiplier=-1))
            const(pool.affine_select(out=head_ones[:, DH:P], in_=head_ones[:, DH:P], compare_op=ALU.is_ge, fill=0.0,
                                     base=-DH, pattern=[[0, DH]], channel_multiplier=1))
            pool.dma_start(rel_aug[0:BUCKETS, :], a["rel_bias_2"]).then_inc(bias_in, 16)
            pool.dma_start(bucket_sb[:], a["bucket_rows"]).then_inc(bias_in, 16)
            pool.dma_start(tail_raw[:], QKV_W["fox"][:, :, 3 * D:3 * D + HEADS]).then_inc(tail_in, 16)
            pool.wait_ge(bias_sb, 1)
            pool.dma_start(bias_dram.ap(), bias_rows[:].unsqueeze(1).to_broadcast([HEADS, P, BIAS_ROW])).then_inc(bias_out, 16)
            pool.wait_ge(bias_out, 16)
            moved = bass.AP(tensor=bias_dram.ap().tensor, offset=P - 1,
                            ap=[[BIAS_ROW - 1, P], [P * BIAS_ROW, HEADS], [1, 2 * P]])
            pool.dma_start(bias[:], moved).then_inc(bias_back, 16)

            def load_ada(s, u, first):
                w = ADA_W[s // 3]
                for hf in range(2):
                    if not first:
                        pool.wait_ge(mod_step, u * C + (s * MOD_UNITS * C - C + 4 + 4 * hf))
                    pool.dma_start(ada_raw[:, hf, :].rearrange("p (k n) -> p k n", k=4),
                                   w[:, 4 * hf:4 * hf + 4, bass.ds(u * COLS + (s % 3) * 3 * D, COLS)]).then_inc(ada_in[hf], 16)

            load_ada(0, 0, True)
            for s in range(6):
                with pool.Fori(1 if s == 0 else 0, MOD_UNITS) as u:
                    load_ada(s, u, False)

        @block.scalar
        def _(act):
            def at(i, h):
                return h if isinstance(i, int) else i * 4 + h

            def split(h, i=0):
                s = h % SLOTS
                if isinstance(i, int):
                    act.wait_ge(raw_in[s], 16 * (h // SLOTS + 1))
                    if h >= SLOTS:
                        act.wait_ge(pe_used, h - SLOTS + 1)
                else:
                    act.wait_ge(raw_in[s], i * 16 + 16 * (h // SLOTS + 1))
                    act.wait_ge(pe_used, i * 4 + (h - SLOTS + 1))
                act.activation(w_hi[:, s, :], raw_w[:, s, :], ACT.Copy).then_inc(hi_ready, 1)

            def norm(name):
                n = NORMS.index(name)
                act.preload_act_table_set("natural_log_exp_and_others")
                for c in range(C):
                    act.wait_ge(x_ready, n * C + c + 1)
                    if n * C + c >= 2:
                        act.wait_ge(sumsq, n * C + c - 1)
                    act.activation(sq[:, c % 2, :], xT[:, c, :], ACT.Square).then_inc(sq_done, 1)
                if n > 0:
                    for h in deferred[name]:
                        split(h)
                act.wait_ge(sumsq, n * C + C)
                act.activation(ln_ms[:], STAT[:, 0:T], ACT.Ln, bias=eps_col[:, 0:1], scale=1.0 / D).then_inc(ln_done, 1)
                act.wait_ge(ln_done, n + 1)
                act.activation(rstd[:], ln_ms[:], ACT.Exp, scale=-0.5).then_inc(rstd_done, 1)
                if name == "final":
                    return
                m = SPLIT_NORMS.index(name)
                for c in range(C):
                    act.wait_ge(hn_done, m * C + c + 1)
                    if name in MOD_SET:
                        act.activation(in_hi[:, c, :], hn[:, c, :], ACT.Identity,
                                       bias=mods[:, MOD_SET[name], c:c + 1]).then_inc(in_hi_done, 1)
                    else:
                        act.activation(in_hi[:, c, :], hn[:, c, :], ACT.Copy).then_inc(in_hi_done, 1)

            def down_splits(b, n, last):
                n = n - 4 if last else n - 2
                for j in range(n % 4):
                    split(b + 4 + j)
                with act.Fori(0, n // 4) as i:
                    for j in range(4):
                        split(b + 4 + n % 4 + j, i)

            def qk_norm(u, bank):
                act.activation(norm_sq[:], bank[:], ACT.Square).then_inc(norm_sq_done, 1)

                def rest():
                    act.wait_ge(norm_stat, u + 1)
                    act.activation(norm_rstd[:], STAT[:], ACT.Ln, bias=eps_col[:, 0:1], scale=1.0 / DH).then_inc(norm_ln, 1)
                    act.wait_ge(norm_ln, u + 1)
                    act.activation(norm_rstd[:], norm_rstd[:], ACT.Exp, scale=-0.5).then_inc(norm_rstd_done, 1)
                return rest

            def proj_pair(b, i, normed):
                split(b + 4, i)
                split(b + 5, i)
                if normed is None:
                    split(b + 6, i)
                    split(b + 7, i)
                    return
                rest = qk_norm(normed, B[0])
                split(b + 6, i)
                rest()
                split(b + 7, i)
                if normed_pair_only_first:
                    return
                act.wait_ge(proj_free, normed_free + (0 if isinstance(i, int) else i * 2))
                qk_norm(normed + 1, B[1])()

            normed_pair_only_first = False
            normed_free = 0

            def attention(st):
                nonlocal normed_pair_only_first, normed_free
                ai = ATTN.index(st)
                b = BASE[st]
                norm(st)
                q, k, v = QKV[st]
                units = UNITS_BEFORE[st]
                if st == "moba":
                    with act.Fori(0, (q + k + v) // 2) as i:
                        proj_pair(b, i, None)
                else:
                    if st == "fox":
                        forget()
                    done = NORMED_BEFORE[st]
                    n_pairs = (q + k) // 2
                    normed_free = units + 3
                    with act.Fori(0, n_pairs) as i:
                        proj_pair(b, i, i * 2 + done)
                    b2 = b + 4 * n_pairs
                    if st == "swa":
                        normed_pair_only_first = True
                        proj_pair(b2, 0, done + 2 * n_pairs)
                        normed_pair_only_first = False
                        act.wait_ge(proj_free, units + q + k + 2)
                        kk = kT.rearrange("p (c t) -> p c t", t=T)
                        act.dma_start(kk[0:64, 2:4, :], kk[64:128, 0:2, :]).then_inc(k_swapped, 16)
                        act.dma_start(kk[64:128, 2:4, :], kk[0:64, 0:2, :]).then_inc(k_swapped, 16)
                    else:
                        with act.Fori(0, v // 2) as i:
                            proj_pair(b2, i, None)
                core(st, ai)
                down_splits(b + 2 * (q + k + v), 2 * O_UNITS, False)

            def core(st, ai):
                scale = DH ** -0.5 if st == "moba" else 1.0
                for t in range(HEADS + 5):
                    if t < HEADS:
                        h, g = t, ai * HEADS + t
                        act.wait_ge(neg_max_done, g + 1)
                        for blk, (lo, hi) in enumerate(((0, P), (P, KEYS))):
                            act.activation(probs[:, h % 3, lo:hi], probs[:, h % 3, lo:hi], ACT.Exp,
                                           bias=neg_max[:, h, blk:blk + 1], scale=scale,
                                           accum_out=row_sum[:, h, blk:blk + 1]).then_inc(exp_done, 1)
                        if st == "swa":
                            act.activation(sink_exp[:, h, :], neg_max[:, h, :], ACT.Exp,
                                           bias=vec[:, V_SINK + h:V_SINK + h + 1]).then_inc(exp_done, 1)
                    if 0 <= t - 2 < HEADS:
                        h, g = t - 2, ai * HEADS + t - 2
                        act.wait_ge(pt_ps, g + 1)
                        if h >= 2:
                            act.wait_ge(pv_done, g - 1)
                        act.activation(probsT[:, h % 2, :], PT_BANK[h % 2][:, 0:KEYS], ACT.Copy).then_inc(pt_done, 1)
                    if 0 <= t - 4 < HEADS and (t - 4) % 2 == 1:
                        p, g = (t - 4) // 2, ai * HEADS + t - 4
                        act.wait_ge(pv_done, g + 1)
                        act.activation(hid_hi[:, p, :], O_BANK[p % 2][:, 0:T], ACT.Copy).then_inc(o_hi_done, 1)

            def forget():
                act.wait_ge(fl_done, 1)
                act.activation(fl_abs[:], fl[:], ACT.Abs).then_inc(fl_act, 1)
                act.wait_ge(fl_act, 1)
                act.activation(fl_exp[:], fl_abs[:], ACT.Exp, scale=-1.0).then_inc(fl_act, 1)
                act.wait_ge(fl_act, 2)
                act.activation(fl_ln[:], fl_exp[:], ACT.Ln, bias=ones[:, 0:1]).then_inc(fl_act, 1)

            def ffn(st):
                f = int(st[-1])
                b = BASE[st]
                norm(st)
                act.preload_act_table_set("silu_and_others")
                with act.Fori(0, UP_STEPS) as i:
                    g = i + f * UP_STEPS
                    split(b + 4, i)
                    split(b + 5, i)
                    if f == 0:
                        for t in range(2):
                            act.activation(conv_gate[:, t * T:(t + 1) * T], GATE[:, t * T:(t + 1) * T], ACT.Identity,
                                           bias=conv_par(i, 0, t, 3), scale=conv_par(i, 0, t, 2)).then_inc(affine_done, 1)
                        split(b + 6, i)
                        split(b + 7, i)
                        for t in range(2):
                            act.activation(conv_up[:, t * T:(t + 1) * T], UP[:, t * T:(t + 1) * T], ACT.Identity,
                                           bias=conv_par(i, 1, t, 3), scale=conv_par(i, 1, t, 2)).then_inc(affine_done, 1)
                        act.wait_ge(gate_taps, i * 2 + 2)
                        act.activation(silu_gate, conv_gate, ACT.Silu).then_inc(silu_done, 1)
                    else:
                        act.activation(silu_gate, GATE[:], ACT.Silu).then_inc(silu_done, 1)
                        split(b + 6, i)
                        split(b + 7, i)
                    act.wait_ge(hid_done, g + 2)
                    act.activation(hid_hi[:, bass.ds(i * 2, 2), :].rearrange("p c t -> p (c t)"), hidden, ACT.Copy).then_inc(hid_hi_done, 1)
                down_splits(b + 4 * UP_STEPS, HID, st == ORDER[-1])

            def conv_par(i, kind, t, tap):
                return vec[:, bass.ds(i * 16 + (V_CONV + kind * 8 + t * 4 + tap), 1)]

            deferred = {}
            for n, name in enumerate(NORMS):
                deferred[name] = []
                if name in BASE and BASE[name]:
                    deferred[name] = [BASE[name] + 2, BASE[name] + 3]
            deferred["final"], deferred["ffn1"] = deferred["ffn1"], []

            act.wait_ge(vec_in, 16)
            act.activation(c_act[:], vec[:, V_C:V_C + C], ACT.Silu).then_inc(c_done, 1)
            for h in range(SLOTS):
                split(h)
            act.wait_ge(tail_in, 16)
            act.activation(tail_hi[:], tail_raw[:], ACT.Copy).then_inc(tail_hi_done, 1)
            for st in ORDER:
                (attention if st in QKV else ffn)(st)
                if st == "ffn0":
                    norm("final")
            for t in range(2):
                act.wait_ge(out_ps, 2 * t + 2)
                act.activation(hn_tok[:, t, 512:1024], B[2 * t + 1][:], ACT.Copy).then_inc(out_high, 1)

        @block.vector
        def _(dve):
            def split(h, i=0):
                s = h % SLOTS
                dve.wait_ge(hi_ready, h + 1 if isinstance(i, int) else i * 4 + (h + 1))
                dve.tensor_tensor(w_lo[:, s, :], raw_w[:, s, :], w_hi[:, s, :].bitcast(F32), ALU.subtract).then_inc(lo_ready, 1)

            def norm(name):
                n = NORMS.index(name)
                for h in deferred[name]:
                    split(h)
                if name in MOD_SET:
                    s = MOD_SET[name]
                    gain, shift = mod_gain[:, s, :], mods[:, s, 0:C]
                    dve.wait_ge(mod_done, 2 * (s + 1))
                else:
                    at = {"moba": V_MIX, "ffn0": V_FFN, "final": V_FINAL}[name]
                    gain, shift = vec[:, at:at + C], None
                dve.wait_ge(rstd_done, n + 1)
                if name == "final":
                    for c in range(C):
                        dve.scalar_tensor_tensor(out=xT[:, c, :], in0=xT[:, c, :], scalar=gain[:, c:c + 1], in1=rstd[:],
                                                 op0=ALU.mult, op1=ALU.mult).then_inc(x_ready, 1)
                    return
                m = SPLIT_NORMS.index(name)

                def low(c):
                    dve.wait_ge(in_hi_done, m * C + c + 1)
                    hi = in_hi[:, c, :].bitcast(F32)
                    if shift is None:
                        dve.tensor_tensor(in_lo[:, c, :], hn[:, c, :], hi, ALU.subtract).then_inc(in_lo_done, 1)
                    else:
                        dve.scalar_tensor_tensor(out=in_lo[:, c, :], in0=hn[:, c, :], scalar=shift[:, c:c + 1], in1=hi,
                                                 op0=ALU.add, op1=ALU.subtract).then_inc(in_lo_done, 1)

                for c in range(C):
                    dve.scalar_tensor_tensor(out=hn[:, c, :], in0=xT[:, c, :], scalar=gain[:, c:c + 1], in1=rstd[:],
                                             op0=ALU.mult, op1=ALU.mult).then_inc(hn_done, 1)
                    if c:
                        low(c - 1)
                low(C - 1)

            def residual(st):
                d = ORDER.index(st)
                for bk in range(4):
                    if bk < 3:
                        dve.wait_ge(y_done, 3 * d + bk + 1)
                    else:
                        dve.wait_ge(pe_used, (BASE[ORDER[d + 1]] if d + 1 < len(ORDER) else HALVES))
                    for t in range(2):
                        c = 2 * bk + t
                        y = Y[bk][:, t * T:(t + 1) * T]
                        if st in MOD_SET:
                            gate = mods[:, MOD_SET[st], 2 * C + c:2 * C + c + 1]
                            dve.scalar_tensor_tensor(out=xT[:, c, :], in0=y, scalar=gate, in1=xT[:, c, :],
                                                     op0=ALU.mult, op1=ALU.add).then_inc(x_ready, 1)
                        else:
                            dve.tensor_tensor(xT[:, c, :], y, xT[:, c, :], ALU.add).then_inc(x_ready, 1)

            def ada_unit(s, u):
                dst = mod_sum[:, bass.ds(u * COLS, COLS)]
                before = s * MOD_UNITS
                for k in range(C):
                    if k % 4 == 0:
                        dve.wait_ge(ada_in[k // 4], u * 16 + 16 * (before + 1))
                    src = ada_raw[:, k // 4, (k % 4) * COLS:(k % 4 + 1) * COLS]
                    if k == 0:
                        dve.tensor_scalar(dst, src, c_act[:, 0:1], None, ALU.mult).then_inc(mod_step, 1)
                    else:
                        dve.wait_ge(mod_step, u * C + (before * C + k))
                        dve.scalar_tensor_tensor(out=dst, in0=src, scalar=c_act[:, k:k + 1], in1=dst,
                                                 op0=ALU.mult, op1=ALU.add).then_inc(mod_step, 1)

            def mod_finish(s):
                dve.wait_ge(mod_ps, s + 1)
                m = mods[:, s, :]
                dve.tensor_tensor(m, MODB[:, 0:3 * C], vec[:, V_ADA_B + 3 * C * s:V_ADA_B + 3 * C * (s + 1)], ALU.add).then_inc(mod_add, 1)
                dve.wait_ge(mod_add, s + 1)
                dve.scalar_tensor_tensor(out=mod_gain[:, s, :], in0=m[:, C:2 * C], scalar=1.0,
                                         in1=vec[:, V_NORM_G + C * s:V_NORM_G + C * (s + 1)], op0=ALU.add, op1=ALU.mult).then_inc(mod_done, 1)
                half = 0.5 if s % 3 != 1 else 1.0
                dve.tensor_scalar(m[:, 2 * C:3 * C], m[:, 2 * C:3 * C], half, None, ALU.mult).then_inc(mod_done, 1)

            def down_splits(b, n, last, mod):
                n = n - 4 if last else n - 2
                for j in range(n % 4):
                    split(b + 4 + j)
                with dve.Fori(0, n // 4) as i:
                    for j in range(4):
                        split(b + 4 + n % 4 + j, i)
                        if mod is not None and j < 2:
                            ada_unit(mod, i * 2 + j)
                if mod is not None:
                    for u in range(2 * (n // 4), MOD_UNITS):
                        ada_unit(mod, u)

            def proj_pair(b, i, units, evac):
                split(b + 4, i)
                split(b + 5, i)
                split(b + 6, i)
                evac(0, B[0], at(pe_base(b, i), 2))
                split(b + 7, i)
                evac(1, B[1], at(pe_base(b, i), 4))

            def pe_base(b, i):
                return b if isinstance(i, int) else i * 4 + b

            def at(x, y):
                return x + y

            def attention(st):
                ai = ATTN.index(st)
                b = BASE[st]
                norm(st)
                if st == "fox":
                    forget()
                q, k, v = QKV[st]
                units = UNITS_BEFORE[st]

                def evac_qk(dst, gain, i, normed):
                    def evac(u, bank, used):
                        to = dst[:, bass.ds(i * (4 * T) + u * 2 * T, 2 * T)]
                        if normed is None:
                            dve.wait_ge(pe_used, used)
                            dve.tensor_copy(to, bank[:]).then_inc(proj_free, 1)
                        else:
                            dve.wait_ge(norm_rstd_done, normed + (u + 1))
                            dve.scalar_tensor_tensor(out=to, in0=bank[:], scalar=gain, in1=norm_rstd[:],
                                                     op0=ALU.mult, op1=ALU.mult).then_inc(proj_free, 1)
                    return evac

                def evac_v(i):
                    def evac(u, bank, used):
                        dve.wait_ge(pe_used, used)
                        dve.tensor_copy(v_tok[:, :, bass.ds(i * (2 * COLS) + u * COLS, COLS)],
                                        bank[:].rearrange("p (t n) -> p t n", t=2)).then_inc(proj_free, 1)
                    return evac

                done = NORMED_BEFORE.get(st)
                gains = {"moba": (None, None), "swa": (gq8[:, 0:1], vec[:, V_QK_G + 1:V_QK_G + 2]),
                         "fox": (gq8[:, 1:2], vec[:, V_QK_G + 3:V_QK_G + 4])}[st]
                with dve.Fori(0, q // 2) as i:
                    proj_pair(b, i, units, evac_qk(qT, gains[0], i, None if done is None else i * 2 + done))
                b2 = b + 2 * q
                if st == "swa":
                    k_evac, v_evac = evac_qk(kT, gains[1], 0, done + q), evac_v(0)
                    proj_pair(b2, 0, units + q,
                              lambda u, bank, used: k_evac(0, bank, used) if u == 0 else v_evac(0, bank, used))
                else:
                    with dve.Fori(0, k // 2) as i:
                        proj_pair(b2, i, units + q, evac_qk(kT, gains[1], i, None if done is None else i * 2 + done + q))
                    with dve.Fori(0, v // 2) as i:
                        proj_pair(b2 + 2 * k, i, units + q + k, evac_v(i))
                core(st, ai)
                down_splits(b + 2 * (q + k + v), 2 * O_UNITS, False, None)
                residual(st)

            def core(st, ai):
                if st == "swa":
                    dve.wait_ge(bias_back, 16)
                for t in range(HEADS + 6):
                    if t < HEADS:
                        h, g = t, ai * HEADS + t
                        dve.wait_ge(score_done, g + 1)
                        if h >= 3:
                            dve.wait_ge(pt_ps, g - 2)
                        for blk, (lo, hi) in enumerate(((0, P), (P, KEYS))):
                            add = mask[:, lo:hi] if st != "swa" else bias[:, h, P:2 * P] if blk == 0 else bias[:, h, :]
                            dve.tensor_tensor_reduce(out=probs[:, h % 3, lo:hi], in0=SCORE[h % 3][:, lo:hi], in1=add,
                                                     scale=1.0, scalar=3.0 * MASKED, op0=ALU.add, op1=ALU.max,
                                                     accum_out=row_max[:, h, blk:blk + 1]).then_inc(max_done, 1)
                        dve.wait_ge(max_done, 2 * (g + 1))
                        if st == "swa":
                            dve.tensor_scalar(neg_max[:, h, :], row_max[:, h, :], vec[:, V_SINK + h:V_SINK + h + 1], -1.0,
                                              ALU.max, ALU.mult).then_inc(neg_max_done, 1)
                        else:
                            dve.tensor_scalar(neg_max[:, h, :], row_max[:, h, :], -(DH ** -0.5) if st == "moba" else -1.0, None,
                                              ALU.mult).then_inc(neg_max_done, 1)
                    if 0 <= t - 1 < HEADS:
                        h, g = t - 1, ai * HEADS + t - 1
                        dve.wait_ge(exp_done, EXPS_BEFORE[st] + EXPS[st] * (h + 1))
                        den = row_sum[:, h, :]
                        if st == "swa":
                            dve.tensor_tensor(row_den[:, h, :], row_sum[:, h, :], sink_exp[:, h, :], ALU.add).then_inc(den_done, 1)
                            dve.wait_ge(den_done, h + 1)
                            den = row_den[:, h, :]
                        dve.reciprocal(row_inv[:, h, :], den).then_inc(inv_done, 1)
                        dve.wait_ge(inv_done, g + 1)
                        for blk, (lo, hi) in enumerate(((0, P), (P, KEYS))):
                            dve.tensor_scalar(probs[:, h % 3, lo:hi], probs[:, h % 3, lo:hi], row_inv[:, h, blk:blk + 1], None,
                                              ALU.mult).then_inc(prob_done, 1)
                    if 0 <= t - 5 < HEADS and (t - 5) % 2 == 1:
                        p = (t - 5) // 2
                        dve.wait_ge(o_hi_done, ai * C + p + 1)
                        dve.tensor_tensor(hid_lo[:, p, :], O_BANK[p % 2][:, 0:T], hid_hi[:, p, :].bitcast(F32), ALU.subtract).then_inc(o_lo_done, 1)

            def forget():
                dve.wait_ge(fl_ps, 1)
                for t in range(2):
                    dve.tensor_tensor(fl[:, t, :], FORGET[:, t * HEADS:(t + 1) * HEADS], vec[:, V_BF:V_BF + HEADS], ALU.add).then_inc(fl_part, 1)
                dve.wait_ge(fl_part, 2)
                dve.tensor_scalar(fl_min[:], fl[:], 0.0, None, ALU.min).then_inc(fl_done, 1)
                dve.wait_ge(fl_done, 1)
                dve.wait_ge(fl_act, 3)
                dve.tensor_tensor(log_f[:], fl_min[:], fl_ln[:], ALU.subtract).then_inc(logf_done, 1)
                dve.wait_ge(F_ps, 1)
                dve.tensor_copy(neg_F[:], FORGET[0:HEADS, T:2 * T]).then_inc(F_done, 1)

            def taps(bank, dst, i, kind, count):
                for lag in (1, 2):
                    for t in range(2):
                        if lag == 2:
                            dve.wait_ge(tap_done, i * 4 + (2 * kind + t + 1))
                        o = dst[:, t * T + lag:(t + 1) * T]
                        ins = dve.scalar_tensor_tensor(out=o, in0=bank[:, t * T:(t + 1) * T - lag], scalar=conv_par(i, kind, t, 2 - lag),
                                                       in1=o, op0=ALU.mult, op1=ALU.add)
                        ins.then_inc(tap_done if lag == 1 else count, 1)

            def conv_par(i, kind, t, tap):
                return vec[:, bass.ds(i * 16 + (V_CONV + kind * 8 + t * 4 + tap), 1)]

            def ffn(st):
                f = int(st[-1])
                b = BASE[st]
                norm(st)
                mod = MOD_IN_UP.get(st)
                with dve.Fori(0, UP_STEPS) as i:
                    g = i + f * UP_STEPS
                    split(b + 4, i)
                    split(b + 5, i)
                    if f == 0:
                        dve.wait_ge(affine_done, i * 4 + 2)
                        taps(GATE, conv_gate, i, 0, gate_taps)
                    split(b + 6, i)
                    split(b + 7, i)
                    if f == 0:
                        dve.wait_ge(affine_done, i * 4 + 4)
                        taps(UP, conv_up, i, 1, up_taps)
                        dve.wait_ge(up_taps, i * 2 + 2)
                    up = conv_up if f == 0 else UP[:]
                    dve.wait_ge(silu_done, g + 1)
                    dve.tensor_tensor(hidden, silu_gate, up, ALU.mult).then_inc(hid_done, 1)
                    if mod is not None:
                        ada_unit(mod, i)
                    dve.wait_ge(hid_hi_done, g + 1)
                    dve.tensor_tensor(hid_lo[:, bass.ds(i * 2, 2), :].rearrange("p c t -> p (c t)"), hidden,
                                      hid_hi[:, bass.ds(i * 2, 2), :].rearrange("p c t -> p (c t)").bitcast(F32), ALU.subtract).then_inc(hid_lo_done, 1)
                    dve.wait_ge(hid_lo_done, g + 1)
                if mod is not None:
                    ada_unit(mod, UP_STEPS)
                    mod_finish(mod)
                down = MOD_IN_DOWN.get(st)
                down_splits(b + 4 * UP_STEPS, HID, st == ORDER[-1], down)
                residual(st)
                if down is not None:
                    mod_finish(down)

            deferred = {}
            for n, name in enumerate(NORMS):
                deferred[name] = []
                if name in BASE and BASE[name]:
                    deferred[name] = [BASE[name] + 2, BASE[name] + 3]
            deferred["final"], deferred["ffn1"] = deferred["ffn1"], []

            dve.memset(row_max[:, 0, :], 0.0).then_inc(proj_free, 1)
            dve.memset(row_max[:, 1, :], 0.0).then_inc(proj_free, 1)
            dve.memset(row_max[:, 2, :], 0.0).then_inc(hid_done, 1)
            for c in range(C):
                dve.wait_ge(xt_ready, c // 2 + 1)
                dve.tensor_copy(xT[:, c, :], Y[c // 2][:, (c % 2) * T:(c % 2 + 1) * T]).then_inc(x_ready, 1)
            dve.wait_ge(vec_in, 16)
            dve.tensor_scalar(gq8[:, 0:1], vec[:, V_QK_G:V_QK_G + 1], DH ** -0.5, None, ALU.mult).then_inc(gains_done, 1)
            dve.tensor_scalar(gq8[:, 1:2], vec[:, V_QK_G + 2:V_QK_G + 3], DH ** -0.5, None, ALU.mult).then_inc(gains_done, 1)
            dve.wait_ge(gains_done, 2)
            dve.wait_ge(c_done, 1)
            for h in range(SLOTS):
                split(h)
            dve.wait_ge(bias_ps, 1)
            dve.tensor_copy(bias_rows[:], MODB[0:HEADS, 0:BIAS_ROW]).then_inc(bias_sb, 1)
            dve.wait_ge(tail_hi_done, 1)
            dve.tensor_tensor(tail_lo[:], tail_raw[:], tail_hi[:].bitcast(F32), ALU.subtract).then_inc(tail_lo_done, 1)
            for st in ORDER:
                (attention if st in QKV else ffn)(st)
                if st == "ffn0":
                    norm("final")
            for t in range(2):
                dve.wait_ge(out_ps, 2 * t + 1)
                dve.tensor_copy(hn_tok[:, t, 0:512], B[2 * t][:]).then_inc(out_low, 1)

        @block.tensor
        def _(pe):
            def mm(o, lhsT, rhs, start=False, stop=False):
                return pe.matmul(o, lhsT, rhs, start=start, stop=stop, skip_group_check=True)

            def weights(h, i):
                pe.wait_ge(lo_ready, h + 1 if isinstance(i, int) else i * 4 + (h + 1))

            def cols_half(h, i, hf, bank, m=None):
                weights(h, i)
                s = h % SLOTS
                for t in range(2):
                    o = bank[:, t * T:(t + 1) * T]
                    for kk in range(4):
                        k = 4 * hf + kk
                        if m is not None and t == 0:
                            pe.wait_ge(in_lo_done, m * C + k + 1)
                        at = kk * COLS + t * P
                        hi, lo = w_hi[:, s, at:at + P], w_lo[:, s, at:at + P]
                        mm(o, hi, in_hi[:, k, :], start=hf == 0 and t == 0 and kk == 0)
                        mm(o, hi, in_lo[:, k, :])
                        last = mm(o, lo, in_hi[:, k, :], stop=hf == 1 and kk == 3)
                last.then_inc(pe_used, 1)

            def v_half(h, i, hf, bank):
                weights(h, i)
                s = h % SLOTS
                for kk in range(4):
                    k = 4 * hf + kk
                    hi, lo = w_hi[:, s, kk * COLS:(kk + 1) * COLS], w_lo[:, s, kk * COLS:(kk + 1) * COLS]
                    for t in range(2):
                        o = bank[:, t * COLS:(t + 1) * COLS]
                        x_hi, x_lo = in_hi[:, k, t * P:(t + 1) * P], in_lo[:, k, t * P:(t + 1) * P]
                        mm(o, x_hi, hi, start=hf == 0 and t == 0 and kk == 0)
                        mm(o, x_hi, lo)
                        last = mm(o, x_lo, hi, stop=hf == 1 and kk == 3)
                last.then_inc(pe_used, 1)

            def rows_half(h, i, c, first=False, final=False):
                weights(h, i)
                s = h % SLOTS
                if isinstance(c, int):
                    x_hi, x_lo = hid_hi[:, c, :], hid_lo[:, c, :]
                else:
                    x_hi = hid_hi[:, bass.ds(c, 1), :].rearrange("p c t -> p (c t)")
                    x_lo = hid_lo[:, bass.ds(c, 1), :].rearrange("p c t -> p (c t)")
                for t in range(C):
                    o = Y[t // 2][:, (t % 2) * T:(t % 2 + 1) * T]
                    hi, lo = w_hi[:, s, t * P:(t + 1) * P], w_lo[:, s, t * P:(t + 1) * P]
                    mm(o, hi, x_hi, start=first and t % 2 == 0)
                    mm(o, hi, x_lo)
                    last = mm(o, lo, x_hi, stop=final)
                    if final and t % 2 == 1 and t < C - 1:
                        last.then_inc(y_done, 1)
                last.then_inc(pe_used, 1)

            def norm(name):
                n = NORMS.index(name)
                for c in range(C):
                    pe.wait_ge(sq_done, n * C + c + 1)
                    mm(STAT[:, 0:T], ones[:], sq[:, c % 2, :], start=c == 0, stop=c == C - 1).then_inc(sumsq, 1)

            def head_stats(u):
                pe.wait_ge(norm_sq_done, u + 1)
                mm(STAT[:], head_ones[:], norm_sq[:], start=True, stop=True).then_inc(norm_stat, 1)

            def unit_free(u):
                pe.wait_ge(proj_free, u + 1)

            def attention(st):
                ai = ATTN.index(st)
                b = BASE[st]
                norm(st)
                m = SPLIT_NORMS.index(st)
                q, k, v = QKV[st]
                units = UNITS_BEFORE[st]
                if st == "fox":
                    forget_logits(m)
                done = NORMED_BEFORE.get(st)
                qk_pairs = (q + k) // 2
                with pe.Fori(0, qk_pairs) as i:
                    unit_free(i * 2 + units)
                    for hf in range(2):
                        cols_half(b + hf, i, hf, B[0], m)
                    unit_free(i * 2 + (units + 1))
                    cols_half(b + 2, i, 0, B[1])
                    if done is not None:
                        head_stats(i * 2 + done)
                    cols_half(b + 3, i, 1, B[1])
                    if done is not None:
                        head_stats(i * 2 + (done + 1))
                b2, u2 = b + 4 * qk_pairs, units + 2 * qk_pairs
                if st == "swa":
                    unit_free(u2)
                    for hf in range(2):
                        cols_half(b2 + hf, 0, hf, B[0])
                    unit_free(u2 + 1)
                    v_half(b2 + 2, 0, 0, B[1])
                    head_stats(done + 2 * qk_pairs)
                    v_half(b2 + 3, 0, 1, B[1])
                else:
                    with pe.Fori(0, v // 2) as i:
                        unit_free(i * 2 + u2)
                        for hf in range(2):
                            v_half(b2 + hf, i, hf, B[0])
                        unit_free(i * 2 + (u2 + 1))
                        for hf in range(2):
                            v_half(b2 + 2 + hf, i, hf, B[1])
                pe.wait_ge(proj_free, units + q + k + v + 2)
                if st == "swa":
                    pe.wait_ge(k_swapped, 32)
                if st == "fox":
                    forget_sums()
                core(st, ai)
                b3 = b + 2 * (q + k + v)
                pe.wait_ge(o_lo_done, ai * C + C)
                for c in range(C):
                    rows_half(b3 + c, 0, c, first=c == 0, final=c == C - 1)

            def core(st, ai):
                def q_of(h):
                    at = (h % 2) * DH
                    return qT.rearrange("p (c t) -> p c t", t=T)[at:at + DH, h // 2, :]

                def k_of(h):
                    at = (h % 2) * DH
                    kk = kT.rearrange("p (c t) -> p c t", t=T)
                    if st != "swa":
                        return kk[at:at + DH, h // 2, :]
                    kv = h // 4
                    return kk[at:at + DH, kv // 2 + (2 if kv % 2 != h % 2 else 0), :]

                def v_of(h, t):
                    kv = h // 4 if st == "swa" else h
                    return v_tok[:, t, kv * DH:(kv + 1) * DH]

                for t in range(HEADS + 3):
                    if t < HEADS:
                        h, g = t, ai * HEADS + t
                        if h >= 3:
                            pe.wait_ge(max_done, 2 * (g - 2))
                        S = SCORE[h % 3]
                        for blk, (lo, hi) in enumerate(((0, P), (P, KEYS))):
                            n = hi - lo
                            ins = mm(S[:, lo:hi], q_of(h)[:, blk * P:(blk + 1) * P], k_of(h)[:, 0:n], start=True, stop=st != "fox")
                            if st == "fox":
                                ins = mm(S[:, lo:hi], ident[0:HEADS, h:h + 1].to_broadcast([HEADS, P]), neg_F[:, 0:n], stop=True)
                        ins.then_inc(score_done, 1)
                    if 0 <= t - 2 < HEADS:
                        h, g = t - 2, ai * HEADS + t - 2
                        pe.wait_ge(prob_done, 2 * (g + 1))
                        if h >= 2:
                            pe.wait_ge(pt_done, g - 1)
                        for j in range(3):
                            ins = pe.transpose(PT_BANK[h % 2][:, j * P:(j + 1) * P],
                                               probs[:, h % 3, (0, P, 2 * P)[j]:(0, P, 2 * P)[j] + P], ident[:])
                        ins.then_inc(pt_ps, 1)
                    if 0 <= t - 3 < HEADS:
                        h, g = t - 3, ai * HEADS + t - 3
                        pair = h // 2
                        pe.wait_ge(pt_done, g + 1)
                        if h % 2 == 0 and pair >= 2:
                            pe.wait_ge(o_lo_done, ai * C + pair - 1)
                        o = O_BANK[pair % 2][(h % 2) * DH:(h % 2 + 1) * DH, :]
                        mm(o[:, 0:T], v_of(h, 0), probsT[:, h % 2, 0:T], start=True)
                        mm(o[:, P:T], v_of(h, 1), probsT[:, h % 2, T:KEYS], stop=True).then_inc(pv_done, 1)

            def forget_logits(m):
                pe.wait_ge(tail_lo_done, 1)
                for t in range(2):
                    o = FORGET[:, t * HEADS:(t + 1) * HEADS]
                    for k in range(C):
                        pe.wait_ge(in_lo_done, m * C + k + 1)
                        x_hi, x_lo = in_hi[:, k, t * P:(t + 1) * P], in_lo[:, k, t * P:(t + 1) * P]
                        mm(o, x_hi, tail_hi[:, k, :], start=t == 0 and k == 0)
                        mm(o, x_hi, tail_lo[:, k, :])
                        last = mm(o, x_lo, tail_hi[:, k, :], stop=k == C - 1)
                last.then_inc(fl_ps, 1)
                pe.wait_ge(logf_done, 1)
                mm(FORGET[0:HEADS, T:2 * T], log_f[:, 0, :], neg_tri[:], start=True)
                mm(FORGET[0:HEADS, T + P:2 * T], log_f[:, 1, :], neg_tri[:, 0:P], stop=True).then_inc(F_ps, 1)

            def forget_sums():
                pe.wait_ge(F_done, 1)

            def ffn(st):
                f = int(st[-1])
                b = BASE[st]
                norm(st)
                m = SPLIT_NORMS.index(st)
                with pe.Fori(0, UP_STEPS) as i:
                    g = i + f * UP_STEPS
                    for hf in range(2):
                        cols_half(b + hf, i, hf, GATE, m)
                    pe.wait_ge(hid_done, g + 1)
                    for hf in range(2):
                        cols_half(b + 2 + hf, i, hf, UP)
                    if f == 0:
                        pe.wait_ge(gate_taps, i * 2 + 2)
                    else:
                        pe.wait_ge(silu_done, g + 1)
                if st in MOD_IN_UP:
                    mod_reduce(MOD_IN_UP[st])
                b2 = b + 4 * UP_STEPS
                hid = f * UP_STEPS
                for c in range(2):
                    pe.wait_ge(hid_lo_done, hid + 1)
                    rows_half(b2 + c, 0, c, first=c == 0)
                pe.wait_ge(hid_lo_done, hid + UP_STEPS)
                with pe.Fori(0, HID // 4 - 1) as i:
                    for j in range(4):
                        rows_half(b2 + 2 + j, i, i * 4 + (2 + j))
                for c in range(HID - 4, HID):
                    rows_half(b2 + c, 0, c, final=c == HID - 1)
                if st in MOD_IN_DOWN:
                    mod_reduce(MOD_IN_DOWN[st])

            def mod_reduce(s):
                pe.wait_ge(mod_step, C * MOD_UNITS * (s + 1))
                for c in range(3 * C):
                    ins = mm(MODB[:, c:c + 1], mod_sum[:, c * P:(c + 1) * P], ones[:, 0:1], start=c == 0, stop=True)
                ins.then_inc(mod_ps, 1)

            pe.wait_ge(consts, 6)
            pe.wait_ge(x_in, 16)
            for c in range(C):
                for t in range(2):
                    ins = pe.transpose(Y[c // 2][:, (c % 2) * T + t * P:(c % 2) * T + (t + 1) * P], hn_tok[:, t, c * P:(c + 1) * P], ident[:])
                if c % 2 == 1:
                    ins.then_inc(xt_ready, 1)
            pe.wait_ge(bias_in, 32)
            mm(MODB[0:HEADS, 0:BIAS_ROW], rel_aug[:], bucket_sb[:], start=True, stop=True).then_inc(bias_ps, 1)
            for st in ORDER:
                (attention if st in QKV else ffn)(st)
                if st == "ffn0":
                    norm("final")
            for t in range(2):
                for c in range(C):
                    pe.wait_ge(x_ready, len(NORMS) * C + c + 1)
                    ins = pe.transpose(B[2 * t + c // 4][:, (c % 4) * P:(c % 4 + 1) * P], xT[:, c, t * P:(t + 1) * P], ident[:])
                    if c % 4 == 3:
                        ins.then_inc(out_ps, 1)


WEIGHTS = ["x", "ffn_w_up", "ffn_w_down", "moba_w_qkv", "moba_w_o", "ada_w_2", "ffn_w13_2", "ffn_w2_2",
           "rel_bias_2", "swa_w_in_2", "swa_w_out_2", "fox_w_in_2", "fox_w_out_2"]


def bucket_rows():
    rows = np.zeros((BUCKETS + 1, BIAS_ROW), np.float32)
    exact = BUCKETS // 2
    for t in range(BIAS_ROW):
        n = 2 * P - 1 - t
        if not 0 <= n < MAX_DIST:
            rows[BUCKETS, t] = 1.0
            continue
        big = exact + int(np.log(np.float32(max(n, 1) / exact)) / np.log(MAX_DIST / exact) * (BUCKETS - exact)) if n >= exact else 0
        rows[min(n if n < exact else big, BUCKETS - 1), t] = 1.0
    return rows


def pack_vectors(inputs):
    def chunks(v):
        v = np.asarray(v)
        return np.moveaxis(v.reshape(-1, P), 1, 0)

    def rows(v):
        return np.broadcast_to(np.asarray(v).reshape(1, -1), (P, HEADS))

    taps = np.concatenate([np.asarray(inputs["ffn_conv_w"])[0], np.asarray(inputs["ffn_conv_b"])], axis=0)
    conv = taps.reshape(4, 2, UP_STEPS, 2, P).transpose(4, 2, 1, 3, 0).reshape(P, UP_STEPS * 16)

    def head(v):
        return np.tile(np.asarray(v).reshape(DH), 2)[:, None]

    parts = [chunks(inputs["norm_mix"]), chunks(inputs["norm_ffn"]), chunks(inputs["norm_final"]),
             chunks(inputs["norm_g_2"]), chunks(inputs["ada_b_2"]), chunks(inputs["c_2"]), conv,
             head(inputs["swa_q_g_2"]), head(inputs["swa_k_g_2"]), head(inputs["fox_q_g_2"]), head(inputs["fox_k_g_2"]),
             rows(inputs["swa_sink_2"]), rows(inputs["fox_b_f_2"])]
    return np.ascontiguousarray(np.concatenate(parts, axis=1))


def kernel(**inputs):
    import concourse.bacc as _bacc
    from concourse.bass_utils import run_bass_kernel_spmd as _run

    nc = _bacc.Bacc("TRN2", target_bir_lowering=False, num_devices=1)
    data = {name: np.ascontiguousarray(inputs[name]) for name in WEIGHTS}
    data["vectors"] = pack_vectors(inputs)
    data["bucket_rows"] = bucket_rows()
    arrays, aps = {}, {}
    for name, v in data.items():
        arrays[f"in_{name}_dram"] = v
        aps[name] = nc.dram_tensor(f"in_{name}_dram", v.shape, mybir.dt.from_np(v.dtype), kind="ExternalInput").ap()
    out = nc.dram_tensor("out_0_dram", (1, T, D), F32, kind="ExternalOutput").ap()
    build(nc, aps, out)
    r = _run(nc, [arrays], core_ids=[0])
    return r.results[0]["out_0_dram"]
```

```python
from contextlib import ExitStack

import numpy as np
import concourse.bass as bass
from concourse import mybir

ALU = mybir.AluOpType
ACT = mybir.ActivationFunctionType
F32 = mybir.dt.float32
F32R = mybir.dt.float32r

P = 128
D = 1024
T = 256
C = D // P
FF = 2816
HEADS = 16
DH = 64
COLS = 256
HALF = 4 * COLS
SLOTS = 4
PROBS = 4
UP_STEPS = FF // COLS
HID = FF // P
KEYS = 3 * P
EPS = 1e-6
MASKED = -1e30
BUCKETS, MAX_DIST = 32, 128
BIAS_ROW = 3 * P
CONSTS = 6

V_MIX, V_FFN, V_FINAL = 0, C, 2 * C
V_NORM_G = 3 * C
V_ADA_B = V_NORM_G + 6 * C
V_C = V_ADA_B + 6 * 3 * C
V_CONV = V_C + C
V_QK_G = V_CONV + UP_STEPS * 16
V_SINK = V_QK_G + 4
V_BF = V_SINK + HEADS
V_COLS = V_BF + HEADS

QKV = {"moba": (4, 4, 4), "swa": (4, 1, 1), "fox": (4, 4, 4)}
ATTN = ["moba", "swa", "fox"]
ORDER = ["moba", "ffn0", "ffn1", "swa", "ffn2", "ffn3", "fox", "ffn4"]
O_UNITS = D // COLS
BASE = {}
_h = 0
for _s in ORDER:
    BASE[_s] = _h
    _h += 2 * (sum(QKV[_s]) + O_UNITS) if _s in QKV else 2 * (2 * UP_STEPS + HID // 2)
HALVES = _h
NORMS = ["moba", "ffn0", "final", "ffn1", "swa", "ffn2", "ffn3", "fox", "ffn4"]
SPLIT_NORMS = [n for n in NORMS if n != "final"]
MOD_SET = {"ffn1": 0, "swa": 1, "ffn2": 2, "ffn3": 3, "fox": 4, "ffn4": 5}
MOD_UNITS = 3 * D // COLS
KIND = {"shift": 0, "scale": 1, "gate": 2}
KIND_ORDER = ["scale", "shift", "gate"]
GROUPS = 3 * len(MOD_SET)
SUMS = 4
SPLIT_EARLY = {"moba": [0, 1], "ffn1": [4], "swa": [7], "ffn2": [9, 10], "ffn3": [13], "fox": [16, 17]}
SPLIT_LATE = {"ffn0": [2, 3], "ffn1": [5, 6], "swa": [8], "ffn2": [11, 12], "ffn3": [14, 15]}
FIRST_GROUP = {"moba": 0, "ffn0": 2, "ffn1": 4, "swa": 8, "ffn2": 9, "ffn3": 13, "fox": 17}
REDUCE_BEFORE_END = {"ffn1": [4], "swa": [7], "ffn2": [9, 10], "ffn3": [13], "fox": [16]}
REDUCE_IN_NORM = {"ffn0": [0, 1], "final": [2], "ffn1": [3], "swa": [5, 6], "ffn2": [8], "ffn3": [11, 12], "fox": [14, 15],
                  "ffn4": [17]}
UNITS_BEFORE = {"moba": 0, "swa": 12, "fox": 18}
EXPS = {"moba": 2, "swa": 3, "fox": 2}
EXPS_BEFORE = {"moba": 0, "swa": 2 * HEADS, "fox": 5 * HEADS}
NORMED_BEFORE = {"swa": 0, "fox": 5}
EARLY = {"moba": 3, "swa": 2, "fox": 3}


def build(nc, a, out):
    ctx = ExitStack()
    with ctx:
        def sb(name, shape, dt=F32):
            return ctx.enter_context(nc.sbuf_tensor(name, shape, dt))

        def sem(name):
            return ctx.enter_context(nc.semaphore(name))

        raw_w = sb("raw_w", [P, SLOTS, HALF])
        w_hi = sb("w_hi", [P, SLOTS, HALF], F32R)
        w_lo = sb("w_lo", [P, SLOTS, HALF], F32R)
        xT = sb("xT", [P, C, T])
        in_hi = sb("in_hi", [P, C, T], F32R)
        in_lo = sb("in_lo", [P, C, T], F32R)
        rstd = sb("rstd", [P, T])
        with ExitStack() as meanwhile:
            def under(name, shape):
                return meanwhile.enter_context(nc.sbuf_tensor(name, shape, F32))

            hn = under("hn", [P, C, T])
            spare = under("spare", [P, (HID - C) * T])
            under("kept", [P, C, T])
            forget_mask = under("forget_mask", [P, HEADS, P])
        hid_hi = sb("hid_hi", [P, HID, T], F32R)
        hid_lo = sb("hid_lo", [P, HID, T], F32R)
        probs = spare[:, 0:PROBS * KEYS].rearrange("p (n k) -> p n k", n=PROBS)
        probsT = spare[:, 1536:1536 + 2 * KEYS].rearrange("p (n k) -> p n k", n=2)
        norm_sq = spare[:, 2304:2304 + 2 * T]
        norm_rstd = spare[:, 2816:2816 + 2 * T]
        shared = sb("shared", [P, 3 * C * T])
        qT = shared[:, 0:C * T]
        kT = shared[:, C * T:2 * C * T]
        k_swa, q_swa, k_swap = shared[:, 0:2 * T], shared[:, 2 * T:10 * T], shared[:, 10 * T:12 * T]
        v_tok = shared[:, 2 * C * T:3 * C * T].rearrange("p (t d) -> p t d", t=2)
        sq = shared[:, 0:C * T].rearrange("p (c t) -> p c t", c=C)
        silu_gate = shared[:, 3072:3584]
        hidden = shared[:, 3584:4096]
        conv_gate = shared[:, 4096:4608]
        conv_up = shared[:, 4608:5120]
        ada_raw = sb("ada_raw", [P, 2, D])
        with nc.sbuf_tensor("mod_sum", [P, SUMS, D], F32) as mod_sum:
            pass
        mod_lo = sb("mod_lo", [P, SUMS, D], F32R)
        mod_hi = sb("mod_hi", [P, 2, D], F32R)
        ones_r = sb("ones_r", [P, 2], F32R)
        c_act = sb("c_act", [P, C])
        mods = sb("mods", [P, 6, 3 * C])
        mod_gain = sb("mod_gain", [P, 6, C])
        row_max = sb("row_max", [P, HEADS, 2])
        neg_max = sb("neg_max", [P, HEADS, 2])
        row_sum = sb("row_sum", [P, HEADS, 2])
        sink_exp = sb("sink_exp", [P, HEADS, 2])
        row_den = sb("row_den", [P, HEADS, 2])
        row_inv = sb("row_inv", [P, HEADS, 2])
        qk_gain = sb("qk_gain", [P, 16])
        bias = sb("bias", [P, HEADS, 2 * P])
        rel_aug = sb("rel_aug", [BUCKETS + 1, HEADS])
        bucket_sb = sb("bucket_sb", [BUCKETS + 1, BIAS_ROW])
        bias_rows = sb("bias_rows", [HEADS, BIAS_ROW])
        tail_raw = sb("tail_raw", [P, C, HEADS])
        tail_hi = sb("tail_hi", [P, C, HEADS], F32R)
        tail_lo = sb("tail_lo", [P, C, HEADS], F32R)
        fl = sb("fl", [P, 2, HEADS])
        fl_abs = sb("fl_abs", [P, 2, HEADS])
        fl_exp = sb("fl_exp", [P, 2, HEADS])
        fl_ln = sb("fl_ln", [P, 2, HEADS])
        fl_min = sb("fl_min", [P, 2, HEADS])
        log_f = sb("log_f", [P, 2, HEADS])
        neg_F = sb("neg_F", [HEADS, T])
        vec = sb("vec", [P, V_COLS])
        ident = sb("ident", [P, P])
        ones = sb("ones", [P, P])
        head_ones = sb("head_ones", [P, P])
        neg_tri = sb("neg_tri", [P, T])
        mask = sb("mask", [P, KEYS])
        eps_col = sb("eps_col", [P, 1])

        B = [ctx.enter_context(nc.psum_tensor(f"bank{i}", [P, 512], F32)) for i in range(8)]
        GATE, UP, STAT, MODB = B[0], B[1], B[2], B[3]
        FIRST = [B[5], B[1]]
        V_BANK = [B[5], B[6]]
        X_BANK = B[4:8]
        Y_FFN = [(B[4], 0), (B[4], T), (B[5], 0), (B[5], T), (B[6], 0), (B[6], T), (B[7], 0), (B[0], 0)]
        Y_ATTN = [(B[0], 0), (B[0], T), (B[1], 0), (B[1], T), (B[2], 0), (B[2], T), (B[7], 0), (B[4], 0)]
        SCORE = B[0:3]
        PT_BANK = [B[3], B[4]]
        O_BANK = [B[5], B[6]]
        FORGET = B[7]
        OUT_BANK = [(B[1], B[2]), (B[3], B[0])]

        forget_dram = nc.dram_tensor("forget_scratch", (HEADS, T), F32, kind="Internal")
        bias_dram = nc.dram_tensor("bias_scratch", (HEADS, P, BIAS_ROW), F32, kind="Internal")

        raw_in = [sem(f"raw_in{i}") for i in range(SLOTS)]
        hi_ready = sem("hi_ready")
        lo_ready = sem("lo_ready")
        pe_used = sem("pe_used")
        x_in = sem("x_in")
        vec_in = sem("vec_in")
        bias_in = sem("bias_in")
        bias_out = sem("bias_out")
        bias_back = sem("bias_back")
        tail_in = sem("tail_in")
        ada_in = [sem(f"ada_in{i}") for i in range(2)]
        out_done = sem("out_done")
        consts = sem("consts")
        memsets = sem("memsets")
        xt_ready = sem("xt_ready")
        x_ready = sem("x_ready")
        sq_done = sem("sq_done")
        sq_added = sem("sq_added")
        sumsq = sem("sumsq")
        ln_done = sem("ln_done")
        rstd_done = sem("rstd_done")
        hn_done = sem("hn_done")
        in_hi_done = sem("in_hi_done")
        in_lo_done = sem("in_lo_done")
        silu_done = sem("silu_done")
        affine_done = sem("affine_done")
        tap_done = sem("tap_done")
        gate_taps = sem("gate_taps")
        hid_done = sem("hid_done")
        hid_hi_done = sem("hid_hi_done")
        hid_lo_done = sem("hid_lo_done")
        y_done = sem("y_done")
        c_done = sem("c_done")
        mod_zero = sem("mod_zero")
        mod_step = sem("mod_step")
        mod_hi_done = sem("mod_hi_done")
        mod_lo_done = sem("mod_lo_done")
        mod_ps = sem("mod_ps")
        mod_add = sem("mod_add")
        mod_done = sem("mod_done")
        ones_done = sem("ones_done")
        proj_free = sem("proj_free")
        norm_sq_done = sem("norm_sq_done")
        norm_stat = sem("norm_stat")
        norm_ln = sem("norm_ln")
        norm_rstd_done = sem("norm_rstd_done")
        k_swapped = sem("k_swapped")
        score_done = sem("score_done")
        max_done = sem("max_done")
        neg_max_done = sem("neg_max_done")
        exp_done = sem("exp_done")
        den_done = sem("den_done")
        inv_done = sem("inv_done")
        prob_done = sem("prob_done")
        pt_ps = sem("pt_ps")
        pt_done = sem("pt_done")
        pv_done = sem("pv_done")
        o_hi_done = sem("o_hi_done")
        o_lo_done = sem("o_lo_done")
        tail_hi_done = sem("tail_hi_done")
        tail_lo_done = sem("tail_lo_done")
        fl_ps = sem("fl_ps")
        fl_done = sem("fl_done")
        fl_act = sem("fl_act")
        logf_done = sem("logf_done")
        F_ps = sem("F_ps")
        F_done = sem("F_done")
        F_out = sem("F_out")
        F_back = sem("F_back")
        forget_masked = sem("forget_masked")
        bias_ps = sem("bias_ps")
        bias_sb = sem("bias_sb")
        out_ps = sem("out_ps")
        out_low = sem("out_low")
        out_high = sem("out_high")
        up_taps = sem("up_taps")
        fl_part = sem("fl_part")
        gains_done = sem("gains_done")

        block = ctx.enter_context(nc.Block())

        def y_tiles(st):
            return Y_ATTN if st in QKV else Y_FFN

        def stat_bank(name):
            before = NORMS.index(name) - 1
            return B[6] if before >= 0 and NORMS[before] in QKV else STAT

        def cols_view(w):
            return w.rearrange("(k p) n -> p k n", p=P)

        QKV_W = {"moba": cols_view(a["moba_w_qkv"][0]), "swa": cols_view(a["swa_w_in_2"][0]),
                 "fox": cols_view(a["fox_w_in_2"][0])}
        O_W = {"moba": cols_view(a["moba_w_o"][0]), "swa": cols_view(a["swa_w_out_2"][0]),
               "fox": cols_view(a["fox_w_out_2"][0])}
        UP_W = {"ffn0": cols_view(a["ffn_w_up"][0])}
        DOWN_W = {"ffn0": cols_view(a["ffn_w_down"][0])}
        for i in range(4):
            UP_W[f"ffn{i + 1}"] = cols_view(a["ffn_w13_2"][i // 2, i % 2])
            DOWN_W[f"ffn{i + 1}"] = cols_view(a["ffn_w2_2"][i // 2, i % 2])
        ADA_W = [cols_view(a["ada_w_2"][i]) for i in range(2)]

        hn_tok = hn[:].rearrange("p c t -> p (c t)").rearrange("p (t d) -> p t d", t=2)

        @block.sync
        def _(sp):
            sp.dma_start(hn_tok, a["x"][0].rearrange("(t p) d -> p t d", p=P)).then_inc(x_in, 16)
            sp.dma_start(vec[:], a["vectors"]).then_inc(vec_in, 16)

            def load(h, i, src):
                s = h % SLOTS
                if isinstance(i, int):
                    if h + 4 * i >= SLOTS:
                        sp.wait_ge(lo_ready, h + 4 * i - SLOTS + 1)
                else:
                    sp.wait_ge(lo_ready, i * 4 + (h - SLOTS + 1))
                sp.dma_start(raw_w[:, s, :].rearrange("p (k n) -> p k n", k=src.shape[1]), src).then_inc(raw_in[s], 16)

            def load_cols(h, i, w, col):
                for hf in range(2):
                    load(h + hf, i, w[:, 4 * hf:4 * hf + 4, bass.ds(col, COLS)])

            def load_first(b, w, cols):
                for hf in range(2):
                    for u in range(2):
                        load(b + 2 * hf + u, 0, w[:, 4 * hf:4 * hf + 4, bass.ds(cols[u], COLS)])

            def attention(st):
                b, w, units = BASE[st], QKV_W[st], sum(QKV[st])
                if st == "swa":
                    load_first(b, w, (D, 0))
                    for u, col in enumerate((COLS, 2 * COLS, 3 * COLS, D + COLS)):
                        load_cols(b + 4 + 2 * u, 0, w, col)
                else:
                    load_first(b, w, (0, COLS))
                    with sp.Fori(1, units // 2) as i:
                        for u in range(2):
                            load_cols(b + 2 * u, i, w, i * (2 * COLS) + u * COLS)
                b += 2 * units
                for c in range(C):
                    load(b + c, 0, O_W[st][:, c:c + 1, :])

            def ffn(st):
                b, w = BASE[st], UP_W[st]
                load_first(b, w, (0, FF))
                with sp.Fori(1, UP_STEPS) as i:
                    load_cols(b, i, w, i * COLS)
                    load_cols(b + 2, i, w, i * COLS + FF)
                b += 4 * UP_STEPS
                w = DOWN_W[st]
                for c in range(2):
                    load(b + c, 0, w[:, c:c + 1, :])
                with sp.Fori(0, HID // 4) as i:
                    for c in range(4):
                        load(b + 2 + c, i, w[:, bass.ds(i * 4 + 2 + c, 1), :])

            for st in ORDER:
                (attention if st in QKV else ffn)(st)

            for t in range(2):
                sp.wait_ge(out_low, t + 1)
                sp.wait_ge(out_high, t + 1)
                sp.dma_start(out[0, t * P:(t + 1) * P, :], hn_tok[:, t, :]).then_inc(out_done, 16)
            sp.wait_ge(out_done, 32)

        @block.gpsimd
        def _(pool):
            def const(ins):
                ins.then_inc(consts, 1)

            pool.memset(ident[:], 0.0).then_inc(memsets, 1)
            pool.wait_ge(memsets, 1)
            const(pool.affine_select(out=ident[:], in_=ident[:], compare_op=ALU.not_equal, fill=1.0, base=0,
                                     pattern=[[-1, P]], channel_multiplier=1))
            pool.memset(ones[:], 1.0).then_inc(memsets, 1)
            pool.memset(eps_col[:], EPS).then_inc(memsets, 1)
            pool.memset(neg_tri[:], -1.0).then_inc(memsets, 1)
            pool.memset(mask[:], 0.0).then_inc(memsets, 1)
            pool.memset(head_ones[:], 1.0).then_inc(memsets, 1)
            pool.memset(rel_aug[:], MASKED).then_inc(memsets, 1)
            pool.wait_ge(memsets, 7)
            const(pool.affine_select(out=neg_tri[:], in_=neg_tri[:], compare_op=ALU.is_ge, fill=0.0, base=0,
                                     pattern=[[1, T]], channel_multiplier=-1))
            for at in (0, 2 * P):
                const(pool.affine_select(out=mask[:, at:at + P], in_=mask[:, at:at + P], compare_op=ALU.is_ge,
                                         fill=MASKED, base=0, pattern=[[-1, P]], channel_multiplier=1))
            const(pool.affine_select(out=head_ones[:, 0:DH], in_=head_ones[:, 0:DH], compare_op=ALU.is_ge, fill=0.0,
                                     base=DH - 1, pattern=[[0, DH]], channel_multiplier=-1))
            const(pool.affine_select(out=head_ones[:, DH:P], in_=head_ones[:, DH:P], compare_op=ALU.is_ge, fill=0.0,
                                     base=-DH, pattern=[[0, DH]], channel_multiplier=1))
            pool.dma_start(rel_aug[0:BUCKETS, :], a["rel_bias_2"]).then_inc(bias_in, 16)
            pool.dma_start(bucket_sb[:], a["bucket_rows"]).then_inc(bias_in, 16)
            pool.dma_start(tail_raw[:], QKV_W["fox"][:, :, 3 * D:3 * D + HEADS]).then_inc(tail_in, 16)
            def bias_tiles():
                pool.wait_ge(bias_sb, 1)
                pool.dma_start(bias_dram.ap(), bias_rows[:].unsqueeze(1).to_broadcast([HEADS, P, BIAS_ROW])).then_inc(bias_out, 16)
                pool.wait_ge(bias_out, 16)
                moved = bass.AP(tensor=bias_dram.ap().tensor, offset=P - 1,
                                ap=[[BIAS_ROW - 1, P], [P * BIAS_ROW, HEADS], [1, 2 * P]])
                pool.dma_start(bias[:], moved).then_inc(bias_back, 16)

            def group(q):
                s, kind = q // 3, KIND[KIND_ORDER[q % 3]]
                w, col = ADA_W[s // 3], ((s % 3) * 3 + kind) * D
                if q >= SUMS:
                    pool.wait_ge(mod_ps, q - SUMS + 1)
                pool.memset(mod_sum[:, q % SUMS, :], 0.0).then_inc(mod_zero, 1)

                def load_ada(i, j):
                    if not (q == 0 and isinstance(i, int)):
                        pool.wait_ge(mod_step, i * 2 + (C * q + j - 1))
                    k = j if isinstance(i, int) and i == 0 else i * 2 + j
                    pool.dma_start(ada_raw[:, j, :].unsqueeze(1), w[:, bass.ds(k, 1), col:col + D]).then_inc(ada_in[j], 16)

                if q == 0:
                    for j in range(2):
                        load_ada(0, j)
                with pool.Fori(1 if q == 0 else 0, C // 2) as i:
                    for j in range(2):
                        load_ada(i, j)

            for q in range(GROUPS):
                group(q)
                if q == 1:
                    bias_tiles()
            pool.wait_ge(F_done, 1)
            pool.dma_start(forget_dram.ap(), neg_F[:]).then_inc(F_out, 16)
            pool.wait_ge(F_out, 16)
            pool.dma_start(bias[:], bass.AP(tensor=forget_dram.ap().tensor, offset=0,
                                            ap=[[0, P], [T, HEADS], [1, T]])).then_inc(F_back, 16)
            pool.wait_ge(F_back, 16)
            causal = mask[:, 0:P].unsqueeze(1).to_broadcast([P, HEADS, P])
            pool.tensor_tensor(forget_mask[:], bias[:, :, 0:P], causal, ALU.add).then_inc(forget_masked, 1)
            pool.tensor_tensor(bias[:, :, P:2 * P], bias[:, :, P:2 * P], causal, ALU.add).then_inc(forget_masked, 1)

        @block.scalar
        def _(act):
            def at(i, h):
                return h if isinstance(i, int) else i * 4 + h

            def split(h, i=0):
                s = h % SLOTS
                if isinstance(i, int):
                    h += 4 * i
                    act.wait_ge(raw_in[s], 16 * (h // SLOTS + 1))
                    if h >= SLOTS:
                        act.wait_ge(pe_used, h - SLOTS + 1)
                else:
                    act.wait_ge(raw_in[s], i * 16 + 16 * (h // SLOTS + 1))
                    act.wait_ge(pe_used, i * 4 + (h - SLOTS + 1))
                act.activation(w_hi[:, s, :], raw_w[:, s, :], ACT.Copy).then_inc(hi_ready, 1)

            def mod_split(groups):
                for q in groups:
                    act.wait_ge(mod_step, C * (q + 1))
                    if q >= 2:
                        act.wait_ge(mod_ps, q - 1)
                    act.activation(mod_hi[:, q % 2, :], mod_sum[:, q % SUMS, :], ACT.Copy).then_inc(mod_hi_done, 1)

            def norm(name):
                n = NORMS.index(name)
                if n == 0 or NORMS[n - 1] in BASE and NORMS[n - 1] not in QKV:
                    act.preload_act_table_set("natural_log_exp_and_others")
                for c in range(C):
                    act.wait_ge(x_ready, n * C + c + 1)
                    act.activation(sq[:, c, :], xT[:, c, :], ACT.Square).then_inc(sq_done, 1)
                if n == 0:
                    for h in range(2):
                        split(h)
                act.wait_ge(sumsq, n + 1)
                act.activation(rstd[:], stat_bank(name)[:, 0:T], ACT.Ln, bias=eps_col[:, 0:1], scale=1.0 / D).then_inc(ln_done, 1)
                act.wait_ge(ln_done, n + 1)
                act.activation(rstd[:], rstd[:], ACT.Exp, scale=-0.5).then_inc(rstd_done, 1)
                if name == "final":
                    return
                m = SPLIT_NORMS.index(name)
                for c in range(C):
                    act.wait_ge(hn_done, m * C + c + 1)
                    if name in MOD_SET:
                        act.activation(in_hi[:, c, :], hn[:, c, :], ACT.Identity,
                                       bias=mods[:, MOD_SET[name], c:c + 1]).then_inc(in_hi_done, 1)
                    else:
                        act.activation(in_hi[:, c, :], hn[:, c, :], ACT.Copy).then_inc(in_hi_done, 1)
                    if c in (2, 4):
                        split(BASE[name] + 1 + c // 2)

            def down_splits(b, n, st):
                n = n - 4 if st == ORDER[-1] else n - 2
                for j in range(n % 4):
                    split(b + 4 + j)
                if n // 4 > 1:
                    with act.Fori(0, n // 4 - 1) as i:
                        for j in range(4):
                            split(b + 4 + n % 4 + j, i)
                if st in QKV:
                    for j in range(4):
                        split(b + n + j)
                    mod_split(SPLIT_LATE.get(st, []))
                else:
                    mod_split(SPLIT_LATE.get(st, []))
                    for j in range(4):
                        split(b + n + j)

            def squares(bank, used):
                act.wait_ge(pe_used, used)
                act.activation(norm_sq, bank[:], ACT.Square).then_inc(norm_sq_done, 1)

            def qk_rstd(u, unit):
                act.wait_ge(norm_stat, u + 1)
                act.wait_ge(proj_free, unit + 2)
                act.activation(norm_rstd, STAT[:], ACT.Ln, bias=eps_col[:, 0:1], scale=1.0 / DH).then_inc(norm_ln, 1)
                act.wait_ge(norm_ln, u + 1)
                act.activation(norm_rstd, norm_rstd, ACT.Exp, scale=-0.5).then_inc(norm_rstd_done, 1)

            def attention(st):
                ai = ATTN.index(st)
                b = BASE[st]
                norm(st)
                q, k, v = QKV[st]
                units, done = UNITS_BEFORE[st], NORMED_BEFORE.get(st)
                pairs = (q + k) // 2
                for j in range(4, 6):
                    split(b + j)
                if done is not None:
                    squares(FIRST[0], b + 3)
                split(b + 6)
                if done is not None:
                    qk_rstd(done, units)
                    squares(FIRST[1], b + 4)
                split(b + 7)
                if st == "fox":
                    forget()

                def normed_pair(b, i, u, unit, bank=B[0], last=False):
                    qk_rstd(u - 1, unit - 1)
                    split(b + 4, i)
                    squares(bank, i * 4 + (b + 2))
                    split(b + 5, i)
                    split(b + 6, i)
                    qk_rstd(u, unit)
                    if not last:
                        squares(B[1], i * 4 + (b + 4))
                        split(b + 7, i)

                with act.Fori(1, pairs) as i:
                    if done is None:
                        for j in range(4, 8):
                            split(b + j, i)
                    else:
                        normed_pair(b, i, i * 2 + done, i * 2 + units)
                b2 = b + 4 * pairs
                if st == "swa":
                    normed_pair(b2, 0, done + 2 * pairs, units + 2 * pairs, V_BANK[0], last=True)
                    core(st, ai, 0, EARLY[st])
                else:
                    if done is not None:
                        qk_rstd(done + 2 * pairs - 1, units + 2 * pairs - 1)
                    with act.Fori(0, v // 2 - 1) as i:
                        for j in range(4, 8):
                            split(b2 + j, i)
                    b3 = b2 + 2 * v - 4
                    split(b3 + 4)
                    split(b3 + 5)
                    core(st, ai, 0, EARLY[st])
                core(st, ai, EARLY[st], HEADS + 6)
                b3 = b + 2 * (q + k + v)
                for j in range(3 if st == "swa" else 2, 4):
                    split(b3 + j)
                mod_split(SPLIT_EARLY.get(st, []))
                down_splits(b + 2 * (q + k + v), 2 * O_UNITS, st)

            def core(st, ai, begin, end):
                scale = DH ** -0.5 if st == "moba" else 1.0
                for t in range(begin, end):
                    if 0 <= t - 5 < HEADS and (t - 5) % 2 == 1:
                        p, g = (t - 5) // 2, ai * HEADS + t - 5
                        act.wait_ge(pv_done, g + 1)
                        act.activation(hid_hi[:, p, :], O_BANK[p % 2][:, 0:T], ACT.Copy).then_inc(o_hi_done, 1)
                    if 0 <= t - 3 < HEADS:
                        h, g = t - 3, ai * HEADS + t - 3
                        act.wait_ge(pt_ps, g + 1)
                        if h >= 2:
                            act.wait_ge(pv_done, g - 1)
                        act.activation(probsT[:, h % 2, :], PT_BANK[h % 2][:, 0:KEYS], ACT.Copy).then_inc(pt_done, 1)
                    if t < HEADS:
                        h, g = t, ai * HEADS + t
                        act.wait_ge(neg_max_done, g + 1)
                        for blk, (lo, hi) in enumerate(((0, P), (P, KEYS))):
                            act.activation(probs[:, h % PROBS, lo:hi], probs[:, h % PROBS, lo:hi], ACT.Exp,
                                           bias=neg_max[:, h, blk:blk + 1], scale=scale,
                                           accum_out=row_sum[:, h, blk:blk + 1]).then_inc(exp_done, 1)
                        if st == "swa":
                            act.activation(sink_exp[:, h, :], neg_max[:, h, :], ACT.Exp,
                                           bias=vec[:, V_SINK + h:V_SINK + h + 1]).then_inc(exp_done, 1)

            def forget():
                act.wait_ge(fl_done, 1)
                act.activation(fl_abs[:], fl[:], ACT.Abs).then_inc(fl_act, 1)
                act.wait_ge(fl_act, 1)
                act.activation(fl_exp[:], fl_abs[:], ACT.Exp, scale=-1.0).then_inc(fl_act, 1)
                act.wait_ge(fl_act, 2)
                act.activation(fl_ln[:], fl_exp[:], ACT.Ln, bias=ones[:, 0:1]).then_inc(fl_act, 1)

            def ffn(st):
                f = int(st[-1])
                b = BASE[st]
                norm(st)
                act.preload_act_table_set("silu_and_others")
                if f == 0:
                    act.wait_ge(tail_in, 16)
                    act.activation(tail_hi[:], tail_raw[:], ACT.Copy).then_inc(tail_hi_done, 1)

                def step(i):
                    first = isinstance(i, int)
                    g = i + f * UP_STEPS
                    for j in (4, 5, 6) if first else (4, 5):
                        split(b + j, i)
                    if f == 0:
                        for t in range(2):
                            act.activation(conv_gate[:, t * T:(t + 1) * T], GATE[:, t * T:(t + 1) * T], ACT.Identity,
                                           bias=conv_par(i, 0, t, 3), scale=conv_par(i, 0, t, 2)).then_inc(affine_done, 1)
                        for j in (7,) if first else (6, 7):
                            split(b + j, i)
                        for t in range(2):
                            act.activation(conv_up[:, t * T:(t + 1) * T], UP[:, t * T:(t + 1) * T], ACT.Identity,
                                           bias=conv_par(i, 1, t, 3), scale=conv_par(i, 1, t, 2)).then_inc(affine_done, 1)
                        act.wait_ge(gate_taps, i * 2 + 2)
                        act.activation(silu_gate, conv_gate, ACT.Silu).then_inc(silu_done, 1)
                    else:
                        act.activation(silu_gate, GATE[:], ACT.Silu).then_inc(silu_done, 1)
                        for j in (7,) if first else (6, 7):
                            split(b + j, i)
                    act.wait_ge(hid_done, g + 2)
                    act.activation(hid_hi[:, bass.ds(i * 2, 2), :].rearrange("p c t -> p (c t)"), hidden, ACT.Copy).then_inc(hid_hi_done, 1)

                step(0)
                with act.Fori(1, UP_STEPS) as i:
                    step(i)
                mod_split(SPLIT_EARLY.get(st, []))
                down_splits(b + 4 * UP_STEPS, HID, st)

            def conv_par(i, kind, t, tap):
                return vec[:, bass.ds(i * 16 + (V_CONV + kind * 8 + t * 4 + tap), 1)]

            act.wait_ge(vec_in, 16)
            act.activation(c_act[:], vec[:, V_C:V_C + C], ACT.Silu).then_inc(c_done, 1)
            act.wait_ge(consts, CONSTS)
            act.activation(ones_r[:], ones[:, 0:2], ACT.Copy).then_inc(ones_done, 1)
            for st in ORDER:
                (attention if st in QKV else ffn)(st)
                if st == "ffn0":
                    norm("final")
            for t in range(2):
                act.wait_ge(out_ps, 2 * t + 2)
                act.activation(hn_tok[:, t, 512:1024], OUT_BANK[t][1][:], ACT.Copy).then_inc(out_high, 1)

        @block.vector
        def _(dve):
            def split(h, i=0):
                s = h % SLOTS
                dve.wait_ge(hi_ready, i * 4 + (h + 1))
                dve.tensor_tensor(w_lo[:, s, :], raw_w[:, s, :], w_hi[:, s, :].bitcast(F32), ALU.subtract).then_inc(lo_ready, 1)

            def pair_add(n, p):
                dve.wait_ge(sq_done, n * C + 2 * p + 2)
                dve.tensor_tensor(sq[:, 2 * p, :], sq[:, 2 * p, :], sq[:, 2 * p + 1, :], ALU.add).then_inc(sq_added, 1)

            def norm(name):
                n = NORMS.index(name)
                if name in MOD_SET:
                    s = MOD_SET[name]
                    gain, shift = mod_gain[:, s, :], mods[:, s, 0:C]
                    dve.wait_ge(mod_done, 3 * s + 2)
                else:
                    at = {"moba": V_MIX, "ffn0": V_FFN, "final": V_FINAL}[name]
                    gain, shift = vec[:, at:at + C], None
                if n == 0:
                    for h in range(2):
                        split(h)
                if NORMS[n - 1] in QKV and n > 0:
                    mod_split(SPLIT_LATE.get(NORMS[n - 1], []))
                dve.wait_ge(rstd_done, n + 1)
                if name == "final":
                    for c in range(C):
                        dve.scalar_tensor_tensor(out=xT[:, c, :], in0=xT[:, c, :], scalar=gain[:, c:c + 1], in1=rstd[:],
                                                 op0=ALU.mult, op1=ALU.mult).then_inc(x_ready, 1)
                        if c in (3, 5, 7):
                            pair_add(n + 1, (c - 3) // 2)
                    mod_finish(REDUCE_IN_NORM[name])
                    return
                m = SPLIT_NORMS.index(name)

                def low(c):
                    dve.wait_ge(in_hi_done, m * C + c + 1)
                    hi = in_hi[:, c, :].bitcast(F32)
                    if shift is None:
                        dve.tensor_tensor(in_lo[:, c, :], hn[:, c, :], hi, ALU.subtract).then_inc(in_lo_done, 1)
                    else:
                        dve.scalar_tensor_tensor(out=in_lo[:, c, :], in0=hn[:, c, :], scalar=shift[:, c:c + 1], in1=hi,
                                                 op0=ALU.add, op1=ALU.subtract).then_inc(in_lo_done, 1)

                for c in range(C):
                    dve.scalar_tensor_tensor(out=hn[:, c, :], in0=xT[:, c, :], scalar=gain[:, c:c + 1], in1=rstd[:],
                                             op0=ALU.mult, op1=ALU.mult).then_inc(hn_done, 1)
                    if c:
                        low(c - 1)
                    if c in (4, 6):
                        split(BASE[name] + c // 2)
                low(C - 1)
                mod_finish(REDUCE_IN_NORM.get(name, []))

            def residual(st):
                d = ORDER.index(st)
                tiles = y_tiles(st)
                last = st == ORDER[-1]
                n = None if last else NORMS.index(st) + 1
                if st in MOD_SET:
                    dve.wait_ge(mod_done, 3 * MOD_SET[st] + 3)
                for c, (bank, at) in enumerate(tiles):
                    if c in (0, 2, 4, 6):
                        dve.wait_ge(y_done, 4 * d + c // 2 + 1)
                    elif c == C - 1:
                        dve.wait_ge(pe_used, BASE[ORDER[d + 1]] if not last else HALVES)
                    y = bank[:, at:at + T]
                    if st in MOD_SET:
                        gate = mods[:, MOD_SET[st], 2 * C + c:2 * C + c + 1]
                        dve.scalar_tensor_tensor(out=xT[:, c, :], in0=y, scalar=gate, in1=xT[:, c, :],
                                                 op0=ALU.mult, op1=ALU.add).then_inc(x_ready, 1)
                    else:
                        dve.tensor_tensor(xT[:, c, :], y, xT[:, c, :], ALU.add).then_inc(x_ready, 1)
                    if not last and c in (3, 5, 6):
                        pair_add(n, (c - 2) // 2)

            def ada(q, i, j, off=0):
                k = i * 2 + (j + off)
                dve.wait_ge(ada_in[j], i * 16 + 16 * (C // 2 * q + off // 2 + 1))
                if not isinstance(i, int) or C * q + k > 0:
                    dve.wait_ge(mod_step, i * 2 + (C * q + j + off))
                dve.wait_ge(mod_zero, q + 1)
                sums = mod_sum[:, q % SUMS, :]
                dve.scalar_tensor_tensor(out=sums, in0=ada_raw[:, j, :], scalar=c_act[:, bass.ds(k, 1)], in1=sums,
                                         op0=ALU.mult, op1=ALU.add).then_inc(mod_step, 1)

            def mod_split(groups):
                for q in groups:
                    dve.wait_ge(mod_hi_done, q + 1)
                    sums = mod_sum[:, q % SUMS, :]
                    dve.tensor_tensor(mod_lo[:, q % SUMS, :], sums, mod_hi[:, q % 2, :].bitcast(F32), ALU.subtract).then_inc(mod_lo_done, 1)

            adds = [0]

            def mod_finish(groups):
                for at, q in enumerate(groups):
                    s, kind = q // 3, KIND_ORDER[q % 3]
                    dve.wait_ge(mod_ps, q + 1)
                    m = mods[:, s, KIND[kind] * C:(KIND[kind] + 1) * C]
                    total = MODB[:, 2 * C * at:2 * C * (at + 1)].rearrange("p (c two) -> p c two", two=2)[:, :, 0]
                    v = V_ADA_B + 3 * C * s + KIND[kind] * C
                    half = kind == "gate" and s % 3 != 1
                    ins = dve.tensor_tensor(m, total, vec[:, v:v + C], ALU.add)
                    if kind == "shift" or kind == "gate" and not half:
                        ins.then_inc(mod_done, 1)
                        continue
                    ins.then_inc(mod_add, 1)
                    adds[0] += 1
                    dve.wait_ge(mod_add, adds[0])
                    if kind == "scale":
                        dve.scalar_tensor_tensor(out=mod_gain[:, s, :], in0=m, scalar=1.0, in1=vec[:, V_NORM_G + C * s:V_NORM_G + C * (s + 1)],
                                                 op0=ALU.add, op1=ALU.mult).then_inc(mod_done, 1)
                    else:
                        dve.tensor_scalar(m, m, 0.5, None, ALU.mult).then_inc(mod_done, 1)

            def attention(st):
                ai = ATTN.index(st)
                b = BASE[st]
                norm(st)
                q, k, v = QKV[st]
                units, done = UNITS_BEFORE[st], NORMED_BEFORE.get(st)
                pairs = (q + k) // 2
                group = FIRST_GROUP[st]
                gains = None if done is None else qk_gain[:, (ai - 1) * 8:ai * 8]

                def evac(unit, bank, used):
                    to = shared[:, bass.ds(unit * (2 * T), 2 * T)]
                    if done is None:
                        dve.wait_ge(pe_used, used)
                        dve.tensor_copy(to, bank[:]).then_inc(proj_free, 1)
                    else:
                        dve.wait_ge(norm_rstd_done, unit + (done + 1))
                        dve.scalar_tensor_tensor(out=to, in0=bank[:], scalar=gains[:, bass.ds(unit, 1)], in1=norm_rstd,
                                                 op0=ALU.mult, op1=ALU.mult).then_inc(proj_free, 1)

                def evac_v(i, u, bank, used):
                    dve.wait_ge(pe_used, used)
                    dve.tensor_copy(v_tok[:, :, bass.ds(i * (2 * COLS) + u * COLS, COLS)],
                                    bank[:].rearrange("p (t n) -> p t n", t=2)).then_inc(proj_free, 1)

                for j in range(4, 7):
                    split(b + j)
                evac(0, FIRST[0], b + 3)
                split(b + 7)
                if done is None:
                    evac(1, FIRST[1], b + 4)
                for j in range(2):
                    ada(group, 0, j)
                if st == "moba":
                    dve.wait_ge(bias_ps, 1)
                    dve.tensor_copy(bias_rows[:], MODB[0:HEADS, 0:BIAS_ROW]).then_inc(bias_sb, 1)
                if st == "fox":
                    forget()
                with dve.Fori(1, pairs) as i:
                    if done is not None:
                        evac(i * 2 - 1, B[1], None)
                    split(b + 4, i)
                    split(b + 5, i)
                    if done is None:
                        evac(i * 2, B[0], i * 4 + (b + 2))
                    ada(group, i, 0)
                    split(b + 6, i)
                    if done is not None:
                        evac(i * 2, B[0], None)
                    split(b + 7, i)
                    if done is None:
                        evac(i * 2 + 1, B[1], i * 4 + (b + 4))
                    ada(group, i, 1)
                b2 = b + 4 * pairs
                if st == "swa":
                    evac(2 * pairs - 1, B[1], None)
                    for to, at in ((0, DH), (DH, 0)):
                        dve.tensor_copy(k_swap[to:to + DH, :], k_swa[at:at + DH, :]).then_inc(k_swapped, 1)
                    split(b2 + 4)
                    split(b2 + 5)
                    split(b2 + 6)
                    evac(2 * pairs, V_BANK[0], None)
                    core(st, ai, 0, EARLY[st])
                    evac_v(0, 0, V_BANK[1], b2 + 4)
                else:
                    if done is not None:
                        evac(2 * pairs - 1, B[1], None)
                    if st == "fox":
                        forget_sums()
                    last = v // 2 - 1
                    with dve.Fori(0, last) as i:
                        split(b2 + 4, i)
                        split(b2 + 5, i)
                        evac_v(i, 0, V_BANK[0], i * 4 + (b2 + 2))
                        if st == "moba":
                            ada(group + 1, i, 0)
                        split(b2 + 6, i)
                        split(b2 + 7, i)
                        evac_v(i, 1, V_BANK[1], i * 4 + (b2 + 4))
                        if st == "moba":
                            ada(group + 1, i, 1)
                    b3 = b2 + 4 * last
                    for j in range(2):
                        split(b3 + 4 + j)
                        if st == "moba":
                            ada(group + 1, last, j)
                    evac_v(last, 0, V_BANK[0], b3 + 2)
                    core(st, ai, 0, EARLY[st])
                    evac_v(last, 1, V_BANK[1], b3 + 4)
                core(st, ai, EARLY[st], HEADS + 7)
                b3 = b + 2 * (q + k + v)
                for j in range(3 if st == "swa" else 2, 4):
                    split(b3 + j)
                mod_split(SPLIT_EARLY.get(st, []))
                left = {"moba": [(2, 0), (2, 1)], "swa": [(8, 2), (8, 3)], "fox": []}[st]
                b3 = b + 2 * (q + k + v)
                for j in range(2 * O_UNITS - 2):
                    split(b3 + 4 + j)
                    if j % 2 == 1 and j // 2 < len(left):
                        for hf in range(2):
                            ada(left[j // 2][0], left[j // 2][1], hf)
                mod_finish(REDUCE_BEFORE_END.get(st, []))
                residual(st)

            def core(st, ai, begin, end):
                if st == "swa":
                    dve.wait_ge(bias_back, 16)
                if st == "fox":
                    dve.wait_ge(forget_masked, 2)
                for t in range(begin, end):
                    if 0 <= t - 6 < HEADS and (t - 6) % 2 == 1:
                        p = (t - 6) // 2
                        dve.wait_ge(o_hi_done, ai * C + p + 1)
                        dve.tensor_tensor(hid_lo[:, p, :], O_BANK[p % 2][:, 0:T], hid_hi[:, p, :].bitcast(F32), ALU.subtract).then_inc(o_lo_done, 1)
                    if t < HEADS:
                        h, g = t, ai * HEADS + t
                        dve.wait_ge(score_done, g + 1)
                        if h >= PROBS:
                            dve.wait_ge(pt_ps, g - PROBS + 1)
                        for blk, (lo, hi) in enumerate(((0, P), (P, KEYS))):
                            add = {"moba": mask[:, lo:hi], "swa": bias[:, h, P:2 * P] if blk == 0 else bias[:, h, :],
                                   "fox": forget_mask[:, h, :] if blk == 0 else bias[:, h, :]}[st]
                            dve.tensor_tensor_reduce(out=probs[:, h % PROBS, lo:hi], in0=SCORE[h % 3][:, lo:hi], in1=add,
                                                     scale=1.0, scalar=3.0 * MASKED, op0=ALU.add, op1=ALU.max,
                                                     accum_out=row_max[:, h, blk:blk + 1]).then_inc(max_done, 1)
                        dve.wait_ge(max_done, 2 * (g + 1))
                        if st == "swa":
                            dve.tensor_scalar(neg_max[:, h, :], row_max[:, h, :], vec[:, V_SINK + h:V_SINK + h + 1], -1.0,
                                              ALU.max, ALU.mult).then_inc(neg_max_done, 1)
                        else:
                            dve.tensor_scalar(neg_max[:, h, :], row_max[:, h, :], -(DH ** -0.5) if st == "moba" else -1.0, None,
                                              ALU.mult).then_inc(neg_max_done, 1)
                    if 0 <= t - 1 < HEADS:
                        h, g = t - 1, ai * HEADS + t - 1
                        dve.wait_ge(exp_done, EXPS_BEFORE[st] + EXPS[st] * (h + 1))
                        den = row_sum[:, h, :]
                        if st == "swa":
                            dve.tensor_tensor(row_den[:, h, :], row_sum[:, h, :], sink_exp[:, h, :], ALU.add).then_inc(den_done, 1)
                            dve.wait_ge(den_done, h + 1)
                            den = row_den[:, h, :]
                        dve.reciprocal(row_inv[:, h, :], den).then_inc(inv_done, 1)
                        dve.wait_ge(inv_done, g + 1)
                        for blk, (lo, hi) in enumerate(((0, P), (P, KEYS))):
                            dve.tensor_scalar(probs[:, h % PROBS, lo:hi], probs[:, h % PROBS, lo:hi], row_inv[:, h, blk:blk + 1], None,
                                              ALU.mult).then_inc(prob_done, 1)
                    if st == "moba" and t in (4, 7, 10, 13):
                        ada(1, 2 + (t - 4) // 6, (t - 4) // 3 % 2)

            def forget():
                dve.wait_ge(fl_ps, 1)
                for t in range(2):
                    dve.tensor_tensor(fl[:, t, :], FORGET[:, t * HEADS:(t + 1) * HEADS], vec[:, V_BF:V_BF + HEADS], ALU.add).then_inc(fl_part, 1)
                dve.wait_ge(fl_part, 2)
                dve.tensor_scalar(fl_min[:], fl[:], 0.0, None, ALU.min).then_inc(fl_done, 1)
                dve.wait_ge(fl_done, 1)
                dve.wait_ge(fl_act, 3)
                dve.tensor_tensor(log_f[:], fl_min[:], fl_ln[:], ALU.subtract).then_inc(logf_done, 1)

            def forget_sums():
                dve.wait_ge(F_ps, 1)
                dve.tensor_copy(neg_F[:], FORGET[0:HEADS, T:2 * T]).then_inc(F_done, 1)

            def taps(bank, dst, i, kind, count):
                for lag in (1, 2):
                    for t in range(2):
                        if lag == 2:
                            dve.wait_ge(tap_done, i * 4 + (2 * kind + t + 1))
                        o = dst[:, t * T + lag:(t + 1) * T]
                        ins = dve.scalar_tensor_tensor(out=o, in0=bank[:, t * T:(t + 1) * T - lag], scalar=conv_par(i, kind, t, 2 - lag),
                                                       in1=o, op0=ALU.mult, op1=ALU.add)
                        ins.then_inc(tap_done if lag == 1 else count, 1)

            def conv_par(i, kind, t, tap):
                return vec[:, bass.ds(i * 16 + (V_CONV + kind * 8 + t * 4 + tap), 1)]

            def ffn(st):
                f = int(st[-1])
                b = BASE[st]
                norm(st)
                group = FIRST_GROUP.get(st)

                def step(i):
                    g = i + f * UP_STEPS
                    first = isinstance(i, int)
                    for j in (4, 5, 6) if first else (4, 5):
                        split(b + j, i)
                    if f == 0:
                        dve.wait_ge(affine_done, i * 4 + 2)
                        taps(GATE, conv_gate, i, 0, gate_taps)
                    for j in (7,) if first else (6, 7):
                        split(b + j, i)
                    if f == 0:
                        dve.wait_ge(affine_done, i * 4 + 4)
                        taps(UP, conv_up, i, 1, up_taps)
                        dve.wait_ge(up_taps, i * 2 + 2)
                    up = conv_up if f == 0 else UP[:]
                    dve.wait_ge(silu_done, g + 1)
                    dve.tensor_tensor(hidden, silu_gate, up, ALU.mult).then_inc(hid_done, 1)

                def low(i):
                    g = i + f * UP_STEPS
                    dve.wait_ge(hid_hi_done, g + 1)
                    dve.tensor_tensor(hid_lo[:, bass.ds(i * 2, 2), :].rearrange("p c t -> p (c t)"), hidden,
                                      hid_hi[:, bass.ds(i * 2, 2), :].rearrange("p c t -> p (c t)").bitcast(F32), ALU.subtract).then_inc(hid_lo_done, 1)
                    dve.wait_ge(hid_lo_done, g + 1)

                step(0)
                low(0)
                if f == 0:
                    dve.wait_ge(tail_hi_done, 1)
                    dve.tensor_tensor(tail_lo[:], tail_raw[:], tail_hi[:].bitcast(F32), ALU.subtract).then_inc(tail_lo_done, 1)
                if group is None or f == 0:
                    with dve.Fori(1, UP_STEPS) as i:
                        step(i)
                        low(i)
                else:
                    for at, n in ((0, 4), (1, 4), (2, 2)):
                        with dve.Fori(1 + 4 * at, 1 + 4 * at + n) as i:
                            step(i)
                            for j in range(2):
                                ada(group + at, i, j, -2 - C * at)
                            low(i)
                mod_split(SPLIT_EARLY.get(st, []))
                b2 = b + 4 * UP_STEPS
                n = HID - 4 if st == ORDER[-1] else HID - 2
                peeled = (n - 1) % 4 + 1
                third = None if group is None else group if f == 0 else group + 2
                for j in range(peeled):
                    split(b2 + 4 + j)
                    if group is not None:
                        ada(third, 2 + j // 2, j % 2)
                loops = (n - peeled) // 4

                def splits(i):
                    for j in range(4):
                        split(b2 + peeled + j, i)
                        yield j

                for j in splits(1):
                    if group is not None:
                        ada(third + 1, j // 2, j % 2)
                with dve.Fori(2, loops) as i:
                    for j in splits(i):
                        if group is not None and j % 2 == 1:
                            ada(third + 1, i, j // 2)
                late = SPLIT_LATE.get(st, [])
                for j in splits(loops):
                    if j == 0:
                        mod_split(late[0:1])
                    elif j == 2:
                        mod_split(late[1:])
                mod_finish(REDUCE_BEFORE_END.get(st, []))
                residual(st)

            dve.memset(row_max[:, 0, :], 0.0).then_inc(proj_free, 1)
            dve.memset(row_max[:, 1, :], 0.0).then_inc(proj_free, 1)
            dve.memset(row_max[:, 2, :], 0.0).then_inc(hid_done, 1)
            for c in range(C):
                dve.wait_ge(xt_ready, c // 2 + 1)
                dve.tensor_copy(xT[:, c, :], X_BANK[c // 2][:, (c % 2) * T:(c % 2 + 1) * T]).then_inc(x_ready, 1)
                if c in (3, 5, 7):
                    pair_add(0, (c - 3) // 2)
            dve.wait_ge(vec_in, 16)
            for at, n, g in ((0, 1, 1), (1, 4, 0), (8, 4, 2), (12, 4, 3)):
                dve.tensor_scalar(qk_gain[:, at:at + n], vec[:, V_QK_G + g:V_QK_G + g + 1].to_broadcast([P, n]),
                                  DH ** -0.5 if g % 2 == 0 else 1.0, None, ALU.mult).then_inc(gains_done, 1)
            dve.wait_ge(gains_done, 4)
            dve.wait_ge(c_done, 1)
            dve.wait_ge(consts, CONSTS)
            for st in ORDER:
                (attention if st in QKV else ffn)(st)
                if st == "ffn0":
                    norm("final")
            for t in range(2):
                dve.wait_ge(out_ps, 2 * t + 1)
                dve.tensor_copy(hn_tok[:, t, 0:512], OUT_BANK[t][0][:]).then_inc(out_low, 1)

        @block.tensor
        def _(pe):
            def mm(o, lhsT, rhs, start=False, stop=False):
                return pe.matmul(o, lhsT, rhs, start=start, stop=stop, skip_group_check=True)

            def weights(h, i):
                pe.wait_ge(lo_ready, i * 4 + (h + 1))

            def cols_half(h, i, hf, bank, m=None, between=None):
                weights(h, i)
                s = h % SLOTS
                for t in range(2):
                    o = bank[:, t * T:(t + 1) * T]
                    for kk in range(4):
                        k = 4 * hf + kk
                        if m is not None and t == 0:
                            pe.wait_ge(in_lo_done, m * C + k + 1)
                        at = kk * COLS + t * P
                        hi, lo = w_hi[:, s, at:at + P], w_lo[:, s, at:at + P]
                        mm(o, hi, in_hi[:, k, :], start=hf == 0 and t == 0 and kk == 0)
                        mm(o, hi, in_lo[:, k, :])
                        last = mm(o, lo, in_hi[:, k, :], stop=hf == 1 and kk == 3)
                    if t == 0 and between is not None:
                        between()
                last.then_inc(pe_used, 1)

            def v_half(h, i, hf, bank):
                weights(h, i)
                s = h % SLOTS
                for kk in range(4):
                    k = 4 * hf + kk
                    hi, lo = w_hi[:, s, kk * COLS:(kk + 1) * COLS], w_lo[:, s, kk * COLS:(kk + 1) * COLS]
                    for t in range(2):
                        o = bank[:, t * COLS:(t + 1) * COLS]
                        x_hi, x_lo = in_hi[:, k, t * P:(t + 1) * P], in_lo[:, k, t * P:(t + 1) * P]
                        mm(o, x_hi, hi, start=hf == 0 and t == 0 and kk == 0)
                        mm(o, x_hi, lo)
                        last = mm(o, x_lo, hi, stop=hf == 1 and kk == 3)
                last.then_inc(pe_used, 1)

            def first_pair(b, m, banks, stats=None):
                weights(b + 1, 0)
                for k in range(4):
                    pe.wait_ge(in_lo_done, m * C + k + 1)
                    for u in range(2):
                        for t in range(2):
                            at = k * COLS + t * P
                            hi, lo = w_hi[:, (b + u) % SLOTS, at:at + P], w_lo[:, (b + u) % SLOTS, at:at + P]
                            o = banks[u][:, t * T:(t + 1) * T]
                            mm(o, hi, in_hi[:, k, :], start=k == 0 and t == 0)
                            mm(o, hi, in_lo[:, k, :])
                            last = mm(o, lo, in_hi[:, k, :])
                last.then_inc(pe_used, 2)
                cols_half(b + 2, 0, 1, banks[0], m)
                cols_half(b + 3, 0, 1, banks[1], m, between=stats)

            def out_tile(t, h, c, st, start, stop):
                s = h % SLOTS
                if isinstance(c, int):
                    x_hi, x_lo = hid_hi[:, c, :], hid_lo[:, c, :]
                else:
                    x_hi = hid_hi[:, bass.ds(c, 1), :].rearrange("p c t -> p (c t)")
                    x_lo = hid_lo[:, bass.ds(c, 1), :].rearrange("p c t -> p (c t)")
                bank, at = y_tiles(st)[t]
                o = bank[:, at:at + T]
                hi, lo = w_hi[:, s, t * P:(t + 1) * P], w_lo[:, s, t * P:(t + 1) * P]
                mm(o, hi, x_hi, start=start and at == 0)
                mm(o, hi, x_lo)
                return mm(o, lo, x_hi, stop=stop)

            def rows_half(h, i, c, st, first=False):
                weights(h, i)
                for t in range(C):
                    last = out_tile(t, h, c, st, first, False)
                last.then_inc(pe_used, 1)

            def rows_end(h, c, st):
                weights(h + 1, 0)
                for t in range(C):
                    out_tile(t, h, c, st, False, False)
                    last = out_tile(t, h + 1, c + 1, st, False, True)
                    if t in (1, 3, 5, 6):
                        last.then_inc(y_done, 1)
                last.then_inc(pe_used, 2)

            def norm(name):
                n = NORMS.index(name)
                stat = stat_bank(name)[:, 0:T]
                for p in range(3):
                    pe.wait_ge(sq_added, 3 * n + p + 1)
                    mm(stat, ones[:], sq[:, 2 * p, :], start=p == 0)
                for c in (6, 7):
                    pe.wait_ge(sq_done, n * C + c + 1)
                    last = mm(stat, ones[:], sq[:, c, :], stop=c == 7)
                last.then_inc(sumsq, 1)
                mod_reduce(REDUCE_IN_NORM.get(name, []))

            def head_stats(u):
                pe.wait_ge(norm_sq_done, u + 1)
                mm(STAT[:], head_ones[:], norm_sq, start=True, stop=True).then_inc(norm_stat, 1)

            def unit_free(u):
                pe.wait_ge(proj_free, u + 1)

            def attention(st):
                ai = ATTN.index(st)
                b = BASE[st]
                norm(st)
                m = SPLIT_NORMS.index(st)
                q, k, v = QKV[st]
                units = UNITS_BEFORE[st]
                done = NORMED_BEFORE.get(st)
                pairs = (q + k) // 2
                unit_free(units + 1)
                first_pair(b, m, FIRST, None if done is None else lambda: head_stats(done))
                if st == "moba":
                    pe.wait_ge(bias_in, 32)
                    mm(MODB[0:HEADS, 0:BIAS_ROW], rel_aug[:], bucket_sb[:], start=True, stop=True).then_inc(bias_ps, 1)
                if st == "fox":
                    forget_logits()
                with pe.Fori(1, pairs) as i:
                    cols_half(b, i, 0, B[0])
                    if done is not None:
                        head_stats(i * 2 + (done - 1))
                    cols_half(b + 1, i, 1, B[0])
                    unit_free(i * 2 + (units + 1))
                    cols_half(b + 2, i, 0, B[1])
                    if done is not None:
                        head_stats(i * 2 + done)
                    cols_half(b + 3, i, 1, B[1])
                    unit_free(i * 2 + (units + 2))
                b2, u2 = b + 4 * pairs, units + 2 * pairs
                if st == "swa":
                    cols_half(b2, 0, 0, V_BANK[0])
                    head_stats(done + 2 * pairs - 1)
                    cols_half(b2 + 1, 0, 1, V_BANK[0])
                    unit_free(u2 + 1)
                    v_half(b2 + 2, 0, 0, V_BANK[1])
                    head_stats(done + 2 * pairs)
                else:
                    if done is not None:
                        head_stats(done + 2 * pairs - 1)
                    if st == "fox":
                        forget_sums()
                    last = v // 2 - 1
                    with pe.Fori(0, last) as i:
                        for u in range(2):
                            unit_free(i * 2 + (u2 + u))
                            for hf in range(2):
                                v_half(b2 + 2 * u + hf, i, hf, V_BANK[u])
                    unit_free(last * 2 + u2)
                    for hf in range(2):
                        v_half(b2 + 4 * last + hf, 0, hf, V_BANK[0])
                    b2 += 4 * last
                pe.wait_ge(proj_free, u2 + 2)
                core(st, ai, 0, EARLY[st])
                if st == "swa":
                    v_half(b2 + 3, 0, 1, V_BANK[1])
                else:
                    unit_free(last * 2 + u2 + 1)
                    for hf in range(2):
                        v_half(b2 + 2 + hf, 0, hf, V_BANK[1])
                pe.wait_ge(proj_free, units + q + k + 2)
                if st in MOD_SET:
                    pe.wait_ge(mod_done, REDUCE_IN_NORM[st][-1] + 1)
                else:
                    pe.wait_ge(bias_sb, 1)
                core(st, ai, EARLY[st], HEADS + 4, units + q + k + v + 2)
                b3 = b + 2 * (q + k + v)
                for c in range(C - 2):
                    if c == C - 4:
                        mod_reduce(REDUCE_BEFORE_END.get(st, []))
                    pe.wait_ge(o_lo_done, ai * C + c + 1)
                    rows_half(b3 + c, 0, c, st, first=c == 0)
                pe.wait_ge(o_lo_done, ai * C + C)
                rows_end(b3 + C - 2, C - 2, st)

            def core(st, ai, begin, end, v_ready=None):
                def q_of(h):
                    at = (h % 2) * DH
                    q = q_swa if st == "swa" else qT
                    return q.rearrange("p (c t) -> p c t", t=T)[at:at + DH, h // 2, :]

                def k_of(h):
                    at = (h % 2) * DH
                    if st != "swa":
                        return kT.rearrange("p (c t) -> p c t", t=T)[at:at + DH, h // 2, :]
                    kv = h // 4
                    kk = k_swa if kv % 2 == h % 2 else k_swap
                    return kk.rearrange("p (c t) -> p c t", t=T)[at:at + DH, kv // 2, :]

                def v_of(h, t):
                    kv = h // 4 if st == "swa" else h
                    return v_tok[:, t, kv * DH:(kv + 1) * DH]

                for t in range(begin, end):
                    if t < HEADS:
                        h, g = t, ai * HEADS + t
                        if h >= 3:
                            pe.wait_ge(max_done, 2 * (g - 2))
                        if st == "swa" and h == 1:
                            pe.wait_ge(k_swapped, 2)
                        S = SCORE[h % 3]
                        for blk, (lo, hi) in enumerate(((0, P), (P, KEYS))):
                            n = hi - lo
                            ins = mm(S[:, lo:hi], q_of(h)[:, blk * P:(blk + 1) * P], k_of(h)[:, 0:n], start=True, stop=True)
                        ins.then_inc(score_done, 1)
                    if 0 <= t - 3 < HEADS:
                        h, g = t - 3, ai * HEADS + t - 3
                        pe.wait_ge(prob_done, 2 * (g + 1))
                        if h >= 2:
                            pe.wait_ge(pt_done, g - 1)
                        for j in range(3):
                            ins = pe.transpose(PT_BANK[h % 2][:, j * P:(j + 1) * P],
                                               probs[:, h % PROBS, (0, P, 2 * P)[j]:(0, P, 2 * P)[j] + P], ident[:])
                        ins.then_inc(pt_ps, 1)
                    if 0 <= t - 4 < HEADS:
                        h, g = t - 4, ai * HEADS + t - 4
                        pair = h // 2
                        if h == 0:
                            pe.wait_ge(proj_free, v_ready)
                        pe.wait_ge(pt_done, g + 1)
                        if h % 2 == 0 and pair >= 2:
                            pe.wait_ge(o_lo_done, ai * C + pair - 1)
                        o = O_BANK[pair % 2][(h % 2) * DH:(h % 2 + 1) * DH, :]
                        mm(o[:, 0:T], v_of(h, 0), probsT[:, h % 2, 0:T], start=True)
                        mm(o[:, P:T], v_of(h, 1), probsT[:, h % 2, T:KEYS], stop=True).then_inc(pv_done, 1)

            def forget_logits():
                pe.wait_ge(tail_lo_done, 1)
                for t in range(2):
                    o = FORGET[:, t * HEADS:(t + 1) * HEADS]
                    for k in range(C):
                        x_hi, x_lo = in_hi[:, k, t * P:(t + 1) * P], in_lo[:, k, t * P:(t + 1) * P]
                        mm(o, x_hi, tail_hi[:, k, :], start=t == 0 and k == 0)
                        mm(o, x_hi, tail_lo[:, k, :])
                        last = mm(o, x_lo, tail_hi[:, k, :], stop=k == C - 1)
                last.then_inc(fl_ps, 1)

            def forget_sums():
                pe.wait_ge(logf_done, 1)
                mm(FORGET[0:HEADS, T:2 * T], log_f[:, 0, :], neg_tri[:], start=True)
                mm(FORGET[0:HEADS, T + P:2 * T], log_f[:, 1, :], neg_tri[:, 0:P], stop=True).then_inc(F_ps, 1)

            def ffn(st):
                f = int(st[-1])
                b = BASE[st]
                norm(st)
                m = SPLIT_NORMS.index(st)

                def gate_read(g):
                    pe.wait_ge(gate_taps, g * 2 + 2) if f == 0 else pe.wait_ge(silu_done, g + 1)

                pe.wait_ge(hid_done, f * UP_STEPS + 1)
                first_pair(b, m, [GATE, UP])
                gate_read(f * UP_STEPS)
                with pe.Fori(1, UP_STEPS) as i:
                    g = i + f * UP_STEPS
                    for hf in range(2):
                        cols_half(b + hf, i, hf, GATE)
                    pe.wait_ge(hid_done, g + 1)
                    for hf in range(2):
                        cols_half(b + 2 + hf, i, hf, UP)
                    gate_read(g)
                b2 = b + 4 * UP_STEPS
                hid = f * UP_STEPS
                for c in range(2):
                    pe.wait_ge(hid_lo_done, hid + 1)
                    rows_half(b2 + c, 0, c, st, first=c == 0)
                pe.wait_ge(hid_lo_done, hid + UP_STEPS - 2)
                with pe.Fori(0, HID // 4 - 1) as i:
                    for j in range(4):
                        rows_half(b2 + 2 + j, i, i * 4 + (2 + j), st)
                mod_reduce(REDUCE_BEFORE_END.get(st, []))
                pe.wait_ge(hid_lo_done, hid + UP_STEPS)
                for c in range(HID - 4, HID - 2):
                    rows_half(b2 + c, 0, c, st)
                rows_end(b2 + HID - 2, HID - 2, st)

            def mod_reduce(groups):
                for at, q in enumerate(groups):
                    pe.wait_ge(mod_lo_done, q + 1)
                    if at == 0 and q > 0:
                        pe.wait_ge(mod_done, q)
                    for c in range(C):
                        o = MODB[:, 2 * (C * at + c):2 * (C * at + c) + 2]
                        mm(o, mod_hi[:, q % 2, c * P:(c + 1) * P], ones_r[:], start=at == 0 and c == 0)
                        last = mm(o, mod_lo[:, q % SUMS, c * P:(c + 1) * P], ones_r[:], stop=True)
                if groups:
                    last.then_inc(mod_ps, len(groups))

            pe.wait_ge(consts, 1)
            pe.wait_ge(x_in, 16)
            for c in range(C):
                for t in range(2):
                    ins = pe.transpose(X_BANK[c // 2][:, (c % 2) * T + t * P:(c % 2) * T + (t + 1) * P], hn_tok[:, t, c * P:(c + 1) * P], ident[:])
                if c % 2 == 1:
                    ins.then_inc(xt_ready, 1)
            pe.wait_ge(ones_done, 1)
            for st in ORDER:
                (attention if st in QKV else ffn)(st)
                if st == "ffn0":
                    norm("final")
            for t in range(2):
                for c in range(C):
                    pe.wait_ge(x_ready, len(NORMS) * C + c + 1)
                    ins = pe.transpose(OUT_BANK[t][c // 4][:, (c % 4) * P:(c % 4 + 1) * P], xT[:, c, t * P:(t + 1) * P], ident[:])
                    if c % 4 == 3:
                        ins.then_inc(out_ps, 1)


WEIGHTS = ["x", "ffn_w_up", "ffn_w_down", "moba_w_qkv", "moba_w_o", "ada_w_2", "ffn_w13_2", "ffn_w2_2",
           "rel_bias_2", "swa_w_in_2", "swa_w_out_2", "fox_w_in_2", "fox_w_out_2"]


def bucket_rows():
    rows = np.zeros((BUCKETS + 1, BIAS_ROW), np.float32)
    exact = BUCKETS // 2
    for t in range(BIAS_ROW):
        n = 2 * P - 1 - t
        if not 0 <= n < MAX_DIST:
            rows[BUCKETS, t] = 1.0
            continue
        big = exact + int(np.log(np.float32(max(n, 1) / exact)) / np.log(MAX_DIST / exact) * (BUCKETS - exact)) if n >= exact else 0
        rows[min(n if n < exact else big, BUCKETS - 1), t] = 1.0
    return rows


def pack_vectors(inputs):
    def chunks(v):
        v = np.asarray(v)
        return np.moveaxis(v.reshape(-1, P), 1, 0)

    def rows(v):
        return np.broadcast_to(np.asarray(v).reshape(1, -1), (P, HEADS))

    taps = np.concatenate([np.asarray(inputs["ffn_conv_w"])[0], np.asarray(inputs["ffn_conv_b"])], axis=0)
    conv = taps.reshape(4, 2, UP_STEPS, 2, P).transpose(4, 2, 1, 3, 0).reshape(P, UP_STEPS * 16)

    def head(v):
        return np.tile(np.asarray(v).reshape(DH), 2)[:, None]

    parts = [chunks(inputs["norm_mix"]), chunks(inputs["norm_ffn"]), chunks(inputs["norm_final"]),
             chunks(inputs["norm_g_2"]), chunks(inputs["ada_b_2"]), chunks(inputs["c_2"]), conv,
             head(inputs["swa_q_g_2"]), head(inputs["swa_k_g_2"]), head(inputs["fox_q_g_2"]), head(inputs["fox_k_g_2"]),
             rows(inputs["swa_sink_2"]), rows(inputs["fox_b_f_2"])]
    return np.ascontiguousarray(np.concatenate(parts, axis=1))


def kernel(**inputs):
    import concourse.bacc as _bacc
    from concourse.bass_utils import run_bass_kernel_spmd as _run

    nc = _bacc.Bacc("TRN2", target_bir_lowering=False, num_devices=1)
    data = {name: np.ascontiguousarray(inputs[name]) for name in WEIGHTS}
    data["vectors"] = pack_vectors(inputs)
    data["bucket_rows"] = bucket_rows()
    arrays, aps = {}, {}
    for name, v in data.items():
        arrays[f"in_{name}_dram"] = v
        aps[name] = nc.dram_tensor(f"in_{name}_dram", v.shape, mybir.dt.from_np(v.dtype), kind="ExternalInput").ap()
    out = nc.dram_tensor("out_0_dram", (1, T, D), F32, kind="ExternalOutput").ap()
    build(nc, aps, out)
    r = _run(nc, [arrays], core_ids=[0])
    return r.results[0]["out_0_dram"]
```

```python
from contextlib import ExitStack

import numpy as np
import concourse.bass as bass
from concourse import mybir

ALU = mybir.AluOpType
ACT = mybir.ActivationFunctionType
F32 = mybir.dt.float32
F32R = mybir.dt.float32r

P = 128
D = 1024
T = 256
C = D // P
FF = 2816
HEADS = 16
DH = 64
COLS = 256
HALF = 4 * COLS
SLOTS = 4
PROBS = 4
UP_STEPS = FF // COLS
HID = FF // P
KEYS = 3 * P
EPS = 1e-6
MASKED = -1e30
BUCKETS, MAX_DIST = 32, 128
BIAS_ROW = 3 * P
CONSTS = 7

V_MIX, V_FFN, V_FINAL = 0, C, 2 * C
V_NORM_G = 3 * C
V_ADA_B = V_NORM_G + 6 * C
V_C = V_ADA_B + 6 * 3 * C
V_CONV = V_C + C
V_QK_G = V_CONV + UP_STEPS * 16
V_SINK = V_QK_G + 4
V_BF = V_SINK + HEADS
V_COLS = V_BF + HEADS

QKV = {"moba": (4, 4, 4), "swa": (4, 1, 1), "fox": (4, 4, 4)}
ATTN = ["moba", "swa", "fox"]
ORDER = ["moba", "ffn0", "ffn1", "swa", "ffn2", "ffn3", "fox", "ffn4"]
O_UNITS = D // COLS
BASE = {}
_h = 0
for _s in ORDER:
    BASE[_s] = _h
    _h += 2 * (sum(QKV[_s]) + O_UNITS) if _s in QKV else 2 * (2 * UP_STEPS + HID // 2)
HALVES = _h
NORMS = ["moba", "ffn0", "final", "ffn1", "swa", "ffn2", "ffn3", "fox", "ffn4"]
SPLIT_NORMS = [n for n in NORMS if n != "final"]
MOD_SET = {"ffn1": 0, "swa": 1, "ffn2": 2, "ffn3": 3, "fox": 4, "ffn4": 5}
MOD_UNITS = 3 * D // COLS
KIND = {"shift": 0, "scale": 1, "gate": 2}
KIND_ORDER = ["scale", "shift", "gate"]
GROUPS = 3 * len(MOD_SET)
SUMS = 4
SPLIT_EARLY = {"moba": [0], "ffn1": [4, 5], "swa": [7], "ffn2": [9, 10], "ffn3": [13, 14], "fox": [16, 17]}
SPLIT_LATE = {"moba": [1], "ffn0": [2, 3], "ffn1": [6], "swa": [8], "ffn2": [11, 12], "ffn3": [15]}
FIRST_GROUP = {"moba": 0, "ffn0": 2, "ffn1": 4, "swa": 8, "ffn2": 9, "ffn3": 13, "fox": 17}
REDUCE_IN_NORM = {"ffn0": [1], "final": [2], "ffn1": [3], "swa": [6], "ffn2": [8], "ffn3": [11, 12], "fox": [15], "ffn4": [17]}
REDUCE_IN_OUT = {"moba": [0], "ffn1": [4, 5], "swa": [7], "ffn2": [9, 10], "ffn3": [13, 14], "fox": [16]}
UNITS_BEFORE = {"moba": 0, "swa": 12, "fox": 18}
EXPS = {"moba": 2, "swa": 3, "fox": 2}
EXPS_BEFORE = {"moba": 0, "swa": 2 * HEADS, "fox": 5 * HEADS}
NORMED_BEFORE = {"swa": 0, "fox": 5}
WARM_UP = 16
FORGET_HEADS = 8
EARLY = {"moba": 3, "swa": 2, "fox": 3}


def build(nc, a, out):
    ctx = ExitStack()
    with ctx:
        def sb(name, shape, dt=F32):
            return ctx.enter_context(nc.sbuf_tensor(name, shape, dt))

        def sem(name):
            return ctx.enter_context(nc.semaphore(name))

        raw_w = sb("raw_w", [P, SLOTS, HALF])
        w_hi = sb("w_hi", [P, SLOTS, HALF], F32R)
        w_lo = sb("w_lo", [P, SLOTS, HALF], F32R)
        xT = sb("xT", [P, C, T])
        in_hi = sb("in_hi", [P, C, T], F32R)
        in_lo = sb("in_lo", [P, C, T], F32R)
        rstd = sb("rstd", [P, T])
        with ExitStack() as meanwhile:
            def under(name, shape):
                return meanwhile.enter_context(nc.sbuf_tensor(name, shape, F32))

            hn = under("hn", [P, C, T])
            spare = under("spare", [P, (HID - C) * T])
            under("kept", [P, C, T])
            forget_mask = under("forget_mask", [P, HEADS, P])
        hid_hi = sb("hid_hi", [P, HID, T], F32R)
        hid_lo = sb("hid_lo", [P, HID, T], F32R)
        probs = spare[:, 0:PROBS * KEYS].rearrange("p (n k) -> p n k", n=PROBS)
        probsT = spare[:, 1536:1536 + 2 * KEYS].rearrange("p (n k) -> p n k", n=2)
        norm_sq = spare[:, 2304:2304 + 2 * T]
        norm_rstd = spare[:, 2816:2816 + 2 * T]
        shared = sb("shared", [P, 3 * C * T])
        qT = shared[:, 0:C * T]
        kT = shared[:, C * T:2 * C * T]
        k_swa, q_swa, k_swap = shared[:, 0:2 * T], shared[:, 2 * T:10 * T], shared[:, 10 * T:12 * T]
        v_tok = shared[:, 2 * C * T:3 * C * T].rearrange("p (t d) -> p t d", t=2)
        sq = shared[:, 0:C * T].rearrange("p (c t) -> p c t", c=C)
        silu_gate = shared[:, 3072:3584]
        hidden = shared[:, 3584:4096]
        conv_gate = shared[:, 4096:4608]
        conv_up = shared[:, 4608:5120]
        ada_raw = sb("ada_raw", [P, 2, D])
        with nc.sbuf_tensor("mod_sum", [P, SUMS, D], F32) as mod_sum:
            pass
        mod_lo = sb("mod_lo", [P, SUMS, D], F32R)
        mod_hi = sb("mod_hi", [P, 2, D], F32R)
        ones_r = sb("ones_r", [P, P], F32R)
        diagonal = sb("diagonal", [P, P])
        picked = sb("picked", [P, D])
        c_act = sb("c_act", [P, C])
        mods = sb("mods", [P, 6, 3 * C])
        mod_gain = sb("mod_gain", [P, 6, C])
        row_max = sb("row_max", [P, HEADS, 2])
        neg_max = sb("neg_max", [P, HEADS, 2])
        row_sum = sb("row_sum", [P, HEADS, 2])
        sink_exp = sb("sink_exp", [P, HEADS, 2])
        row_den = sb("row_den", [P, HEADS, 2])
        row_inv = sb("row_inv", [P, HEADS, 2])
        qk_gain = sb("qk_gain", [P, 16])
        bias = sb("bias", [P, HEADS, 2 * P])
        rel_aug = sb("rel_aug", [BUCKETS + 1, HEADS])
        bucket_sb = sb("bucket_sb", [BUCKETS + 1, BIAS_ROW])
        bias_rows = sb("bias_rows", [HEADS, BIAS_ROW])
        tail_raw = sb("tail_raw", [P, C, HEADS])
        tail_hi = sb("tail_hi", [P, C, HEADS], F32R)
        tail_lo = sb("tail_lo", [P, C, HEADS], F32R)
        fl = sb("fl", [P, 2, HEADS])
        fl_abs = sb("fl_abs", [P, 2, HEADS])
        fl_exp = sb("fl_exp", [P, 2, HEADS])
        fl_ln = sb("fl_ln", [P, 2, HEADS])
        fl_min = sb("fl_min", [P, 2, HEADS])
        log_f = sb("log_f", [P, 2, HEADS])
        head_rows = sb("head_rows", [HEADS, T])
        vec = sb("vec", [P, V_COLS])
        ident = sb("ident", [P, P])
        ones = sb("ones", [P, P])
        head_ones = sb("head_ones", [P, P])
        neg_tri = sb("neg_tri", [P, T])
        mask = sb("mask", [P, KEYS])
        eps_col = sb("eps_col", [P, 1])

        B = [ctx.enter_context(nc.psum_tensor(f"bank{i}", [P, 512], F32)) for i in range(8)]
        GATE, UP, STAT, MODB = B[0], B[1], B[2], B[3]
        FIRST = [B[5], B[1]]
        V_BANK = [B[5], B[6]]
        X_BANK = B[4:8]
        Y_FFN = [(B[4], 0), (B[4], T), (B[5], 0), (B[5], T), (B[6], 0), (B[6], T), (B[7], 0), (B[0], 0)]
        Y_ATTN = [(B[0], 0), (B[0], T), (B[1], 0), (B[1], T), (B[2], 0), (B[2], T), (B[7], 0), (B[4], 0)]
        SCORE = B[0:3]
        PT_BANK = [B[3], B[4]]
        O_BANK = [B[5], B[6]]
        FORGET = B[7]
        MOD_BEHIND_FFN, MOD_BEHIND_ATTN = [(B[4], B[6]), (B[5], B[7])], [(B[3], B[4])]
        MOD_IN_FFN, MOD_IN_ATTN = (B[3], B[1]), (B[3], B[5])
        OUT_BANK = [(B[1], B[2]), (B[3], B[0])]

        forget_dram = nc.dram_tensor("forget_scratch", (HEADS, T), F32, kind="Internal")
        bias_dram = nc.dram_tensor("bias_scratch", (HEADS, P, BIAS_ROW), F32, kind="Internal")

        raw_in = [sem(f"raw_in{i}") for i in range(SLOTS)]
        hi_ready = sem("hi_ready")
        lo_ready = sem("lo_ready")
        pe_used = sem("pe_used")
        x_in = [sem(f"x_in{half}") for half in range(2)]
        vec_in = sem("vec_in")
        bias_in = sem("bias_in")
        bias_out = sem("bias_out")
        bias_back = sem("bias_back")
        tail_in = sem("tail_in")
        ada_in = [sem(f"ada_in{i}") for i in range(2)]
        out_done = sem("out_done")
        consts = sem("consts")
        memsets = sem("memsets")
        xt_ready = sem("xt_ready")
        x_ready = sem("x_ready")
        sq_done = sem("sq_done")
        sq_added = sem("sq_added")
        sumsq = sem("sumsq")
        ln_done = sem("ln_done")
        rstd_done = sem("rstd_done")
        hn_done = sem("hn_done")
        in_hi_done = sem("in_hi_done")
        in_lo_done = sem("in_lo_done")
        silu_done = sem("silu_done")
        affine_done = sem("affine_done")
        tap_done = sem("tap_done")
        gate_taps = sem("gate_taps")
        hid_done = sem("hid_done")
        hid_hi_done = sem("hid_hi_done")
        hid_lo_done = sem("hid_lo_done")
        y_done = sem("y_done")
        c_done = sem("c_done")
        mod_zero = sem("mod_zero")
        mod_step = sem("mod_step")
        mod_hi_done = sem("mod_hi_done")
        mod_lo_done = sem("mod_lo_done")
        mod_ps = sem("mod_ps")
        mod_picked = sem("mod_picked")
        mod_add = sem("mod_add")
        mod_done = sem("mod_done")
        ones_done = sem("ones_done")
        proj_free = sem("proj_free")
        norm_sq_done = sem("norm_sq_done")
        norm_stat = sem("norm_stat")
        norm_ln = sem("norm_ln")
        norm_rstd_done = sem("norm_rstd_done")
        k_swapped = sem("k_swapped")
        score_done = sem("score_done")
        max_done = sem("max_done")
        neg_max_done = sem("neg_max_done")
        exp_done = sem("exp_done")
        den_done = sem("den_done")
        inv_done = sem("inv_done")
        prob_done = sem("prob_done")
        pt_ps = sem("pt_ps")
        pt_done = sem("pt_done")
        pv_done = sem("pv_done")
        o_hi_done = sem("o_hi_done")
        o_lo_done = sem("o_lo_done")
        tail_hi_done = sem("tail_hi_done")
        tail_lo_done = sem("tail_lo_done")
        logits_ps = sem("logits_ps")
        logits_sb = sem("logits_sb")
        fl_ps = sem("fl_ps")
        fl_done = sem("fl_done")
        fl_act = sem("fl_act")
        logf_done = sem("logf_done")
        F_ps = sem("F_ps")
        F_done = sem("F_done")
        F_out = sem("F_out")
        F_back = sem("F_back")
        forget_masked = sem("forget_masked")
        bias_ps = sem("bias_ps")
        bias_sb = sem("bias_sb")
        out_ps = sem("out_ps")
        out_low = sem("out_low")
        out_high = sem("out_high")
        up_taps = sem("up_taps")
        fl_part = sem("fl_part")
        gains_done = sem("gains_done")

        block = ctx.enter_context(nc.Block())

        def y_tiles(st):
            return Y_ATTN if st in QKV else Y_FFN

        def stat_bank(name):
            before = NORMS.index(name) - 1
            return B[6] if before >= 0 and NORMS[before] in QKV else STAT

        def mod_banks(name):
            return MOD_BEHIND_ATTN if NORMS[NORMS.index(name) - 1] in QKV else MOD_BEHIND_FFN

        def cols_view(w):
            return w.rearrange("(k p) n -> p k n", p=P)

        QKV_W = {"moba": cols_view(a["moba_w_qkv"][0]), "swa": cols_view(a["swa_w_in_2"][0]),
                 "fox": cols_view(a["fox_w_in_2"][0])}
        O_W = {"moba": cols_view(a["moba_w_o"][0]), "swa": cols_view(a["swa_w_out_2"][0]),
               "fox": cols_view(a["fox_w_out_2"][0])}
        UP_W = {"ffn0": cols_view(a["ffn_w_up"][0])}
        DOWN_W = {"ffn0": cols_view(a["ffn_w_down"][0])}
        for i in range(4):
            UP_W[f"ffn{i + 1}"] = cols_view(a["ffn_w13_2"][i // 2, i % 2])
            DOWN_W[f"ffn{i + 1}"] = cols_view(a["ffn_w2_2"][i // 2, i % 2])
        ADA_W = [cols_view(a["ada_w_2"][i]) for i in range(2)]

        hn_tok = hn[:].rearrange("p c t -> p (c t)").rearrange("p (t d) -> p t d", t=2)

        @block.sync
        def _(sp):
            x_rows = a["x"][0].rearrange("(t p) d -> p t d", p=P)
            for half in range(2):
                cols = slice(half * (D // 2), (half + 1) * (D // 2))
                sp.dma_start(hn_tok[:, :, cols], x_rows[:, :, cols]).then_inc(x_in[half], 16)
            sp.dma_start(vec[:], a["vectors"]).then_inc(vec_in, 16)

            def load(h, i, src):
                s = h % SLOTS
                if isinstance(i, int):
                    if h + 4 * i >= SLOTS:
                        sp.wait_ge(lo_ready, h + 4 * i - SLOTS + 1)
                else:
                    sp.wait_ge(lo_ready, i * 4 + (h - SLOTS + 1))
                sp.dma_start(raw_w[:, s, :].rearrange("p (k n) -> p k n", k=src.shape[1]), src).then_inc(raw_in[s], 16)

            def load_cols(h, i, w, col):
                for hf in range(2):
                    load(h + hf, i, w[:, 4 * hf:4 * hf + 4, bass.ds(col, COLS)])

            def load_first(b, w, cols):
                for hf in range(2):
                    for u in range(2):
                        load(b + 2 * hf + u, 0, w[:, 4 * hf:4 * hf + 4, bass.ds(cols[u], COLS)])

            def attention(st):
                b, w, units = BASE[st], QKV_W[st], sum(QKV[st])
                if st == "swa":
                    load_first(b, w, (D, 0))
                    for u, col in enumerate((COLS, 2 * COLS, 3 * COLS, D + COLS)):
                        load_cols(b + 4 + 2 * u, 0, w, col)
                else:
                    load_first(b, w, (0, COLS))
                    with sp.Fori(1, units // 2) as i:
                        for u in range(2):
                            load_cols(b + 2 * u, i, w, i * (2 * COLS) + u * COLS)
                b += 2 * units
                for c in range(C):
                    load(b + c, 0, O_W[st][:, c:c + 1, :])

            def ffn(st):
                b, w = BASE[st], UP_W[st]
                load_first(b, w, (0, FF))
                with sp.Fori(1, UP_STEPS) as i:
                    load_cols(b, i, w, i * COLS)
                    load_cols(b + 2, i, w, i * COLS + FF)
                b += 4 * UP_STEPS
                w = DOWN_W[st]
                for c in range(2):
                    load(b + c, 0, w[:, c:c + 1, :])
                with sp.Fori(0, HID // 4) as i:
                    for c in range(4):
                        load(b + 2 + c, i, w[:, bass.ds(i * 4 + 2 + c, 1), :])

            for st in ORDER:
                (attention if st in QKV else ffn)(st)

            for t in range(2):
                sp.wait_ge(out_low, t + 1)
                sp.wait_ge(out_high, t + 1)
                sp.dma_start(out[0, t * P:(t + 1) * P, :], hn_tok[:, t, :]).then_inc(out_done, 16)
            sp.wait_ge(out_done, 32)

        @block.gpsimd
        def _(pool):
            def const(ins):
                ins.then_inc(consts, 1)

            pool.memset(ident[:], 0.0).then_inc(memsets, 1)
            pool.wait_ge(memsets, 1)
            const(pool.affine_select(out=ident[:], in_=ident[:], compare_op=ALU.not_equal, fill=1.0, base=0,
                                     pattern=[[-1, P]], channel_multiplier=1))
            pool.memset(ones[:], 1.0).then_inc(memsets, 1)
            pool.memset(eps_col[:], EPS).then_inc(memsets, 1)
            pool.memset(neg_tri[:], -1.0).then_inc(memsets, 1)
            pool.memset(mask[:], 0.0).then_inc(memsets, 1)
            pool.memset(head_ones[:], 1.0).then_inc(memsets, 1)
            pool.memset(diagonal[:], 0.0).then_inc(memsets, 1)
            pool.memset(rel_aug[:], MASKED).then_inc(memsets, 1)
            pool.wait_ge(memsets, 8)
            const(pool.affine_select(out=diagonal[:], in_=diagonal[:], compare_op=ALU.is_equal, fill=MASKED, base=0,
                                     pattern=[[-1, P]], channel_multiplier=1))
            const(pool.affine_select(out=neg_tri[:], in_=neg_tri[:], compare_op=ALU.is_ge, fill=0.0, base=0,
                                     pattern=[[1, T]], channel_multiplier=-1))
            for at in (0, 2 * P):
                const(pool.affine_select(out=mask[:, at:at + P], in_=mask[:, at:at + P], compare_op=ALU.is_ge,
                                         fill=MASKED, base=0, pattern=[[-1, P]], channel_multiplier=1))
            const(pool.affine_select(out=head_ones[:, 0:DH], in_=head_ones[:, 0:DH], compare_op=ALU.is_ge, fill=0.0,
                                     base=DH - 1, pattern=[[0, DH]], channel_multiplier=-1))
            const(pool.affine_select(out=head_ones[:, DH:P], in_=head_ones[:, DH:P], compare_op=ALU.is_ge, fill=0.0,
                                     base=-DH, pattern=[[0, DH]], channel_multiplier=1))
            pool.dma_start(rel_aug[0:BUCKETS, :], a["rel_bias_2"]).then_inc(bias_in, 16)
            pool.dma_start(bucket_sb[:], a["bucket_rows"]).then_inc(bias_in, 16)
            pool.dma_start(tail_raw[:], QKV_W["fox"][:, :, 3 * D:3 * D + HEADS]).then_inc(tail_in, 16)
            def bias_tiles():
                pool.wait_ge(bias_sb, 1)
                pool.dma_start(bias_dram.ap(), bias_rows[:].unsqueeze(1).to_broadcast([HEADS, P, BIAS_ROW])).then_inc(bias_out, 16)
                pool.wait_ge(bias_out, 16)
                moved = bass.AP(tensor=bias_dram.ap().tensor, offset=P - 1,
                                ap=[[BIAS_ROW - 1, P], [P * BIAS_ROW, HEADS], [1, 2 * P]])
                pool.dma_start(bias[:], moved).then_inc(bias_back, 16)

            def group(q):
                s, kind = q // 3, KIND[KIND_ORDER[q % 3]]
                w, col = ADA_W[s // 3], ((s % 3) * 3 + kind) * D
                if q >= SUMS:
                    pool.wait_ge(mod_ps, q - SUMS + 1)
                pool.memset(mod_sum[:, q % SUMS, :], 0.0).then_inc(mod_zero, 1)

                def load_ada(i, j):
                    if not (q == 0 and isinstance(i, int)):
                        pool.wait_ge(mod_step, i * 2 + (C * q + j - 1))
                    k = j if isinstance(i, int) and i == 0 else i * 2 + j
                    pool.dma_start(ada_raw[:, j, :].unsqueeze(1), w[:, bass.ds(k, 1), col:col + D]).then_inc(ada_in[j], 16)

                if q == 0:
                    for j in range(2):
                        load_ada(0, j)
                with pool.Fori(1 if q == 0 else 0, C // 2) as i:
                    for j in range(2):
                        load_ada(i, j)

            for q in range(GROUPS):
                group(q)
                if q == 1:
                    bias_tiles()
            pool.wait_ge(F_done, 1)
            pool.dma_start(forget_dram.ap(), head_rows[:]).then_inc(F_out, 16)
            pool.wait_ge(F_out, 16)
            pool.dma_start(bias[:], bass.AP(tensor=forget_dram.ap().tensor, offset=0,
                                            ap=[[0, P], [T, HEADS], [1, T]])).then_inc(F_back, 16)
            pool.wait_ge(F_back, 16)
            for at in range(0, HEADS, FORGET_HEADS):
                heads = slice(at, at + FORGET_HEADS)
                causal = mask[:, 0:P].unsqueeze(1).to_broadcast([P, FORGET_HEADS, P])
                pool.tensor_tensor(forget_mask[:, heads, :], bias[:, heads, 0:P], causal, ALU.add).then_inc(forget_masked, 1)
                pool.tensor_tensor(bias[:, heads, P:2 * P], bias[:, heads, P:2 * P], causal, ALU.add).then_inc(forget_masked, 1)

        @block.scalar
        def _(act):
            def at(i, h):
                return h if isinstance(i, int) else i * 4 + h

            def split(h, i=0):
                s = h % SLOTS
                if isinstance(i, int):
                    h += 4 * i
                    act.wait_ge(raw_in[s], 16 * (h // SLOTS + 1))
                    if h >= SLOTS:
                        act.wait_ge(pe_used, h - SLOTS + 1)
                else:
                    act.wait_ge(raw_in[s], i * 16 + 16 * (h // SLOTS + 1))
                    act.wait_ge(pe_used, i * 4 + (h - SLOTS + 1))
                act.activation(w_hi[:, s, :], raw_w[:, s, :], ACT.Copy).then_inc(hi_ready, 1)

            def mod_split(groups):
                for q in groups:
                    act.wait_ge(mod_step, C * (q + 1))
                    if q >= 2:
                        act.wait_ge(mod_ps, q - 1)
                    act.activation(mod_hi[:, q % 2, :], mod_sum[:, q % SUMS, :], ACT.Copy).then_inc(mod_hi_done, 1)

            def norm(name):
                n = NORMS.index(name)
                if n == 0 or NORMS[n - 1] in BASE and NORMS[n - 1] not in QKV:
                    act.preload_act_table_set("natural_log_exp_and_others")
                for c in range(C):
                    act.wait_ge(x_ready, n * C + c + 1)
                    act.activation(sq[:, c, :], xT[:, c, :], ACT.Square).then_inc(sq_done, 1)
                if n == 0:
                    for h in range(2):
                        split(h)
                act.wait_ge(sumsq, n + 1)
                act.activation(rstd[:], stat_bank(name)[:, 0:T], ACT.Ln, bias=eps_col[:, 0:1], scale=1.0 / D).then_inc(ln_done, 1)
                act.wait_ge(ln_done, n + 1)
                act.activation(rstd[:], rstd[:], ACT.Exp, scale=-0.5).then_inc(rstd_done, 1)
                if name == "final":
                    return
                m = SPLIT_NORMS.index(name)
                for c in range(C):
                    act.wait_ge(hn_done, m * C + c + 1)
                    if name in MOD_SET:
                        act.activation(in_hi[:, c, :], hn[:, c, :], ACT.Identity,
                                       bias=mods[:, MOD_SET[name], c:c + 1]).then_inc(in_hi_done, 1)
                    else:
                        act.activation(in_hi[:, c, :], hn[:, c, :], ACT.Copy).then_inc(in_hi_done, 1)
                    if c in (2, 4):
                        split(BASE[name] + 1 + c // 2)

            def down_splits(b, n, st):
                n = n - 4 if st == ORDER[-1] else n - 2
                for j in range(n % 4):
                    split(b + 4 + j)
                if n // 4 > 1:
                    with act.Fori(0, n // 4 - 1) as i:
                        for j in range(4):
                            split(b + 4 + n % 4 + j, i)
                if st in QKV:
                    for j in range(4):
                        split(b + n + j)
                    mod_split(SPLIT_LATE.get(st, []))
                else:
                    mod_split(SPLIT_LATE.get(st, []))
                    for j in range(4):
                        split(b + n + j)

            def squares(bank, used):
                act.wait_ge(pe_used, used)
                act.activation(norm_sq, bank[:], ACT.Square).then_inc(norm_sq_done, 1)

            def qk_rstd(u, unit):
                act.wait_ge(norm_stat, u + 1)
                act.wait_ge(proj_free, unit + 2)
                act.activation(norm_rstd, STAT[:], ACT.Ln, bias=eps_col[:, 0:1], scale=1.0 / DH).then_inc(norm_ln, 1)
                act.wait_ge(norm_ln, u + 1)
                act.activation(norm_rstd, norm_rstd, ACT.Exp, scale=-0.5).then_inc(norm_rstd_done, 1)

            def attention(st):
                ai = ATTN.index(st)
                b = BASE[st]
                norm(st)
                q, k, v = QKV[st]
                units, done = UNITS_BEFORE[st], NORMED_BEFORE.get(st)
                pairs = (q + k) // 2
                for j in range(4, 6):
                    split(b + j)
                if done is not None:
                    squares(FIRST[0], b + 3)
                split(b + 6)
                if done is not None:
                    qk_rstd(done, units)
                    squares(FIRST[1], b + 4)
                split(b + 7)
                if st == "fox":
                    forget()

                def normed_pair(b, i, u, unit, bank=B[0], last=False):
                    qk_rstd(u - 1, unit - 1)
                    split(b + 4, i)
                    squares(bank, i * 4 + (b + 2))
                    split(b + 5, i)
                    split(b + 6, i)
                    qk_rstd(u, unit)
                    if not last:
                        squares(B[1], i * 4 + (b + 4))
                        split(b + 7, i)

                with act.Fori(1, pairs) as i:
                    if done is None:
                        for j in range(4, 8):
                            split(b + j, i)
                    else:
                        normed_pair(b, i, i * 2 + done, i * 2 + units)
                b2 = b + 4 * pairs
                if st == "swa":
                    normed_pair(b2, 0, done + 2 * pairs, units + 2 * pairs, V_BANK[0], last=True)
                    core(st, ai, 0, EARLY[st])
                else:
                    if done is not None:
                        qk_rstd(done + 2 * pairs - 1, units + 2 * pairs - 1)
                    with act.Fori(0, v // 2 - 1) as i:
                        for j in range(4, 8):
                            split(b2 + j, i)
                    b3 = b2 + 2 * v - 4
                    split(b3 + 4)
                    split(b3 + 5)
                    core(st, ai, 0, EARLY[st])
                core(st, ai, EARLY[st], HEADS + 6)
                b3 = b + 2 * (q + k + v)
                for j in range(3 if st == "swa" else 2, 4):
                    split(b3 + j)
                mod_split(SPLIT_EARLY.get(st, []))
                down_splits(b + 2 * (q + k + v), 2 * O_UNITS, st)

            def core(st, ai, begin, end):
                scale = DH ** -0.5 if st == "moba" else 1.0
                for t in range(begin, end):
                    if 0 <= t - 5 < HEADS and (t - 5) % 2 == 1:
                        p, g = (t - 5) // 2, ai * HEADS + t - 5
                        act.wait_ge(pv_done, g + 1)
                        act.activation(hid_hi[:, p, :], O_BANK[p % 2][:, 0:T], ACT.Copy).then_inc(o_hi_done, 1)
                    if 0 <= t - 3 < HEADS:
                        h, g = t - 3, ai * HEADS + t - 3
                        act.wait_ge(pt_ps, g + 1)
                        if h >= 2:
                            act.wait_ge(pv_done, g - 1)
                        act.activation(probsT[:, h % 2, :], PT_BANK[h % 2][:, 0:KEYS], ACT.Copy).then_inc(pt_done, 1)
                    if t < HEADS:
                        h, g = t, ai * HEADS + t
                        act.wait_ge(neg_max_done, g + 1)
                        for blk, (lo, hi) in enumerate(((0, P), (P, KEYS))):
                            act.activation(probs[:, h % PROBS, lo:hi], probs[:, h % PROBS, lo:hi], ACT.Exp,
                                           bias=neg_max[:, h, blk:blk + 1], scale=scale,
                                           accum_out=row_sum[:, h, blk:blk + 1]).then_inc(exp_done, 1)
                        if st == "swa":
                            act.activation(sink_exp[:, h, :], neg_max[:, h, :], ACT.Exp,
                                           bias=vec[:, V_SINK + h:V_SINK + h + 1]).then_inc(exp_done, 1)

            def forget():
                act.wait_ge(fl_done, 1)
                act.activation(fl_abs[:], fl[:], ACT.Abs).then_inc(fl_act, 1)
                act.wait_ge(fl_act, 1)
                act.activation(fl_exp[:], fl_abs[:], ACT.Exp, scale=-1.0).then_inc(fl_act, 1)
                act.wait_ge(fl_act, 2)
                act.activation(fl_ln[:], fl_exp[:], ACT.Ln, bias=ones[:, 0:1]).then_inc(fl_act, 1)

            def ffn(st):
                f = int(st[-1])
                b = BASE[st]
                norm(st)

                def step(i):
                    first = isinstance(i, int)
                    g = i + f * UP_STEPS
                    split(b + 4, i)
                    if first:
                        act.preload_act_table_set("silu_and_others")
                    elif f > 0:
                        split(b + 5, i)
                    act.wait_ge(pe_used, b + 3 if first else i * 4 + (b + 2))
                    if f == 0:
                        for t in range(2):
                            act.activation(conv_gate[:, t * T:(t + 1) * T], GATE[:, t * T:(t + 1) * T], ACT.Identity,
                                           bias=conv_par(i, 0, t, 3), scale=conv_par(i, 0, t, 2)).then_inc(affine_done, 1)
                    else:
                        act.activation(silu_gate, GATE[:], ACT.Silu).then_inc(silu_done, 1)
                    if first or f == 0:
                        split(b + 5, i)
                    split(b + 6, i)
                    if f == 0:
                        act.wait_ge(pe_used, i * 4 + (b + 4))
                        for t in range(2):
                            act.activation(conv_up[:, t * T:(t + 1) * T], UP[:, t * T:(t + 1) * T], ACT.Identity,
                                           bias=conv_par(i, 1, t, 3), scale=conv_par(i, 1, t, 2)).then_inc(affine_done, 1)
                        act.wait_ge(gate_taps, i * 2 + 2)
                        act.activation(silu_gate, conv_gate, ACT.Silu).then_inc(silu_done, 1)
                    split(b + 7, i)
                    act.wait_ge(hid_done, g + 2)
                    act.activation(hid_hi[:, bass.ds(i * 2, 2), :].rearrange("p c t -> p (c t)"), hidden, ACT.Copy).then_inc(hid_hi_done, 1)

                step(0)
                if f == 0:
                    act.wait_ge(tail_in, 16)
                    act.activation(tail_hi[:], tail_raw[:], ACT.Copy).then_inc(tail_hi_done, 1)
                with act.Fori(1, UP_STEPS) as i:
                    step(i)
                mod_split(SPLIT_EARLY.get(st, []))
                down_splits(b + 4 * UP_STEPS, HID, st)

            def conv_par(i, kind, t, tap):
                return vec[:, bass.ds(i * 16 + (V_CONV + kind * 8 + t * 4 + tap), 1)]

            act.wait_ge(vec_in, 16)
            act.activation(c_act[:], vec[:, V_C:V_C + C], ACT.Silu).then_inc(c_done, 1)
            act.wait_ge(consts, CONSTS)
            act.activation(ones_r[:], ones[:], ACT.Copy).then_inc(ones_done, 1)
            for st in ORDER:
                (attention if st in QKV else ffn)(st)
                if st == "ffn0":
                    norm("final")
            for t in range(2):
                act.wait_ge(out_ps, 2 * t + 2)
                act.activation(hn_tok[:, t, 512:1024], OUT_BANK[t][1][:], ACT.Copy).then_inc(out_high, 1)

        @block.vector
        def _(dve):
            def split(h, i=0):
                s = h % SLOTS
                dve.wait_ge(hi_ready, i * 4 + (h + 1))
                dve.tensor_tensor(w_lo[:, s, :], raw_w[:, s, :], w_hi[:, s, :].bitcast(F32), ALU.subtract).then_inc(lo_ready, 1)

            def pair_add(n, p):
                dve.wait_ge(sq_done, n * C + 2 * p + 2)
                dve.tensor_tensor(sq[:, 2 * p, :], sq[:, 2 * p, :], sq[:, 2 * p + 1, :], ALU.add).then_inc(sq_added, 1)

            def norm(name):
                n = NORMS.index(name)
                if name in MOD_SET:
                    s = MOD_SET[name]
                    gain, shift = mod_gain[:, s, :], mods[:, s, 0:C]
                else:
                    at = {"moba": V_MIX, "ffn0": V_FFN, "final": V_FINAL}[name]
                    gain, shift = vec[:, at:at + C], None
                if n == 0:
                    for h in range(2):
                        split(h)
                if n > 0 and NORMS[n - 1] in BASE and NORMS[n - 1] not in QKV:
                    mod_finish(REDUCE_IN_OUT.get(NORMS[n - 1], [])[1:], [MOD_IN_FFN])
                if NORMS[n - 1] in QKV and n > 0:
                    mod_split(SPLIT_LATE.get(NORMS[n - 1], []))
                if name in MOD_SET:
                    dve.wait_ge(mod_done, 3 * MOD_SET[name] + 2)
                dve.wait_ge(rstd_done, n + 1)
                if name == "final":
                    for c in range(C):
                        dve.scalar_tensor_tensor(out=xT[:, c, :], in0=xT[:, c, :], scalar=gain[:, c:c + 1], in1=rstd[:],
                                                 op0=ALU.mult, op1=ALU.mult).then_inc(x_ready, 1)
                        if c in (3, 5, 7):
                            pair_add(n + 1, (c - 3) // 2)
                    mod_finish(REDUCE_IN_NORM[name], mod_banks(name))
                    return
                m = SPLIT_NORMS.index(name)

                def low(c):
                    dve.wait_ge(in_hi_done, m * C + c + 1)
                    hi = in_hi[:, c, :].bitcast(F32)
                    if shift is None:
                        dve.tensor_tensor(in_lo[:, c, :], hn[:, c, :], hi, ALU.subtract).then_inc(in_lo_done, 1)
                    else:
                        dve.scalar_tensor_tensor(out=in_lo[:, c, :], in0=hn[:, c, :], scalar=shift[:, c:c + 1], in1=hi,
                                                 op0=ALU.add, op1=ALU.subtract).then_inc(in_lo_done, 1)

                for c in range(C):
                    dve.scalar_tensor_tensor(out=hn[:, c, :], in0=xT[:, c, :], scalar=gain[:, c:c + 1], in1=rstd[:],
                                             op0=ALU.mult, op1=ALU.mult).then_inc(hn_done, 1)
                    if c:
                        low(c - 1)
                    if c == 4:
                        split(BASE[name] + 2)
                low(C - 1)
                split(BASE[name] + 3)

            def residual(st):
                d = ORDER.index(st)
                tiles = y_tiles(st)
                last = st == ORDER[-1]
                n = None if last else NORMS.index(st) + 1
                if st in MOD_SET:
                    dve.wait_ge(mod_done, 3 * MOD_SET[st] + 3)
                for c, (bank, at) in enumerate(tiles):
                    if c in (0, 2, 4, 6):
                        dve.wait_ge(y_done, 4 * d + c // 2 + 1)
                    elif c == C - 1:
                        dve.wait_ge(pe_used, BASE[ORDER[d + 1]] if not last else HALVES)
                    y = bank[:, at:at + T]
                    if st in MOD_SET:
                        gate = mods[:, MOD_SET[st], 2 * C + c:2 * C + c + 1]
                        dve.scalar_tensor_tensor(out=xT[:, c, :], in0=y, scalar=gate, in1=xT[:, c, :],
                                                 op0=ALU.mult, op1=ALU.add).then_inc(x_ready, 1)
                    else:
                        dve.tensor_tensor(xT[:, c, :], y, xT[:, c, :], ALU.add).then_inc(x_ready, 1)
                    if not last and c in (3, 5, 6):
                        pair_add(n, (c - 2) // 2)

            def ada(q, i, j, off=0):
                k = i * 2 + (j + off)
                dve.wait_ge(ada_in[j], i * 16 + 16 * (C // 2 * q + off // 2 + 1))
                if not isinstance(i, int) or C * q + k > 0:
                    dve.wait_ge(mod_step, i * 2 + (C * q + j + off))
                dve.wait_ge(mod_zero, q + 1)
                sums = mod_sum[:, q % SUMS, :]
                dve.scalar_tensor_tensor(out=sums, in0=ada_raw[:, j, :], scalar=c_act[:, bass.ds(k, 1)], in1=sums,
                                         op0=ALU.mult, op1=ALU.add).then_inc(mod_step, 1)

            def mod_split(groups):
                for q in groups:
                    dve.wait_ge(mod_hi_done, q + 1)
                    sums = mod_sum[:, q % SUMS, :]
                    dve.tensor_tensor(mod_lo[:, q % SUMS, :], sums, mod_hi[:, q % 2, :].bitcast(F32), ALU.subtract).then_inc(mod_lo_done, 1)

            adds = [0]

            def mod_finish(groups, banks):
                for q, bank in zip(groups, banks):
                    s, kind = q // 3, KIND_ORDER[q % 3]
                    dve.wait_ge(mod_ps, q + 1)
                    m = mods[:, s, KIND[kind] * C:(KIND[kind] + 1) * C]
                    for c in range(C):
                        dve.tensor_tensor_reduce(out=picked[:, c * P:(c + 1) * P], in0=bank[c // 4][:, (c % 4) * P:(c % 4 + 1) * P],
                                                 in1=diagonal[:], scale=1.0, scalar=3.0 * MASKED, op0=ALU.add, op1=ALU.max,
                                                 accum_out=m[:, c:c + 1]).then_inc(mod_picked, 1)
                    dve.wait_ge(mod_picked, C * (q + 1))
                    v = V_ADA_B + 3 * C * s + KIND[kind] * C
                    half = kind == "gate" and s % 3 != 1
                    ins = dve.tensor_tensor(m, m, vec[:, v:v + C], ALU.add)
                    if kind == "shift" or kind == "gate" and not half:
                        ins.then_inc(mod_done, 1)
                        continue
                    ins.then_inc(mod_add, 1)
                    adds[0] += 1
                    dve.wait_ge(mod_add, adds[0])
                    if kind == "scale":
                        dve.scalar_tensor_tensor(out=mod_gain[:, s, :], in0=m, scalar=1.0, in1=vec[:, V_NORM_G + C * s:V_NORM_G + C * (s + 1)],
                                                 op0=ALU.add, op1=ALU.mult).then_inc(mod_done, 1)
                    else:
                        dve.tensor_scalar(m, m, 0.5, None, ALU.mult).then_inc(mod_done, 1)

            def attention(st):
                ai = ATTN.index(st)
                b = BASE[st]
                norm(st)
                q, k, v = QKV[st]
                units, done = UNITS_BEFORE[st], NORMED_BEFORE.get(st)
                pairs = (q + k) // 2
                group = FIRST_GROUP[st]
                gains = None if done is None else qk_gain[:, (ai - 1) * 8:ai * 8]

                def evac(unit, bank, used):
                    to = shared[:, bass.ds(unit * (2 * T), 2 * T)]
                    if done is None:
                        dve.wait_ge(pe_used, used)
                        dve.tensor_copy(to, bank[:]).then_inc(proj_free, 1)
                    else:
                        dve.wait_ge(norm_rstd_done, unit + (done + 1))
                        dve.scalar_tensor_tensor(out=to, in0=bank[:], scalar=gains[:, bass.ds(unit, 1)], in1=norm_rstd,
                                                 op0=ALU.mult, op1=ALU.mult).then_inc(proj_free, 1)

                def evac_v(i, u, bank, used):
                    dve.wait_ge(pe_used, used)
                    dve.tensor_copy(v_tok[:, :, bass.ds(i * (2 * COLS) + u * COLS, COLS)],
                                    bank[:].rearrange("p (t n) -> p t n", t=2)).then_inc(proj_free, 1)

                for j in range(4, 7):
                    split(b + j)
                mod_finish(REDUCE_IN_NORM.get(st, []), mod_banks(st))
                if st == "fox":
                    dve.wait_ge(logits_ps, 1)
                    dve.tensor_copy(head_rows[:], FORGET[0:HEADS, T:2 * T]).then_inc(logits_sb, 1)
                evac(0, FIRST[0], b + 3)
                split(b + 7)
                if done is None:
                    evac(1, FIRST[1], b + 4)
                if st == "fox":
                    forget()
                ada(group, 0, 0)
                if done is not None:
                    evac(1, FIRST[1], None)
                ada(group, 0, 1)
                if st == "moba":
                    dve.wait_ge(bias_ps, 1)
                    dve.tensor_copy(bias_rows[:], MODB[0:HEADS, 0:BIAS_ROW]).then_inc(bias_sb, 1)
                with dve.Fori(1, pairs) as i:
                    split(b + 4, i)
                    split(b + 5, i)
                    if done is None:
                        evac(i * 2, B[0], i * 4 + (b + 2))
                    ada(group, i, 0)
                    split(b + 6, i)
                    if done is not None:
                        evac(i * 2, B[0], None)
                    split(b + 7, i)
                    if done is None:
                        evac(i * 2 + 1, B[1], i * 4 + (b + 4))
                    ada(group, i, 1)
                    if done is not None:
                        evac(i * 2 + 1, B[1], None)
                b2 = b + 4 * pairs
                if st == "swa":
                    for to, at in ((0, DH), (DH, 0)):
                        dve.tensor_copy(k_swap[to:to + DH, :], k_swa[at:at + DH, :]).then_inc(k_swapped, 1)
                    split(b2 + 4)
                    split(b2 + 5)
                    split(b2 + 6)
                    evac(2 * pairs, V_BANK[0], None)
                    core(st, ai, 0, EARLY[st])
                    evac_v(0, 0, V_BANK[1], b2 + 4)
                else:
                    if st == "fox":
                        forget_sums()
                    last = v // 2 - 1
                    with dve.Fori(0, last) as i:
                        split(b2 + 4, i)
                        split(b2 + 5, i)
                        evac_v(i, 0, V_BANK[0], i * 4 + (b2 + 2))
                        if st == "moba":
                            ada(group + 1, i, 0)
                        split(b2 + 6, i)
                        split(b2 + 7, i)
                        evac_v(i, 1, V_BANK[1], i * 4 + (b2 + 4))
                        if st == "moba":
                            ada(group + 1, i, 1)
                    b3 = b2 + 4 * last
                    for j in range(2):
                        split(b3 + 4 + j)
                        if st == "moba":
                            ada(group + 1, last, j)
                    evac_v(last, 0, V_BANK[0], b3 + 2)
                    core(st, ai, 0, EARLY[st])
                    evac_v(last, 1, V_BANK[1], b3 + 4)
                core(st, ai, EARLY[st], HEADS + 7)
                b3 = b + 2 * (q + k + v)
                for j in range(3 if st == "swa" else 2, 4):
                    split(b3 + j)
                mod_split(SPLIT_EARLY.get(st, []))
                left = {"moba": [(2, 0)], "swa": [(8, 2), (8, 3)], "fox": []}[st]
                b3 = b + 2 * (q + k + v)
                for j in range(2 * O_UNITS - 2):
                    if j == 4:
                        mod_finish(REDUCE_IN_OUT.get(st, []), [MOD_IN_ATTN])
                    split(b3 + 4 + j)
                    if j % 2 == 1 and j // 2 < len(left):
                        for hf in range(2):
                            ada(left[j // 2][0], left[j // 2][1], hf)
                residual(st)

            def core(st, ai, begin, end):
                if st == "swa":
                    dve.wait_ge(bias_back, 16)
                for t in range(begin, end):
                    if 0 <= t - 6 < HEADS and (t - 6) % 2 == 1:
                        p = (t - 6) // 2
                        dve.wait_ge(o_hi_done, ai * C + p + 1)
                        dve.tensor_tensor(hid_lo[:, p, :], O_BANK[p % 2][:, 0:T], hid_hi[:, p, :].bitcast(F32), ALU.subtract).then_inc(o_lo_done, 1)
                    if t < HEADS:
                        h, g = t, ai * HEADS + t
                        dve.wait_ge(score_done, g + 1)
                        if st == "fox" and h % FORGET_HEADS == 0:
                            dve.wait_ge(forget_masked, 2 * (h // FORGET_HEADS + 1))
                        if h >= PROBS:
                            dve.wait_ge(pt_ps, g - PROBS + 1)
                        for blk, (lo, hi) in enumerate(((0, P), (P, KEYS))):
                            add = {"moba": mask[:, lo:hi], "swa": bias[:, h, P:2 * P] if blk == 0 else bias[:, h, :],
                                   "fox": forget_mask[:, h, :] if blk == 0 else bias[:, h, :]}[st]
                            dve.tensor_tensor_reduce(out=probs[:, h % PROBS, lo:hi], in0=SCORE[h % 3][:, lo:hi], in1=add,
                                                     scale=1.0, scalar=3.0 * MASKED, op0=ALU.add, op1=ALU.max,
                                                     accum_out=row_max[:, h, blk:blk + 1]).then_inc(max_done, 1)
                    last = t - 1 if 0 <= t - 1 < HEADS else None
                    if last is not None:
                        dve.wait_ge(exp_done, EXPS_BEFORE[st] + EXPS[st] * (last + 1))
                        den = row_sum[:, last, :]
                        if st == "swa":
                            den = row_den[:, last, :]
                            dve.tensor_tensor(den, row_sum[:, last, :], sink_exp[:, last, :], ALU.add).then_inc(den_done, 1)
                        else:
                            dve.reciprocal(row_inv[:, last, :], den).then_inc(inv_done, 1)
                    if t < HEADS:
                        dve.wait_ge(max_done, 2 * (g + 1))
                        if st == "swa":
                            dve.tensor_scalar(neg_max[:, h, :], row_max[:, h, :], vec[:, V_SINK + h:V_SINK + h + 1], -1.0,
                                              ALU.max, ALU.mult).then_inc(neg_max_done, 1)
                        else:
                            dve.tensor_scalar(neg_max[:, h, :], row_max[:, h, :], -(DH ** -0.5) if st == "moba" else -1.0, None,
                                              ALU.mult).then_inc(neg_max_done, 1)
                    if last is not None:
                        if st == "swa":
                            dve.wait_ge(den_done, last + 1)
                            dve.reciprocal(row_inv[:, last, :], den).then_inc(inv_done, 1)
                        dve.wait_ge(inv_done, ai * HEADS + last + 1)
                        for blk, (lo, hi) in enumerate(((0, P), (P, KEYS))):
                            dve.tensor_scalar(probs[:, last % PROBS, lo:hi], probs[:, last % PROBS, lo:hi], row_inv[:, last, blk:blk + 1], None,
                                              ALU.mult).then_inc(prob_done, 1)
                    if st == "moba" and t in (4, 7, 10, 13):
                        ada(1, 2 + (t - 4) // 6, (t - 4) // 3 % 2)

            def forget():
                dve.wait_ge(fl_ps, 1)
                for t in range(2):
                    dve.tensor_tensor(fl[:, t, :], FORGET[:, t * HEADS:(t + 1) * HEADS], vec[:, V_BF:V_BF + HEADS], ALU.add).then_inc(fl_part, 1)
                dve.wait_ge(fl_part, 2)
                dve.tensor_scalar(fl_min[:], fl[:], 0.0, None, ALU.min).then_inc(fl_done, 1)
                dve.wait_ge(fl_done, 1)
                dve.wait_ge(fl_act, 3)
                dve.tensor_tensor(log_f[:], fl_min[:], fl_ln[:], ALU.subtract).then_inc(logf_done, 1)

            def forget_sums():
                dve.wait_ge(F_ps, 1)
                dve.tensor_copy(head_rows[:], FORGET[0:HEADS, T:2 * T]).then_inc(F_done, 1)

            def taps(bank, dst, i, kind, count):
                for lag in (1, 2):
                    for t in range(2):
                        if lag == 2:
                            dve.wait_ge(tap_done, i * 4 + (2 * kind + t + 1))
                        o = dst[:, t * T + lag:(t + 1) * T]
                        ins = dve.scalar_tensor_tensor(out=o, in0=bank[:, t * T:(t + 1) * T - lag], scalar=conv_par(i, kind, t, 2 - lag),
                                                       in1=o, op0=ALU.mult, op1=ALU.add)
                        ins.then_inc(tap_done if lag == 1 else count, 1)

            def conv_par(i, kind, t, tap):
                return vec[:, bass.ds(i * 16 + (V_CONV + kind * 8 + t * 4 + tap), 1)]

            def ffn(st):
                f = int(st[-1])
                b = BASE[st]
                norm(st)
                group = FIRST_GROUP.get(st)

                def step(i):
                    g = i + f * UP_STEPS
                    split(b + 4, i)
                    if f == 0:
                        dve.wait_ge(affine_done, i * 4 + 2)
                        taps(GATE, conv_gate, i, 0, gate_taps)
                    split(b + 5, i)
                    split(b + 6, i)
                    if f == 0:
                        dve.wait_ge(affine_done, i * 4 + 4)
                        taps(UP, conv_up, i, 1, up_taps)
                        dve.wait_ge(up_taps, i * 2 + 2)
                    else:
                        split(b + 7, i)
                    up = conv_up if f == 0 else UP[:]
                    dve.wait_ge(silu_done, g + 1)
                    dve.tensor_tensor(hidden, silu_gate, up, ALU.mult).then_inc(hid_done, 1)
                    if f == 0:
                        split(b + 7, i)

                def low(i):
                    g = i + f * UP_STEPS
                    dve.wait_ge(hid_hi_done, g + 1)
                    dve.tensor_tensor(hid_lo[:, bass.ds(i * 2, 2), :].rearrange("p c t -> p (c t)"), hidden,
                                      hid_hi[:, bass.ds(i * 2, 2), :].rearrange("p c t -> p (c t)").bitcast(F32), ALU.subtract).then_inc(hid_lo_done, 1)
                    dve.wait_ge(hid_lo_done, g + 1)

                step(0)
                low(0)
                mod_finish(REDUCE_IN_NORM.get(st, []), mod_banks(st))
                if f == 0:
                    dve.wait_ge(tail_hi_done, 1)
                    dve.tensor_tensor(tail_lo[:], tail_raw[:], tail_hi[:].bitcast(F32), ALU.subtract).then_inc(tail_lo_done, 1)
                if group is None:
                    with dve.Fori(1, UP_STEPS) as i:
                        step(i)
                        low(i)
                elif f == 0:
                    for j, (begin, end) in enumerate(((1, 4), (4, 7), (7, UP_STEPS))):
                        with dve.Fori(begin, end) as i:
                            step(i)
                            low(i)
                        if j < 2:
                            ada(group, 1, j)
                else:
                    for at, n in ((0, 4), (1, 4), (2, 2)):
                        with dve.Fori(1 + 4 * at, 1 + 4 * at + n) as i:
                            step(i)
                            for j in range(2):
                                ada(group + at, i, j, -2 - C * at)
                            low(i)
                mod_split(SPLIT_EARLY.get(st, [])[:1])
                b2 = b + 4 * UP_STEPS
                n = HID - 4 if st == ORDER[-1] else HID - 2
                peeled = (n - 1) % 4 + 1
                third = None if group is None else group if f == 0 else group + 2
                for j in range(peeled):
                    split(b2 + 4 + j)
                    if group is not None:
                        ada(third, 2 + j // 2, j % 2)
                loops = (n - peeled) // 4

                def splits(i):
                    for j in range(4):
                        split(b2 + peeled + j, i)
                        yield j

                for j in splits(1):
                    if group is not None:
                        ada(third + 1, j // 2, j % 2)
                for i in range(2, loops):
                    for j in splits(i):
                        if group is not None and j % 2 == 1:
                            ada(third + 1, i, j // 2)
                    if i == 2:
                        mod_finish(REDUCE_IN_OUT.get(st, [])[:1], [MOD_IN_FFN])
                mod_split(SPLIT_EARLY.get(st, [])[1:])
                late = SPLIT_LATE.get(st, [])
                for j in splits(loops):
                    if j == 0:
                        mod_split(late[0:1])
                    elif j == 2:
                        mod_split(late[1:])
                residual(st)

            dve.memset(row_max[:, 0, :], 0.0).then_inc(proj_free, 1)
            dve.memset(row_max[:, 1, :], 0.0).then_inc(proj_free, 1)
            dve.memset(row_max[:, 2, :], 0.0).then_inc(hid_done, 1)
            for c in range(C):
                dve.wait_ge(xt_ready, c // 2 + 1)
                dve.tensor_copy(xT[:, c, :], X_BANK[c // 2][:, (c % 2) * T:(c % 2 + 1) * T]).then_inc(x_ready, 1)
                if c in (3, 5, 7):
                    pair_add(0, (c - 3) // 2)
            dve.wait_ge(vec_in, 16)
            for at, n, g in ((0, 1, 1), (1, 4, 0), (8, 4, 2), (12, 4, 3)):
                dve.tensor_scalar(qk_gain[:, at:at + n], vec[:, V_QK_G + g:V_QK_G + g + 1].to_broadcast([P, n]),
                                  DH ** -0.5 if g % 2 == 0 else 1.0, None, ALU.mult).then_inc(gains_done, 1)
            dve.wait_ge(gains_done, 4)
            dve.wait_ge(c_done, 1)
            dve.wait_ge(consts, CONSTS)
            for st in ORDER:
                (attention if st in QKV else ffn)(st)
                if st == "ffn0":
                    norm("final")
            for t in range(2):
                dve.wait_ge(out_ps, 2 * t + 1)
                dve.tensor_copy(hn_tok[:, t, 0:512], OUT_BANK[t][0][:]).then_inc(out_low, 1)

        @block.tensor
        def _(pe):
            def mm(o, lhsT, rhs, start=False, stop=False):
                return pe.matmul(o, lhsT, rhs, start=start, stop=stop, skip_group_check=True)

            def weights(h, i):
                pe.wait_ge(lo_ready, i * 4 + (h + 1))

            def cols_half(h, i, hf, bank, between=None):
                weights(h, i)
                s = h % SLOTS
                for t in range(2):
                    o = bank[:, t * T:(t + 1) * T]
                    for kk in range(4):
                        k = 4 * hf + kk
                        at = kk * COLS + t * P
                        hi, lo = w_hi[:, s, at:at + P], w_lo[:, s, at:at + P]
                        mm(o, hi, in_hi[:, k, :], start=hf == 0 and t == 0 and kk == 0)
                        mm(o, hi, in_lo[:, k, :])
                        last = mm(o, lo, in_hi[:, k, :], stop=hf == 1 and kk == 3)
                    if t == 0 and between is not None:
                        between()
                last.then_inc(pe_used, 1)

            def v_half(h, i, hf, bank):
                weights(h, i)
                s = h % SLOTS
                for kk in range(4):
                    k = 4 * hf + kk
                    hi, lo = w_hi[:, s, kk * COLS:(kk + 1) * COLS], w_lo[:, s, kk * COLS:(kk + 1) * COLS]
                    for t in range(2):
                        o = bank[:, t * COLS:(t + 1) * COLS]
                        x_hi, x_lo = in_hi[:, k, t * P:(t + 1) * P], in_lo[:, k, t * P:(t + 1) * P]
                        mm(o, x_hi, hi, start=hf == 0 and t == 0 and kk == 0)
                        mm(o, x_hi, lo)
                        last = mm(o, x_lo, hi, stop=hf == 1 and kk == 3)
                last.then_inc(pe_used, 1)

            def first_pair(b, m, banks, stats=None, then=None):
                weights(b + 1, 0)
                tiles = [(u, t) for u in range(2) for t in range(2)]

                def hi_passes(h, k, o, t, start=False):
                    at = k % 4 * COLS + t * P
                    mm(o, w_hi[:, h % SLOTS, at:at + P], in_hi[:, k, :], start=start)
                    return mm(o, w_lo[:, h % SLOTS, at:at + P], in_hi[:, k, :])

                def lo_pass(h, k, o, t, stop=False):
                    at = k % 4 * COLS + t * P
                    return mm(o, w_hi[:, h % SLOTS, at:at + P], in_lo[:, k, :], stop=stop)

                for k in range(4):
                    pe.wait_ge(in_hi_done, m * C + k + 1)
                    for u, t in tiles:
                        hi_passes(b + u, k, banks[u][:, t * T:(t + 1) * T], t, start=k == 0 and t == 0)
                    pe.wait_ge(in_lo_done, m * C + k + 1)
                    for u, t in tiles:
                        last = lo_pass(b + u, k, banks[u][:, t * T:(t + 1) * T], t)
                last.then_inc(pe_used, 2)
                weights(b + 2, 0)
                for k in range(4, C):
                    pe.wait_ge(in_lo_done, m * C + k + 1)
                    for t in range(2):
                        hi_passes(b + 2, k, banks[0][:, t * T:(t + 1) * T], t)
                        last = lo_pass(b + 2, k, banks[0][:, t * T:(t + 1) * T], t, stop=k == C - 1)
                last.then_inc(pe_used, 1)
                if then is not None:
                    then()
                pe.wait_ge(hi_ready, b + 4)
                h = b + 3
                for t in range(2):
                    o = banks[1][:, t * T:(t + 1) * T]
                    for k in range(4, C):
                        at = k % 4 * COLS + t * P
                        mm(o, w_hi[:, h % SLOTS, at:at + P], in_hi[:, k, :])
                        lo_pass(h, k, o, t)
                    weights(h, 0)
                    for k in range(4, C):
                        at = k % 4 * COLS + t * P
                        last = mm(o, w_lo[:, h % SLOTS, at:at + P], in_hi[:, k, :], stop=k == C - 1)
                    if t == 0 and stats is not None:
                        stats()
                last.then_inc(pe_used, 1)

            def out_tile(t, h, c, st, start, stop):
                s = h % SLOTS
                if isinstance(c, int):
                    x_hi, x_lo = hid_hi[:, c, :], hid_lo[:, c, :]
                else:
                    x_hi = hid_hi[:, bass.ds(c, 1), :].rearrange("p c t -> p (c t)")
                    x_lo = hid_lo[:, bass.ds(c, 1), :].rearrange("p c t -> p (c t)")
                bank, at = y_tiles(st)[t]
                o = bank[:, at:at + T]
                hi, lo = w_hi[:, s, t * P:(t + 1) * P], w_lo[:, s, t * P:(t + 1) * P]
                mm(o, hi, x_hi, start=start and at == 0)
                mm(o, hi, x_lo)
                return mm(o, lo, x_hi, stop=stop)

            def rows_half(h, i, c, st, first=False):
                weights(h, i)
                for t in range(C):
                    last = out_tile(t, h, c, st, first, False)
                last.then_inc(pe_used, 1)

            def rows_end(h, c, st):
                weights(h + 1, 0)
                for t in range(C):
                    out_tile(t, h, c, st, False, False)
                    last = out_tile(t, h + 1, c + 1, st, False, True)
                    if t in (1, 3, 5, 6):
                        last.then_inc(y_done, 1)
                last.then_inc(pe_used, 2)

            def norm(name):
                n = NORMS.index(name)
                stat = stat_bank(name)[:, 0:T]
                for p in range(3):
                    pe.wait_ge(sq_added, 3 * n + p + 1)
                    mm(stat, ones[:], sq[:, 2 * p, :], start=p == 0)
                for c in (6, 7):
                    pe.wait_ge(sq_done, n * C + c + 1)
                    last = mm(stat, ones[:], sq[:, c, :], stop=c == 7)
                last.then_inc(sumsq, 1)
                mod_reduce(REDUCE_IN_NORM.get(name, []), mod_banks(name))

            def head_stats(u):
                pe.wait_ge(norm_sq_done, u + 1)
                mm(STAT[:], head_ones[:], norm_sq, start=True, stop=True).then_inc(norm_stat, 1)

            def unit_free(u):
                pe.wait_ge(proj_free, u + 1)

            def attention(st):
                ai = ATTN.index(st)
                b = BASE[st]
                norm(st)
                m = SPLIT_NORMS.index(st)
                q, k, v = QKV[st]
                units = UNITS_BEFORE[st]
                done = NORMED_BEFORE.get(st)
                pairs = (q + k) // 2
                unit_free(units + 1)
                first_pair(b, m, FIRST, None if done is None else lambda: head_stats(done), forget_logits if st == "fox" else None)
                if st == "moba":
                    pe.wait_ge(bias_in, 32)
                    mm(MODB[0:HEADS, 0:BIAS_ROW], rel_aug[:], bucket_sb[:], start=True, stop=True).then_inc(bias_ps, 1)
                if st == "fox":
                    forget_turn()
                with pe.Fori(1, pairs) as i:
                    cols_half(b, i, 0, B[0])
                    if done is not None:
                        head_stats(i * 2 + (done - 1))
                    cols_half(b + 1, i, 1, B[0])
                    unit_free(i * 2 + (units + 1))
                    cols_half(b + 2, i, 0, B[1])
                    if done is not None:
                        head_stats(i * 2 + done)
                    cols_half(b + 3, i, 1, B[1])
                    unit_free(i * 2 + (units + 2))
                b2, u2 = b + 4 * pairs, units + 2 * pairs
                if st == "swa":
                    cols_half(b2, 0, 0, V_BANK[0])
                    head_stats(done + 2 * pairs - 1)
                    cols_half(b2 + 1, 0, 1, V_BANK[0])
                    unit_free(u2 + 1)
                    v_half(b2 + 2, 0, 0, V_BANK[1])
                    head_stats(done + 2 * pairs)
                else:
                    if done is not None:
                        head_stats(done + 2 * pairs - 1)
                    if st == "fox":
                        forget_sums()
                    last = v // 2 - 1
                    with pe.Fori(0, last) as i:
                        for u in range(2):
                            unit_free(i * 2 + (u2 + u))
                            for hf in range(2):
                                v_half(b2 + 2 * u + hf, i, hf, V_BANK[u])
                    unit_free(last * 2 + u2)
                    for hf in range(2):
                        v_half(b2 + 4 * last + hf, 0, hf, V_BANK[0])
                    b2 += 4 * last
                pe.wait_ge(proj_free, u2 + 2)
                core(st, ai, 0, EARLY[st])
                if st == "swa":
                    v_half(b2 + 3, 0, 1, V_BANK[1])
                else:
                    unit_free(last * 2 + u2 + 1)
                    for hf in range(2):
                        v_half(b2 + 2 + hf, 0, hf, V_BANK[1])
                pe.wait_ge(proj_free, units + q + k + 2)
                if st in MOD_SET:
                    pe.wait_ge(mod_done, REDUCE_IN_NORM[st][-1] + 1)
                else:
                    pe.wait_ge(bias_sb, 1)
                core(st, ai, EARLY[st], HEADS + 4, units + q + k + v + 2)
                b3 = b + 2 * (q + k + v)
                for c in range(C - 2):
                    if c == C - 4:
                        pe.wait_ge(o_lo_done, ai * C + C)
                        mod_reduce(REDUCE_IN_OUT.get(st, []), [MOD_IN_ATTN])
                    pe.wait_ge(o_lo_done, ai * C + c + 1)
                    rows_half(b3 + c, 0, c, st, first=c == 0)
                pe.wait_ge(o_lo_done, ai * C + C)
                rows_end(b3 + C - 2, C - 2, st)

            def core(st, ai, begin, end, v_ready=None):
                def q_of(h):
                    at = (h % 2) * DH
                    q = q_swa if st == "swa" else qT
                    return q.rearrange("p (c t) -> p c t", t=T)[at:at + DH, h // 2, :]

                def k_of(h):
                    at = (h % 2) * DH
                    if st != "swa":
                        return kT.rearrange("p (c t) -> p c t", t=T)[at:at + DH, h // 2, :]
                    kv = h // 4
                    kk = k_swa if kv % 2 == h % 2 else k_swap
                    return kk.rearrange("p (c t) -> p c t", t=T)[at:at + DH, kv // 2, :]

                def v_of(h, t):
                    kv = h // 4 if st == "swa" else h
                    return v_tok[:, t, kv * DH:(kv + 1) * DH]

                for t in range(begin, end):
                    if t < HEADS:
                        h, g = t, ai * HEADS + t
                        if h >= 3:
                            pe.wait_ge(max_done, 2 * (g - 2))
                        if st == "swa" and h == 1:
                            pe.wait_ge(k_swapped, 2)
                        S = SCORE[h % 3]
                        for blk, (lo, hi) in enumerate(((0, P), (P, KEYS))):
                            n = hi - lo
                            ins = mm(S[:, lo:hi], q_of(h)[:, blk * P:(blk + 1) * P], k_of(h)[:, 0:n], start=True, stop=True)
                        ins.then_inc(score_done, 1)
                    if 0 <= t - 3 < HEADS:
                        h, g = t - 3, ai * HEADS + t - 3
                        pe.wait_ge(prob_done, 2 * (g + 1))
                        if h >= 2:
                            pe.wait_ge(pt_done, g - 1)
                        for j in range(3):
                            ins = pe.transpose(PT_BANK[h % 2][:, j * P:(j + 1) * P],
                                               probs[:, h % PROBS, (0, P, 2 * P)[j]:(0, P, 2 * P)[j] + P], ident[:])
                        ins.then_inc(pt_ps, 1)
                    if 0 <= t - 4 < HEADS:
                        h, g = t - 4, ai * HEADS + t - 4
                        pair = h // 2
                        if h == 0:
                            pe.wait_ge(proj_free, v_ready)
                        pe.wait_ge(pt_done, g + 1)
                        if h % 2 == 0 and pair >= 2:
                            pe.wait_ge(o_lo_done, ai * C + pair - 1)
                        o = O_BANK[pair % 2][(h % 2) * DH:(h % 2 + 1) * DH, :]
                        mm(o[:, 0:T], v_of(h, 0), probsT[:, h % 2, 0:T], start=True)
                        mm(o[:, P:T], v_of(h, 1), probsT[:, h % 2, T:KEYS], stop=True).then_inc(pv_done, 1)

            def forget_logits():
                pe.wait_ge(tail_lo_done, 1)
                o = FORGET[0:HEADS, T:2 * T]
                for k in range(C):
                    mm(o, tail_hi[:, k, :], in_hi[:, k, :], start=k == 0)
                    mm(o, tail_hi[:, k, :], in_lo[:, k, :])
                    last = mm(o, tail_lo[:, k, :], in_hi[:, k, :], stop=k == C - 1)
                last.then_inc(logits_ps, 1)

            def forget_turn():
                pe.wait_ge(logits_sb, 1)
                for t in range(2):
                    ins = pe.transpose(FORGET[:, t * HEADS:(t + 1) * HEADS], head_rows[:, t * P:(t + 1) * P], ident[0:HEADS, 0:HEADS])
                ins.then_inc(fl_ps, 1)

            def forget_sums():
                pe.wait_ge(logf_done, 1)
                mm(FORGET[0:HEADS, T:2 * T], log_f[:, 0, :], neg_tri[:], start=True)
                mm(FORGET[0:HEADS, T + P:2 * T], log_f[:, 1, :], neg_tri[:, 0:P], stop=True).then_inc(F_ps, 1)

            def ffn(st):
                f = int(st[-1])
                b = BASE[st]
                norm(st)
                m = SPLIT_NORMS.index(st)

                def gate_read(g):
                    pe.wait_ge(gate_taps, g * 2 + 2) if f == 0 else pe.wait_ge(silu_done, g + 1)

                pe.wait_ge(hid_done, f * UP_STEPS + 1)
                first_pair(b, m, [GATE, UP])
                gate_read(f * UP_STEPS)
                with pe.Fori(1, UP_STEPS) as i:
                    g = i + f * UP_STEPS
                    for hf in range(2):
                        cols_half(b + hf, i, hf, GATE)
                    pe.wait_ge(hid_done, g + 1)
                    for hf in range(2):
                        cols_half(b + 2 + hf, i, hf, UP)
                    gate_read(g)
                b2 = b + 4 * UP_STEPS
                hid = f * UP_STEPS
                if st in REDUCE_IN_NORM:
                    pe.wait_ge(mod_done, REDUCE_IN_NORM[st][-1] + 1)
                for c in range(2):
                    pe.wait_ge(hid_lo_done, hid + 1)
                    rows_half(b2 + c, 0, c, st, first=c == 0)
                pe.wait_ge(hid_lo_done, hid + UP_STEPS - 2)
                for c in range(2, 6):
                    rows_half(b2 + c, 0, c, st)
                mod_reduce(REDUCE_IN_OUT.get(st, [])[:1], [MOD_IN_FFN])
                with pe.Fori(1, HID // 4 - 1) as i:
                    for j in range(4):
                        rows_half(b2 + 2 + j, i, i * 4 + (2 + j), st)
                mod_reduce(REDUCE_IN_OUT.get(st, [])[1:], [MOD_IN_FFN])
                pe.wait_ge(hid_lo_done, hid + UP_STEPS)
                for c in range(HID - 4, HID - 2):
                    rows_half(b2 + c, 0, c, st)
                rows_end(b2 + HID - 2, HID - 2, st)

            def mod_reduce(groups, banks):
                if groups and groups[0] > 0:
                    pe.wait_ge(mod_done, groups[0])
                for q, bank in zip(groups, banks):
                    pe.wait_ge(mod_lo_done, q + 1)
                    for half, o in enumerate(bank):
                        cols = slice(half * 512, half * 512 + 512)
                        mm(o[:], ones_r[:], mod_hi[:, q % 2, cols], start=True)
                        last = mm(o[:], ones_r[:], mod_lo[:, q % SUMS, cols], stop=True)
                    last.then_inc(mod_ps, 1)

            pe.wait_ge(consts, 1)
            for _ in range(WARM_UP):
                pe.transpose(B[0][:, 0:P], ident[:], ident[:])
            for c in range(C):
                if c % 4 == 0:
                    pe.wait_ge(x_in[c // 4], 16)
                for t in range(2):
                    ins = pe.transpose(X_BANK[c // 2][:, (c % 2) * T + t * P:(c % 2) * T + (t + 1) * P], hn_tok[:, t, c * P:(c + 1) * P], ident[:])
                if c % 2 == 1:
                    ins.then_inc(xt_ready, 1)
            pe.wait_ge(ones_done, 1)
            for st in ORDER:
                (attention if st in QKV else ffn)(st)
                if st == "ffn0":
                    norm("final")
            for t in range(2):
                for c in range(C):
                    pe.wait_ge(x_ready, len(NORMS) * C + c + 1)
                    ins = pe.transpose(OUT_BANK[t][c // 4][:, (c % 4) * P:(c % 4 + 1) * P], xT[:, c, t * P:(t + 1) * P], ident[:])
                    if c % 4 == 3:
                        ins.then_inc(out_ps, 1)


WEIGHTS = ["x", "ffn_w_up", "ffn_w_down", "moba_w_qkv", "moba_w_o", "ada_w_2", "ffn_w13_2", "ffn_w2_2",
           "rel_bias_2", "swa_w_in_2", "swa_w_out_2", "fox_w_in_2", "fox_w_out_2"]


def bucket_rows():
    rows = np.zeros((BUCKETS + 1, BIAS_ROW), np.float32)
    exact = BUCKETS // 2
    for t in range(BIAS_ROW):
        n = 2 * P - 1 - t
        if not 0 <= n < MAX_DIST:
            rows[BUCKETS, t] = 1.0
            continue
        big = exact + int(np.log(np.float32(max(n, 1) / exact)) / np.log(MAX_DIST / exact) * (BUCKETS - exact)) if n >= exact else 0
        rows[min(n if n < exact else big, BUCKETS - 1), t] = 1.0
    return rows


def pack_vectors(inputs):
    def chunks(v):
        v = np.asarray(v)
        return np.moveaxis(v.reshape(-1, P), 1, 0)

    def rows(v):
        return np.broadcast_to(np.asarray(v).reshape(1, -1), (P, HEADS))

    taps = np.concatenate([np.asarray(inputs["ffn_conv_w"])[0], np.asarray(inputs["ffn_conv_b"])], axis=0)
    conv = taps.reshape(4, 2, UP_STEPS, 2, P).transpose(4, 2, 1, 3, 0).reshape(P, UP_STEPS * 16)

    def head(v):
        return np.tile(np.asarray(v).reshape(DH), 2)[:, None]

    parts = [chunks(inputs["norm_mix"]), chunks(inputs["norm_ffn"]), chunks(inputs["norm_final"]),
             chunks(inputs["norm_g_2"]), chunks(inputs["ada_b_2"]), chunks(inputs["c_2"]), conv,
             head(inputs["swa_q_g_2"]), head(inputs["swa_k_g_2"]), head(inputs["fox_q_g_2"]), head(inputs["fox_k_g_2"]),
             rows(inputs["swa_sink_2"]), rows(inputs["fox_b_f_2"])]
    return np.ascontiguousarray(np.concatenate(parts, axis=1))


def kernel(**inputs):
    import concourse.bacc as _bacc
    from concourse.bass_utils import run_bass_kernel_spmd as _run

    nc = _bacc.Bacc("TRN2", target_bir_lowering=False, num_devices=1)
    data = {name: np.ascontiguousarray(inputs[name]) for name in WEIGHTS}
    data["vectors"] = pack_vectors(inputs)
    data["bucket_rows"] = bucket_rows()
    arrays, aps = {}, {}
    for name, v in data.items():
        arrays[f"in_{name}_dram"] = v
        aps[name] = nc.dram_tensor(f"in_{name}_dram", v.shape, mybir.dt.from_np(v.dtype), kind="ExternalInput").ap()
    out = nc.dram_tensor("out_0_dram", (1, T, D), F32, kind="ExternalOutput").ap()
    build(nc, aps, out)
    r = _run(nc, [arrays], core_ids=[0])
    return r.results[0]["out_0_dram"]
```
